# Optimizing a Trainium2 kernel written in Bass

```python
import jax, jax.numpy as jnp
from jax import lax
import numpy as np
import math
import jax
import jax.numpy as jnp

D_MODEL = 1024
BATCH = 1
SEQ = 256
DEPTH = 1

EPS = 1e-6
POOL_WINDOWS = (2, 4, 8, 16)
N_POOL_GROUPS = len(POOL_WINDOWS)
POOL_WIDTH = D_MODEL // 2
POOL_GC = POOL_WIDTH // N_POOL_GROUPS
HEAD_DIM = 64
N_Q_HEADS = (D_MODEL // 2) // HEAD_DIM
N_KV_HEADS = 2
GROUP = N_Q_HEADS // N_KV_HEADS
ATTN_WIDTH = N_Q_HEADS * HEAD_DIM
KV_WIDTH = N_KV_HEADS * HEAD_DIM
WINDOW = 128
BLOCK = 128
NEG_INF = -1e30
ROPE_THETA = 500000.0
ROT_DIM = HEAD_DIM // 4
N_BRANCHES = 2
GATE_WIDTH = N_BRANCHES * D_MODEL
IN_SPLITS = (POOL_WIDTH, POOL_WIDTH + ATTN_WIDTH, POOL_WIDTH + ATTN_WIDTH + KV_WIDTH,
             POOL_WIDTH + ATTN_WIDTH + 2 * KV_WIDTH)
IN_WIDTH = POOL_WIDTH + ATTN_WIDTH + 2 * KV_WIDTH + GATE_WIDTH
D_FF = 4 * D_MODEL


def _rmsnorm(x, g):
    xf = x.astype(jnp.float32)
    r = lax.rsqrt(jnp.mean(xf * xf, axis=-1, keepdims=True) + EPS)
    return (xf * r * g.astype(jnp.float32)).astype(x.dtype)

def _partial_rotary(t, cos, sin):
    half = ROT_DIM // 2
    t1 = t[..., :half]
    t2 = t[..., half:ROT_DIM]
    c = cos[None, :, None, :].astype(t.dtype)
    s = sin[None, :, None, :].astype(t.dtype)
    return jnp.concatenate([t1 * c - t2 * s, t2 * c + t1 * s, t[..., ROT_DIM:]], axis=-1)

def _multiscale_pool(u, w_pool, pool_scale):
    B, S, _ = u.shape
    uf = u.astype(jnp.float32)
    cs = jnp.pad(jnp.cumsum(uf, axis=1), ((0, 0), (1, 0), (0, 0)))
    t = jnp.arange(S)
    pooled = []
    for gi, w in enumerate(POOL_WINDOWS):
        c = cs[..., gi * POOL_GC:(gi + 1) * POOL_GC]
        upper = c[:, 1:]
        lower = jnp.pad(c[:, :S + 1 - w], ((0, 0), (w - 1, 0), (0, 0)))
        count = jnp.minimum(t + 1, w).astype(jnp.float32)[None, :, None]
        pooled.append((upper - lower) / count)
    pooled = jnp.stack(pooled, axis=2)
    diff = (pooled - uf.reshape(B, S, N_POOL_GROUPS, POOL_GC)).astype(u.dtype)
    mixed = jnp.einsum('bsgc,gcd->bsgd', diff, w_pool)
    return mixed.reshape(B, S, POOL_WIDTH) * pool_scale

def _sliding_window_sink_attention(q, k, v, sinks):
    B, S = q.shape[0], q.shape[1]
    nb = S // BLOCK
    qb = q.reshape(B, nb, BLOCK, N_KV_HEADS, GROUP, HEAD_DIM)

    def with_prev(t):
        tb = t.reshape(B, nb, BLOCK, N_KV_HEADS, HEAD_DIM)
        prev = jnp.pad(tb[:, :-1], ((0, 0), (1, 0), (0, 0), (0, 0), (0, 0)))
        return jnp.concatenate([prev, tb], axis=2)

    kk = with_prev(k)
    vv = with_prev(v)
    scale = HEAD_DIM ** -0.5
    s = jnp.einsum('bnqhgd,bnkhd->bnhgqk', qb, kk).astype(jnp.float32) * scale
    qi = jnp.arange(BLOCK)[:, None]
    kj = jnp.arange(2 * BLOCK)[None, :]
    rel = qi + BLOCK - kj
    band = (rel >= 0) & (rel < WINDOW)
    has_prev = (jnp.arange(nb) > 0)[:, None, None] | (kj >= BLOCK)[None]
    valid = band[None] & has_prev
    s = jnp.where(valid[None, :, None, None], s, NEG_INF)
    sink = jnp.broadcast_to(sinks.astype(jnp.float32).reshape(1, 1, N_KV_HEADS, GROUP, 1, 1),
                            s.shape[:-1] + (1,))
    p = jax.nn.softmax(jnp.concatenate([s, sink], axis=-1), axis=-1)[..., :-1]
    o = jnp.einsum('bnhgqk,bnkhd->bnqhgd', p.astype(v.dtype), vv)
    return o.reshape(B, S, ATTN_WIDTH)

def first_inputs(seed: int = 0) -> dict:
    key = jax.random.key(seed)
    ks = jax.random.split(key, 16)
    nrm = jax.random.normal
    f32 = jnp.float32

    def gain(k):
        return 1.0 + 0.1 * nrm(k, (DEPTH, D_MODEL), f32)

    return {
        "x": nrm(ks[0], (BATCH, SEQ, D_MODEL), f32),
        "g_mix_pre": gain(ks[1]),
        "w_in": nrm(ks[2], (DEPTH, D_MODEL, IN_WIDTH), f32) * D_MODEL ** -0.5,
        "b_in": 0.02 * nrm(ks[3], (DEPTH, IN_WIDTH), f32),
        "w_pool": nrm(ks[4], (DEPTH, N_POOL_GROUPS, POOL_GC, POOL_GC), f32) * POOL_GC ** -0.5,
        "pool_scale": 1.0 + 0.1 * nrm(ks[5], (DEPTH, POOL_WIDTH), f32),
        "attn_sinks": 0.5 * nrm(ks[6], (DEPTH, N_Q_HEADS), f32),
        "w_branch_pool": nrm(ks[7], (DEPTH, POOL_WIDTH, D_MODEL), f32) * POOL_WIDTH ** -0.5,
        "w_branch_attn": nrm(ks[8], (DEPTH, ATTN_WIDTH, D_MODEL), f32) * ATTN_WIDTH ** -0.5,
        "w_out": nrm(ks[9], (DEPTH, D_MODEL, D_MODEL), f32) * D_MODEL ** -0.5,
        "g_mix_post": gain(ks[10]),
        "g_mlp_pre": gain(ks[11]),
        "w_up": nrm(ks[12], (DEPTH, D_MODEL, D_FF), f32) * D_MODEL ** -0.5,
        "w_down": nrm(ks[13], (DEPTH, D_FF, D_MODEL), f32) * D_FF ** -0.5,
        "g_mlp_post": gain(ks[14]),
    }

def first_block(x, g_mix_pre, w_in, b_in, w_pool, pool_scale, attn_sinks, w_branch_pool,
              w_branch_attn, w_out, g_mix_post, g_mlp_pre, w_up, w_down, g_mlp_post):
    B, S, _ = x.shape
    pos = jnp.arange(S, dtype=jnp.float32)
    inv_freq = ROPE_THETA ** (-jnp.arange(0, ROT_DIM, 2, dtype=jnp.float32) / ROT_DIM)
    ang = pos[:, None] * inv_freq[None, :]
    cos, sin = jnp.cos(ang), jnp.sin(ang)

    for l in range(DEPTH):
        h = _rmsnorm(x, g_mix_pre[l])
        proj = jnp.einsum('bsd,de->bse', h, w_in[l]) + b_in[l]
        u_pool, q, k, v, gates = jnp.split(proj, IN_SPLITS, axis=-1)

        y_pool = _multiscale_pool(u_pool, w_pool[l], pool_scale[l])

        q = _partial_rotary(q.reshape(B, S, N_Q_HEADS, HEAD_DIM), cos, sin)
        k = _partial_rotary(k.reshape(B, S, N_KV_HEADS, HEAD_DIM), cos, sin)
        v = v.reshape(B, S, N_KV_HEADS, HEAD_DIM)
        y_attn = _sliding_window_sink_attention(
            q.reshape(B, S, N_KV_HEADS, GROUP, HEAD_DIM), k, v, attn_sinks[l])

        g = jax.nn.sigmoid(gates.astype(jnp.float32)).astype(x.dtype)
        g_pool, g_attn = g[..., :D_MODEL], g[..., D_MODEL:]
        merged = (g_pool * jnp.einsum('bsc,cd->bsd', y_pool, w_branch_pool[l])
                  + g_attn * jnp.einsum('bsc,cd->bsd', y_attn, w_branch_attn[l]))
        mix = jnp.einsum('bsd,de->bse', merged, w_out[l])
        x = x + _rmsnorm(mix, g_mix_post[l])

        h2 = _rmsnorm(x, g_mlp_pre[l])
        ff = jnp.einsum('bsf,fd->bsd',
                        jnp.square(jax.nn.relu(jnp.einsum('bsd,df->bsf', h2, w_up[l]))), w_down[l])
        x = x + _rmsnorm(ff, g_mlp_post[l])
    return x


DEPTH_2 = 2

GRID_W = 64
CTX_LEN = 256
N_MIXERS = 3
FFN_HIDDEN = -(-8 * D_MODEL // (3 * 256)) * 256
CONV_WIDTH = 3
MLA_HEADS = D_MODEL // 64
MLA_Q_LORA = 3 * D_MODEL // 4
MLA_KV_LORA = D_MODEL // 4
MLA_NOPE = 64
MLA_ROPE = 32
MLA_V = 64
DIFF_HEADS = 8
DIFF_HEAD_DIM = D_MODEL // (2 * DIFF_HEADS)
ROPE_THETA_2 = 10000.0
NORM_EPS = 1e-6
Q_BLOCK = 128


def rms_norm(x, g):
    xf = x.astype(jnp.float32)
    y = xf * lax.rsqrt(jnp.mean(xf * xf, axis=-1, keepdims=True) + NORM_EPS)
    return (y * g.astype(jnp.float32)).astype(x.dtype)

def modulate(h, shift, scale):
    return h * (1.0 + scale) + shift

def swiglu(h, w_gate, w_up, w_down):
    return (jax.nn.silu(h @ w_gate) * (h @ w_up)) @ w_down

def axial_rope_tables(rows, rot_dim):
    axis_dim = rot_dim // 2
    inv_freq = ROPE_THETA_2 ** (-jnp.arange(0, axis_dim, 2, dtype=jnp.float32) / axis_dim)
    row = jnp.repeat(jnp.arange(rows, dtype=jnp.float32), GRID_W)
    col = jnp.tile(jnp.arange(GRID_W, dtype=jnp.float32), rows)
    ang_r = row[:, None] * inv_freq
    ang_c = col[:, None] * inv_freq
    ang = jnp.concatenate([ang_r, ang_r, ang_c, ang_c], axis=-1)
    return jnp.cos(ang), jnp.sin(ang)

def apply_axial_rope(x, cos, sin):
    a = x.shape[-1] // 2
    h = a // 2
    xr, xc = x[..., :a], x[..., a:]
    rot = jnp.concatenate([-xr[..., h:], xr[..., :h], -xc[..., h:], xc[..., :h]], axis=-1)
    return x * cos.astype(x.dtype) + rot * sin.astype(x.dtype)

def sweep_query_blocks(block_fn, *qs):
    b, n = qs[0].shape[:2]
    if n % Q_BLOCK or n == Q_BLOCK:
        return block_fn(*qs)
    nb = n // Q_BLOCK
    blocks = tuple(jnp.swapaxes(a.reshape(b, nb, Q_BLOCK, *a.shape[2:]), 0, 1) for a in qs)
    out = lax.map(lambda blk: block_fn(*blk), blocks)
    out = jnp.swapaxes(out, 0, 1)
    return out.reshape(b, n, *out.shape[3:])

def short_conv_mixer(h, w_in, conv_k, conv_b, w_out):
    b_gate, c_gate, u = jnp.split(h @ w_in, 3, axis=-1)
    z = c_gate * u
    pad = CONV_WIDTH // 2
    y = lax.conv_general_dilated(z, conv_k[:, None, :], window_strides=(1,), padding=((pad, pad),),
                                 dimension_numbers=('NWC', 'WIO', 'NWC'), feature_group_count=D_MODEL)
    y = y + conv_b
    return (b_gate * y) @ w_out

def _mla_project(h, cos, sin, with_q, w_in, q_norm_g, w_q_up, kv_norm_g, w_kv_up,
                 qn_nope_g, qn_rope_g, kn_nope_g, kn_rope_g):
    b, n, _ = h.shape
    proj = h @ (w_in if with_q else w_in[:, MLA_Q_LORA:])
    if with_q:
        q_lat, proj = proj[..., :MLA_Q_LORA], proj[..., MLA_Q_LORA:]
    kv_lat, k_pe = proj[..., :MLA_KV_LORA], proj[..., MLA_KV_LORA:]
    kv = (rms_norm(kv_lat, kv_norm_g) @ w_kv_up).reshape(b, n, MLA_HEADS, MLA_NOPE + MLA_V)
    k_nope = rms_norm(kv[..., :MLA_NOPE], kn_nope_g)
    v = kv[..., MLA_NOPE:]
    k_pe = rms_norm(k_pe, kn_rope_g)
    if cos is not None:
        k_pe = apply_axial_rope(k_pe, cos, sin)
    if not with_q:
        return None, None, k_nope, k_pe, v
    q = (rms_norm(q_lat, q_norm_g) @ w_q_up).reshape(b, n, MLA_HEADS, MLA_NOPE + MLA_ROPE)
    q_nope = rms_norm(q[..., :MLA_NOPE], qn_nope_g)
    q_pe = rms_norm(q[..., MLA_NOPE:], qn_rope_g)
    if cos is not None:
        q_pe = apply_axial_rope(q_pe, cos[:, None, :], sin[:, None, :])
    return q_nope, q_pe, k_nope, k_pe, v

def _mla_block(k_nope, k_pe, v):
    scale = (MLA_NOPE + MLA_ROPE) ** -0.5

    def attend(q_nope, q_pe):
        s = (jnp.einsum('bqhd,bkhd->bhqk', q_nope, k_nope)
             + jnp.einsum('bqhr,bkr->bhqk', q_pe, k_pe))
        p = jax.nn.softmax(s.astype(jnp.float32) * scale, axis=-1).astype(v.dtype)
        return jnp.einsum('bhqk,bkhd->bqhd', p, v)
    return attend

def mla_mixer(a_ctx, a_lat, ctx_out, cos, sin, w_in, q_norm_g, w_q_up, kv_norm_g, w_kv_up,
              qn_nope_g, qn_rope_g, kn_nope_g, kn_rope_g, w_out):
    prm = (w_in, q_norm_g, w_q_up, kv_norm_g, w_kv_up, qn_nope_g, qn_rope_g, kn_nope_g, kn_rope_g)
    cq_n, cq_p, ck_n, ck_p, cv = _mla_project(a_ctx, None, None, ctx_out, *prm)
    lq_n, lq_p, lk_n, lk_p, lv = _mla_project(a_lat, cos, sin, True, *prm)
    b, n = a_lat.shape[:2]
    attend_lat = _mla_block(jnp.concatenate([ck_n, lk_n], axis=1),
                            jnp.concatenate([ck_p, lk_p], axis=1),
                            jnp.concatenate([cv, lv], axis=1))
    o_lat = sweep_query_blocks(attend_lat, lq_n, lq_p).reshape(b, n, MLA_HEADS * MLA_V) @ w_out
    o_ctx = None
    if ctx_out:
        o_ctx = sweep_query_blocks(_mla_block(ck_n, ck_p, cv), cq_n, cq_p)
        o_ctx = o_ctx.reshape(b, a_ctx.shape[1], MLA_HEADS * MLA_V) @ w_out
    return o_ctx, o_lat

def _diff_project(h, cos, sin, with_q, w_in, qn_g, kn_g):
    b, n, _ = h.shape
    proj = h @ (w_in if with_q else w_in[:, D_MODEL:])
    parts = jnp.split(proj, 3 if with_q else 2, axis=-1)
    k = rms_norm(parts[-2].reshape(b, n, DIFF_HEADS, 2, DIFF_HEAD_DIM), kn_g)
    v = parts[-1].reshape(b, n, DIFF_HEADS, 2 * DIFF_HEAD_DIM)
    if cos is not None:
        k = apply_axial_rope(k, cos[:, None, None, :], sin[:, None, None, :])
    if not with_q:
        return None, k, v
    q = rms_norm(parts[0].reshape(b, n, DIFF_HEADS, 2, DIFF_HEAD_DIM), qn_g)
    if cos is not None:
        q = apply_axial_rope(q, cos[:, None, None, :], sin[:, None, None, :])
    return q, k, v

def _diff_block(k, v, lam):
    scale = DIFF_HEAD_DIM ** -0.5
    k1, k2 = k[..., 0, :], k[..., 1, :]

    def attend(q):
        s1 = jnp.einsum('bqhd,bkhd->bhqk', q[..., 0, :], k1).astype(jnp.float32) * scale
        s2 = jnp.einsum('bqhd,bkhd->bhqk', q[..., 1, :], k2).astype(jnp.float32) * scale
        p = jax.nn.softmax(s1, axis=-1) - lam * jax.nn.softmax(s2, axis=-1)
        return jnp.einsum('bhqk,bkhe->bqhe', p.astype(v.dtype), v)
    return attend

def diff_mixer(a_ctx, a_lat, ctx_out, cos, sin, lam_init, w_in, qn_g, kn_g,
               lq1, lk1, lq2, lk2, sub_g, w_out):
    lam = (jnp.exp(jnp.sum(lq1.astype(jnp.float32) * lk1.astype(jnp.float32)))
           - jnp.exp(jnp.sum(lq2.astype(jnp.float32) * lk2.astype(jnp.float32))) + lam_init)
    cq, ck, cv = _diff_project(a_ctx, None, None, ctx_out, w_in, qn_g, kn_g)
    lq, lk, lv = _diff_project(a_lat, cos, sin, True, w_in, qn_g, kn_g)

    def finish(o):
        o = rms_norm(o, sub_g) * (1.0 - lam_init)
        return o.reshape(o.shape[0], o.shape[1], D_MODEL) @ w_out

    attend_lat = _diff_block(jnp.concatenate([ck, lk], axis=1), jnp.concatenate([cv, lv], axis=1), lam)
    o_lat = finish(sweep_query_blocks(attend_lat, lq))
    o_ctx = finish(sweep_query_blocks(_diff_block(ck, cv, lam), cq)) if ctx_out else None
    return o_ctx, o_lat

def second_inputs(seed: int = 0) -> dict:
    key = jax.random.key(seed)
    ks = iter(jax.random.split(key, 40))

    def nrm(shape, scale):
        return jax.random.normal(next(ks), shape, jnp.float32) * scale

    def gain(shape):
        return 1.0 + 0.02 * jax.random.normal(next(ks), shape, jnp.float32)

    n_a, n_b, n_c = (len(range(k, DEPTH_2, N_MIXERS)) for k in range(N_MIXERS))
    d, f = D_MODEL, FFN_HIDDEN
    return {
        'x': nrm((BATCH, SEQ, d), 1.0),
        'c': nrm((BATCH, d), 1.0),
        'ctx': nrm((BATCH, CTX_LEN, d), 1.0),
        'c_ctx': nrm((d,), 1.0),
        'norm_mix_g': gain((DEPTH_2, d)),
        'norm_ffn_g': gain((DEPTH_2, d)),
        'mod_w': nrm((DEPTH_2, d, 6 * d), 0.5 * d ** -0.5),
        'mod_b': nrm((DEPTH_2, 6 * d), 0.02),
        'ffn_w_gate': nrm((DEPTH_2, d, f), d ** -0.5),
        'ffn_w_up': nrm((DEPTH_2, d, f), d ** -0.5),
        'ffn_w_down': nrm((DEPTH_2, f, d), f ** -0.5),
        'conv_w_in': nrm((n_a, d, 3 * d), d ** -0.5),
        'conv_k': nrm((n_a, CONV_WIDTH, d), CONV_WIDTH ** -0.5),
        'conv_b': nrm((n_a, d), 0.02),
        'conv_w_out': nrm((n_a, d, d), d ** -0.5),
        'mla_w_in': nrm((n_b, d, MLA_Q_LORA + MLA_KV_LORA + MLA_ROPE), d ** -0.5),
        'mla_q_norm_g': gain((n_b, MLA_Q_LORA)),
        'mla_w_q_up': nrm((n_b, MLA_Q_LORA, MLA_HEADS * (MLA_NOPE + MLA_ROPE)), MLA_Q_LORA ** -0.5),
        'mla_kv_norm_g': gain((n_b, MLA_KV_LORA)),
        'mla_w_kv_up': nrm((n_b, MLA_KV_LORA, MLA_HEADS * (MLA_NOPE + MLA_V)), MLA_KV_LORA ** -0.5),
        'mla_qn_nope_g': gain((n_b, MLA_NOPE)),
        'mla_qn_rope_g': gain((n_b, MLA_ROPE)),
        'mla_kn_nope_g': gain((n_b, MLA_NOPE)),
        'mla_kn_rope_g': gain((n_b, MLA_ROPE)),
        'mla_w_out': nrm((n_b, MLA_HEADS * MLA_V, d), (MLA_HEADS * MLA_V) ** -0.5),
        'diff_w_in': nrm((n_c, d, 3 * d), d ** -0.5),
        'diff_qn_g': gain((n_c, DIFF_HEAD_DIM)),
        'diff_kn_g': gain((n_c, DIFF_HEAD_DIM)),
        'diff_lq1': nrm((n_c, DIFF_HEAD_DIM), 0.1),
        'diff_lk1': nrm((n_c, DIFF_HEAD_DIM), 0.1),
        'diff_lq2': nrm((n_c, DIFF_HEAD_DIM), 0.1),
        'diff_lk2': nrm((n_c, DIFF_HEAD_DIM), 0.1),
        'diff_sub_g': gain((n_c, 2 * DIFF_HEAD_DIM)),
        'diff_w_out': nrm((n_c, d, d), d ** -0.5),
    }

def second_block(x, c, ctx, c_ctx, norm_mix_g, norm_ffn_g, mod_w, mod_b, ffn_w_gate, ffn_w_up, ffn_w_down,
              conv_w_in, conv_k, conv_b, conv_w_out,
              mla_w_in, mla_q_norm_g, mla_w_q_up, mla_kv_norm_g, mla_w_kv_up,
              mla_qn_nope_g, mla_qn_rope_g, mla_kn_nope_g, mla_kn_rope_g, mla_w_out,
              diff_w_in, diff_qn_g, diff_kn_g, diff_lq1, diff_lk1, diff_lq2, diff_lk2, diff_sub_g, diff_w_out):
    n_lat = x.shape[1]
    rows = n_lat // GRID_W
    cos_mla, sin_mla = axial_rope_tables(rows, MLA_ROPE)
    cos_diff, sin_diff = axial_rope_tables(rows, DIFF_HEAD_DIM)
    silu_c = jax.nn.silu(c)
    silu_cctx = jax.nn.silu(c_ctx)
    h_lat, h_ctx = x, ctx
    for i in range(DEPTH_2):
        kind, slot = i % N_MIXERS, i // N_MIXERS
        last = i == DEPTH_2 - 1
        sh1, sc1, g1, sh2, sc2, g2 = jnp.split((silu_c @ mod_w[i] + mod_b[i])[:, None, :], 6, axis=-1)
        a_lat = modulate(rms_norm(h_lat, norm_mix_g[i]), sh1, sc1)
        need_ctx_in = not (last and kind == 0)
        if need_ctx_in:
            csh1, csc1, cg1, csh2, csc2, cg2 = jnp.split(silu_cctx @ mod_w[i] + mod_b[i], 6, axis=-1)
            a_ctx = modulate(rms_norm(h_ctx, norm_mix_g[i]), csh1, csc1)
        if kind == 0:
            o_lat = short_conv_mixer(a_lat, conv_w_in[slot], conv_k[slot], conv_b[slot], conv_w_out[slot])
            o_ctx = None if last else short_conv_mixer(a_ctx, conv_w_in[slot], conv_k[slot], conv_b[slot],
                                                       conv_w_out[slot])
        elif kind == 1:
            o_ctx, o_lat = mla_mixer(a_ctx, a_lat, not last, cos_mla, sin_mla,
                                     mla_w_in[slot], mla_q_norm_g[slot], mla_w_q_up[slot],
                                     mla_kv_norm_g[slot], mla_w_kv_up[slot],
                                     mla_qn_nope_g[slot], mla_qn_rope_g[slot],
                                     mla_kn_nope_g[slot], mla_kn_rope_g[slot], mla_w_out[slot])
        else:
            lam_init = 0.8 - 0.6 * math.exp(-0.3 * i)
            o_ctx, o_lat = diff_mixer(a_ctx, a_lat, not last, cos_diff, sin_diff, lam_init,
                                      diff_w_in[slot], diff_qn_g[slot], diff_kn_g[slot],
                                      diff_lq1[slot], diff_lk1[slot], diff_lq2[slot], diff_lk2[slot],
                                      diff_sub_g[slot], diff_w_out[slot])
        h_lat = h_lat + g1 * o_lat
        h_lat = h_lat + g2 * swiglu(modulate(rms_norm(h_lat, norm_ffn_g[i]), sh2, sc2),
                                    ffn_w_gate[i], ffn_w_up[i], ffn_w_down[i])
        if not last:
            h_ctx = h_ctx + cg1 * o_ctx
            h_ctx = h_ctx + cg2 * swiglu(modulate(rms_norm(h_ctx, norm_ffn_g[i]), csh2, csc2),
                                         ffn_w_gate[i], ffn_w_up[i], ffn_w_down[i])
    return h_lat


def setup_inputs(seed=0):
    out = dict(first_inputs(seed))
    for name, value in second_inputs(seed + 1).items():
        if name != "x":
            out[name + "_2"] = value
    return out


def reference(
    x, g_mix_pre, w_in, b_in, w_pool, pool_scale, attn_sinks, w_branch_pool, w_branch_attn,
    w_out, g_mix_post, g_mlp_pre, w_up, w_down, g_mlp_post, c_2, ctx_2, c_ctx_2, norm_mix_g_2,
    norm_ffn_g_2, mod_w_2, mod_b_2, ffn_w_gate_2, ffn_w_up_2, ffn_w_down_2, conv_w_in_2,
    conv_k_2, conv_b_2, conv_w_out_2, mla_w_in_2, mla_q_norm_g_2, mla_w_q_up_2, mla_kv_norm_g_2,
    mla_w_kv_up_2, mla_qn_nope_g_2, mla_qn_rope_g_2, mla_kn_nope_g_2, mla_kn_rope_g_2,
    mla_w_out_2, diff_w_in_2, diff_qn_g_2, diff_kn_g_2, diff_lq1_2, diff_lk1_2, diff_lq2_2,
    diff_lk2_2, diff_sub_g_2, diff_w_out_2,
):
    x = first_block(
        x, g_mix_pre, w_in, b_in, w_pool, pool_scale, attn_sinks, w_branch_pool, w_branch_attn,
        w_out, g_mix_post, g_mlp_pre, w_up, w_down, g_mlp_post,
    )
    return second_block(
        x, c_2, ctx_2, c_ctx_2, norm_mix_g_2, norm_ffn_g_2, mod_w_2, mod_b_2, ffn_w_gate_2,
        ffn_w_up_2, ffn_w_down_2, conv_w_in_2, conv_k_2, conv_b_2, conv_w_out_2, mla_w_in_2,
        mla_q_norm_g_2, mla_w_q_up_2, mla_kv_norm_g_2, mla_w_kv_up_2, mla_qn_nope_g_2,
        mla_qn_rope_g_2, mla_kn_nope_g_2, mla_kn_rope_g_2, mla_w_out_2, diff_w_in_2,
        diff_qn_g_2, diff_kn_g_2, diff_lq1_2, diff_lk1_2, diff_lq2_2, diff_lk2_2, diff_sub_g_2,
        diff_w_out_2,
    )


_drawn_inputs = setup_inputs


def setup_inputs(seed=0):
    import zlib

    import numpy as np

    out = dict(_drawn_inputs(seed))
    spreads = {}
    factors = {'b_in': 3.151,
     'attn_sinks': 4.764,
     'ctx_2': 24.871,
     'norm_mix_g_2': 6.808,
     'norm_ffn_g_2': 64.0,
     'conv_b_2': 64.0,
     'mla_q_norm_g_2': 64.0,
     'mla_w_q_up_2': 10.459,
     'mla_kv_norm_g_2': 64.0,
     'mla_qn_nope_g_2': 64.0,
     'mla_qn_rope_g_2': 64.0,
     'mla_kn_nope_g_2': 64.0,
     'mla_kn_rope_g_2': 64.0,
     'c_ctx_2': 3.572,
     'mla_w_in_2': 2.849,
     'mla_w_kv_up_2': 2.822,
     'mla_w_out_2': 2.831}
    for name, (base, spread) in spreads.items():
        noise = np.random.default_rng([zlib.crc32(name.encode()), seed]).standard_normal(out[name].shape)
        drawn = base * np.exp(spread * noise) if base else spread * noise
        out[name] = jnp.asarray(drawn.astype(out[name].dtype))
    for name, factor in factors.items():
        out[name] = (out[name] * factor).astype(out[name].dtype)
    return out
```

```python
import contextlib
from collections import Counter

import concourse.bass as bass
import numpy as np
from concourse import mybir

P = 128
D = 1024
KT = D // P
SEQ = 256
NT = SEQ // P
CHUNK = 4096
COLS = 512
EPS = 1e-6

POOL_WINDOWS = (2, 4, 8, 16)
POOL = 512
HEADS = 8
HD = 64
KVH = 2
IN_W = 3328
Q0, K0, V0, G0 = POOL, POOL + HEADS * HD, POOL + HEADS * HD + KVH * HD, POOL + HEADS * HD + 2 * KVH * HD
ROT = 16
FF = 4096

FH = 2816
MH = 16
GH = 4
NOPE, ROPE, VD = 64, 32, 64
QK = NOPE + ROPE
QL, KVL = 768, 256
QKT, KVT = QL // P, KVL // P
KEYS = 2 * SEQ

SECTIONS = (
    ("mod_head", 3, 4096), ("w_in", 2, 4096), ("mod_last", 1, 4096), ("w_kv", 1, 2048), ("w_gates", 4, 4096), ("w_branch", 2, 4096),
    ("w_out", 2, 4096), ("mlp", 24, 4096), ("mod_gate0", 2, 4096), ("conv_in", 8, 3072), ("conv_out", 2, 4096),
    ("mod_gate1", 2, 4096), ("ffn0", 20, 4096), ("ffn0_half", 1, 2048),
    ("mod_gate2", 2, 4096), ("mla_in", 2, 4096), ("mod_gate3", 2, 4096), ("mla_up", 4, 3328), ("mla_out", 2, 4096),
    ("ffn1", 16, 4096), ("ffn1_half", 1, 2048),
)
STREAM = sum(n for _, n, _ in SECTIONS)
X_UPDATES = 16

COL_NAMES = (("g_mix", KT), ("g_mlp", KT), ("pool_scale", 4), ("norm_mix", 2 * KT), ("norm_ffn", 2 * KT),
             ("q_norm", QKT), ("kv_norm", KVT), ("conv_k0", KT), ("conv_k1", KT), ("conv_k2", KT), ("conv_b", KT),
             ("cond", 2 * KT), ("mod_b", 64))
COL, _at = {}, 0
for _name, _n in COL_NAMES:
    COL[_name] = _at
    _at += _n
NCOL = _at

ROW_NAMES = (("sinks", HEADS), ("qn_nope", NOPE), ("qn_rope", ROPE), ("kn_nope", NOPE), ("kn_rope", ROPE))
ROW, _at = {}, 0
for _name, _n in ROW_NAMES:
    ROW[_name] = _at
    _at += _n
NROW = _at

TAB_NAMES = (("ident", P), ("cos1", NT * 8), ("sin1", NT * 8), ("cosm", NT * ROPE), ("sinm", NT * ROPE),
             ("sel_col", 2), ("sel_row", 2 * P))
TAB, _at = {}, 0
for _name, _n in TAB_NAMES:
    TAB[_name] = _at
    _at += _n
NTAB = _at


class Count:

    def __init__(self):
        self.n, self.turn, self.per = Counter(), None, {}

    def at(self, name, back=0):
        value = self.n[name] - back
        assert value >= 0, name
        if self.turn is not None and self.per.get(name):
            assert value > 0, name
            return self.turn * self.per[name] + value
        return value

    def step(self, name, k=1):
        self.n[name] += k
        return self.at(name)

    @contextlib.contextmanager
    def loop(self, eng, turns, **per):
        start = Counter(self.n)
        with eng.Fori(0, turns) as i:
            self.turn, self.per = i, per
            yield i
        for name in set(self.n) | set(per):
            assert self.n[name] - start[name] == per.get(name, 0), (name, self.n[name] - start[name], per)
            self.n[name] = start[name] + turns * per.get(name, 0)
        self.turn, self.per = None, {}


def build(nc, a, out):
    f32, f32r = mybir.dt.float32, mybir.dt.float32r
    ACT, ALU, AX = mybir.ActivationFunctionType, mybir.AluOpType, mybir.AxisListType

    base = -(-nc.sbuf_base // 64) * 64

    def at(name, shape, offset, dtype=f32):
        return nc.alloc_sbuf_tensor_at(name, shape, dtype, offset=base + offset)

    K = 1024
    raw = at("raw", [P, 2, CHUNK], 0)
    w_hi = at("w_hi", [P, 2, CHUNK], 32 * K, f32r)
    w_lo = at("w_lo", [P, 2, CHUNK], 64 * K, f32r)
    x = at("x", [P, NT, D], 96 * K)
    ACT0 = 104 * K
    act_hi = at("act_hi", [P, 2, KT, SEQ], ACT0, f32r)
    act_lo = at("act_lo", [P, 2, KT, SEQ], ACT0 + 16 * K, f32r)
    XN0 = 136 * K
    xn = at("xn", [P, 2, D], XN0)
    scaled = at("scaled", [P, 2, COLS], XN0 + 8 * K)
    M0 = XN0 + 12 * K
    cols = at("cols", [P, NCOL], M0)
    ROWS0 = M0 + -(-4 * NCOL // 32) * 32
    rows = at("rows", [P, NROW], ROWS0)
    TAB0 = ROWS0 + -(-4 * NROW // 32) * 32
    tab = at("tab", [P, NTAB], TAB0)
    M1 = TAB0 + -(-4 * NTAB // 32) * 32
    cond_w = at("cond_w", [P, KT, P], M1, f32r)
    cond_s = at("cond_s", [P, 2 * KT], M1 + 4 * K)
    mod_row = at("mod_row", [5, COLS], M1 + 4 * K + 64)
    mod_col = at("mod_col", [P, 64, 2], M1 + 6 * K + 64)
    stat = at("stat", [P, 160], M1 + 6 * K + 64 + 512)
    coef = at("coef", [P, 4, KT, 2], M1 + 6 * K + 64 + 512 + 640)
    PH = M1 + 6 * K + 64 + 512 + 640 + 256
    END = nc.sbuf_usable_end - base
    assert PH + 48 * K <= END, (PH, END)

    proj = at("proj", [P, NT, IN_W], PH)
    w_pool = at("w_pool", [P, 4, P], PH + 26 * K)
    diff = at("diff", [P, 4, SEQ], PH + 28 * K)
    qT = at("qT", [HD, HEADS, SEQ], PH + 32 * K)
    g_post1 = at("g_post1", [P, D], PH + 32 * K)
    kT = at("kT", [HD, KVH, SEQ], PH + 40 * K)
    pT = at("pT", [P, 2, 4, P], PH + 42 * K)
    mask = at("mask", [P, 2 * P], PH + 46 * K)
    ypool_hi = at("ypool_hi", [P, 4, SEQ], ACT0 + 8 * K, f32r)
    ypool_lo = at("ypool_lo", [P, 4, SEQ], ACT0 + 12 * K, f32r)
    yattn_hi = at("yattn_hi", [P, 4, SEQ], ACT0 + 24 * K, f32r)
    yattn_lo = at("yattn_lo", [P, 4, SEQ], ACT0 + 28 * K, f32r)
    pool_m = at("pool_m", [P, 4, 3, P], ACT0 + 24 * K)
    score = at("score", [P, 2, 2, 2 * P], XN0)
    prob = at("prob", [P, 4, 2, 2 * P], XN0 + 4 * K)
    rope_t = at("rope_t", [P, 4, NT, 10, 8], XN0)
    ctx = at("ctx", [P, NT, D], PH)
    h1_hi = at("h1_hi", [P, 8, SEQ], PH + 8 * K, f32r)
    h1_lo = at("h1_lo", [P, 8, SEQ], PH + 16 * K, f32r)
    mlp = at("mlp", [P, NT, D], PH + 24 * K)
    h1 = at("h1", [P, 2, NT, COLS], PH + 32 * K)
    g_post2 = at("g_post2", [P, D], PH + 40 * K)
    gate = at("gate", [P, 2, D], PH + 8 * K)
    conv_hi = at("conv_hi", [P, KT, 2, SEQ], PH + 16 * K, f32r)
    conv_lo = at("conv_lo", [P, KT, 2, SEQ], PH + 32 * K, f32r)
    c_sb = at("c_sb", [P, 2, SEQ], XN0)
    z_pad = at("z_pad", [P, 2, SEQ + 2], XN0 + 2 * K)
    conv_y = at("conv_y", [P, 2, SEQ], XN0 + 4 * K + 64)
    conv_m = at("conv_m", [P, 2, 2, SEQ], XN0 + 6 * K + 64)
    h2_hi = at("h2_hi", [P, 4, 2, SEQ], PH + 16 * K, f32r)
    h2_lo = at("h2_lo", [P, 4, 2, SEQ], PH + 24 * K, f32r)
    silu = at("silu", [P, 2, COLS], PH + 32 * K)
    h2 = at("h2", [P, 2, COLS], PH + 36 * K)
    gated = at("gated", [P, 2, COLS], XN0 + 8 * K)
    ql_hi = at("ql_hi", [P, QKT, SEQ], PH + 16 * K, f32r)
    ql_lo = at("ql_lo", [P, QKT, SEQ], PH + 22 * K, f32r)
    kvl_hi = at("kvl_hi", [P, KVT, KEYS], PH + 28 * K, f32r)
    kvl_lo = at("kvl_lo", [P, KVT, KEYS], PH + 32 * K, f32r)
    q_nat = at("q_nat", [P, NT, QL], PH + 36 * K)
    kv_nat = at("kv_nat", [P, 2 * NT, KVL], PH + 42 * K)
    pe = at("pe", [P, 2 * NT, ROPE], PH + 46 * K)
    pe_t = at("pe_t", [P, 2 * NT, ROPE], PH + 46 * K + 512)
    w_pe = at("w_pe", [P, KT, ROPE], PH)
    w_pe_hi = at("w_pe_hi", [P, KT, ROPE], PH + 1 * K, f32r)
    w_pe_lo = at("w_pe_lo", [P, KT, ROPE], PH + 2 * K, f32r)
    o_nat = at("o_nat", [P, NT, D], PH)
    qg = at("qg", [P, NT, GH, QK], PH + 36 * K)
    sq = at("sq", [P, 2 * NT * GH * NOPE], PH + 39 * K)
    qr_t = at("qr_t", [P, NT, GH, ROPE], PH + 43 * K)
    kg = at("kg", [P, 2 * NT, GH, QK], ACT0)
    vg = at("vg", [P, 2 * NT, GH, VD], ACT0 + 6 * K)
    qgT = at("qgT", [QK, GH, SEQ], ACT0 + 10 * K)
    kgT = at("kgT", [QK, GH, KEYS], ACT0 + 14 * K)
    pr = at("pr", [P, 2, KEYS], XN0)
    prT = at("prT", [P, 2, 4, P], XN0 + 4 * K)
    h3_hi = at("h3_hi", [P, 2, 4, SEQ], PH + 16 * K, f32r)
    h3_lo = at("h3_lo", [P, 2, 4, SEQ], PH + 24 * K, f32r)
    silu3 = at("silu3", [P, 2, 256], PH + 32 * K)
    h3 = at("h3", [P, 2, NT, 256], PH + 34 * K)

    def res(tt):
        return x[:, tt, :] if tt < NT else ctx[:, tt - NT, :]

    def col(name, j, n=1):
        return cols[:, COL[name] + j:COL[name] + j + n]

    def row(name, n):
        return rows[:, ROW[name]:ROW[name] + n]

    def table(name, n, parts=P, j=0):
        return tab[0:parts, TAB[name] + j:TAB[name] + j + n]

    ident = table("ident", P)

    SS, RT, RS = 0, 16, 32
    NM, LS, ES, RD = 48, 64, 80, 96
    MX, NSINK, EPSC = 112, 120, 128
    GQ = 0

    bank = [nc.alloc_psum_tensor(f"bank{i}", [P, COLS], f32) for i in range(4)]
    turned = [nc.alloc_psum_tensor(f"turned{i}", [P, COLS], f32) for i in range(2)]
    mod_ps = nc.alloc_psum_tensor("mod_ps", [P, COLS], f32)
    small = nc.alloc_psum_tensor("small", [P, COLS], f32)

    S = nc.alloc_semaphore
    loaded = [S("loaded0"), S("loaded1")]
    hi_ready = S("hi_ready")
    lo_ready = S("lo_ready")
    lo_ready_pool = S("lo_ready_pool")
    const_loaded = S("const_loaded")
    x_loaded = S("x_loaded")
    bias_loaded = S("bias_loaded")
    ctx_loaded = S("ctx_loaded")
    post1_loaded = S("post1_loaded")
    post2_loaded = S("post2_loaded")
    pe_loaded = S("pe_loaded")
    modbias_loaded = S("modbias_loaded")
    out_done = S("out_done")
    gemm_done = S("gemm_done")
    gemm_read = S("gemm_read")
    tr_done = S("tr_done")
    tr_read = S("tr_read")
    tr_hi = S("tr_hi")
    mod_done = S("mod_done")
    mod_row_ready = S("mod_row_ready")
    small_done = S("small_done")
    small_read = S("small_read")
    cond_silu = S("cond_silu")
    cond_hi = S("cond_hi")
    cond_zero = S("cond_zero")
    cond_ready = S("cond_ready")
    ss_done = S("ss_done")
    root_ready = S("root_ready")
    rstd_ready = S("rstd_ready")
    xn_ready = S("xn_ready")
    scaled_ready = S("scaled_ready")
    norm_hi = S("norm_hi")
    norm_ready = S("norm_ready")
    x_ready = S("x_ready")
    dve_chain = S("dve_chain")
    gates_ready = S("gates_ready")
    rope_ready = S("rope_ready")
    negmax_ready = S("negmax_ready")
    probs_ready = S("probs_ready")
    scores_done = S("scores_done")
    pv_done = S("pv_done")
    sink_in = S("sink_in")
    sink_exp = S("sink_exp")
    pool_hi = S("pool_hi")
    pool_lo = S("pool_lo")
    merged_ready = S("merged_ready")
    h_ready = S("h_ready")
    silu_ready = S("silu_ready")
    h_hi = S("h_hi")
    h_lo = S("h_lo")
    wpe_hi = S("wpe_hi")
    wpe_lo = S("wpe_lo")
    pe_root = S("pe_root")
    pe_sum = S("pe_sum")
    sq_ready = S("sq_ready")
    gsum_ready = S("gsum_ready")
    groot_ready = S("groot_ready")
    qk_ready = S("qk_ready")

    HALF = CHUNK // 2
    SHARE = 1408

    with nc.Block() as block:

        @block.sync
        def _(sp):
            n = Count()

            def load(section, k, width):
                c = n.step("chunk")
                slot = (n.n["chunk"] - 1) % 2
                if n.n["chunk"] > 2:
                    sp.wait_ge(lo_ready, 2 * n.at("chunk", 2))
                    sp.wait_ge(lo_ready_pool, 2 * n.at("chunk", 2))
                src = a[section][k] if isinstance(k, int) else a[section][bass.ds(k, 1)].rearrange("o p n -> (o p) n")
                sp.dma_start(raw[:, slot, 0:width], src).then_inc(loaded[slot], 16)

            for section, chunks, width in SECTIONS:
                first = 0
                while first < chunks and (chunks < 8 or n.n["chunk"] < 2):
                    load(section, first, width)
                    first += 1
                turns = (chunks - first) // 2
                if turns:
                    with n.loop(sp, turns, chunk=2) as i:
                        load(section, i * 2 + first, width)
                        load(section, i * 2 + first + 1, width)
                if (chunks - first) % 2:
                    load(section, chunks - 1, width)
            for t in range(NT):
                sp.wait_ge(x_ready, X_UPDATES)
                sp.dma_start(out[t * P:(t + 1) * P, :], x[:, t, :]).then_inc(out_done, 16)
            sp.wait_ge(out_done, 16 * NT)

        @block.gpsimd
        def _(pool):
            n = Count()

            def split():
                n.step("chunk")
                s = (n.n["chunk"] - 1) % 2
                for half in range(2):
                    part = slice(half * HALF + SHARE, (half + 1) * HALF)
                    pool.wait_ge(hi_ready, n.step("half"))
                    pool.tensor_tensor(w_lo[:, s, part], raw[:, s, part], w_hi[:, s, part].bitcast(f32),
                                       ALU.subtract).then_inc(lo_ready_pool, 1)

            with n.loop(pool, STREAM // 2, chunk=2, half=4):
                split()
                split()
            if STREAM % 2:
                split()

        @block.tensor
        def _(te):
            n = Count()

            def chunk():
                n.step("chunk")
                split_half(1)
                return (n.n["chunk"] - 1) % 2

            def split_half(back):
                te.wait_ge(lo_ready, 2 * n.at("chunk") - back)
                te.wait_ge(lo_ready_pool, 2 * n.at("chunk") - back)

            def weights(s, j0, j1):
                return w_hi[:, s, j0:j1], w_lo[:, s, j0:j1]

            rot = {"first": 0, "banks": 4}

            def rotation(banks):
                if n.n["unit"]:
                    te.wait_ge(gemm_read, n.at("unit"))
                rot["first"], rot["banks"] = n.n["unit"], banks

            def unit():
                n.step("unit")
                if n.n["unit"] > rot["banks"]:
                    te.wait_ge(gemm_read, n.at("unit", rot["banks"]))
                return bank[(n.n["unit"] - 1 - rot["first"]) % rot["banks"]]

            def product(dst, terms, second=None, also=None):
                for j, ((sh, sl), (mh, ml)) in enumerate(terms):
                    if j == second:
                        split_half(0)
                        if also:
                            also()
                    te.matmul(dst, sh, mh, start=(j == 0), stop=False)
                    te.matmul(dst, sh, ml, start=False, stop=False)
                    last = te.matmul(dst, sl, mh, start=False, stop=(j == len(terms) - 1))
                return last

            def act_rows(tt, k):
                t = slice((tt % NT) * P, (tt % NT + 1) * P)
                return act_hi[:, tt // NT, k, t], act_lo[:, tt // NT, k, t]

            def turn(pieces):
                n.step("tr")
                if n.n["tr"] > 2:
                    te.wait_ge(tr_read, n.at("tr", 2))
                dst = turned[(n.n["tr"] - 1) % 2]
                for j, src in enumerate(pieces):
                    m = src.shape[-1]
                    last = te.transpose(dst[0:m, j * P:(j + 1) * P], src, ident)
                last.then_inc(tr_done, 1)

            def turn_rows(buf):
                te.wait_ge(xn_ready, n.step("xn"))
                for half in range(2):
                    turn([xn[:, buf, (4 * half + j) * P:(4 * half + j + 1) * P] for j in range(4)])

            def mod_product():
                s = chunk()
                m = n.step("mod")
                if n.n["mod"] > 1:
                    te.wait_ge(mod_row_ready, n.at("mod", 1))
                for k in range(KT):
                    if k == KT // 2:
                        split_half(0)
                    h, l = weights(s, k * COLS, (k + 1) * COLS)
                    te.matmul(mod_ps[:, :], cond_w[:, k, :], h, start=(k == 0), stop=False)
                    last = te.matmul(mod_ps[:, :], cond_w[:, k, :], l, start=False, stop=(k == KT - 1))
                last.then_inc(mod_done, 1)

            def small_bank():
                n.step("small")
                if n.n["small"] > 1:
                    te.wait_ge(small_read, n.at("small", 1))

            def mod_columns():
                te.wait_ge(mod_row_ready, n.at("mod"))
                small_bank()
                for j in range(4):
                    last = te.matmul(small[:, 2 * j:2 * j + 2], mod_row[0:4, j * P:(j + 1) * P], table("sel_col", 2, 4),
                                     start=True, stop=True)
                last.then_inc(small_done, 1)

            def mod_gate(seqs):
                te.wait_ge(mod_row_ready, n.at("mod"))
                te.wait_ge(modbias_loaded, 16 * n.step("gate"))
                for s in range(seqs):
                    small_bank()
                    te.matmul(small[:, :], table("sel_row", P, 5, s * P), mod_row[0:5, :], start=True,
                              stop=True).then_inc(small_done, 1)

            te.wait_ge(const_loaded, 16 * 3)
            te.wait_ge(cond_ready, 1)
            mod_product()
            turn_rows(0)
            mod_columns()
            mod_product()
            turn_rows(1)
            mod_columns()
            mod_product()
            mod_columns()
            te.wait_ge(norm_ready, n.step("norm", 4))
            for width in (COLS, COLS, 256):
                if width == 256:
                    mod_product()
                s = chunk()
                for t in range(NT):
                    b = unit()
                    product(b[:, 0:width], [(act_rows(t, k), weights(s, k * width, (k + 1) * width)) for k in range(KT)],
                            second=0 if width < COLS else 4 if t == 0 else None).then_inc(gemm_done, 1)
                if width == 256:
                    mod_columns()
            te.wait_ge(gemm_read, n.at("unit"))
            for pair in range(2):
                b = unit()
                for g in (2 * pair, 2 * pair + 1):
                    d0, c0 = (g % 2) * SEQ, g * P
                    te.matmul(b[:, d0:d0 + P], proj[:, 0, c0:c0 + P], pool_m[:, g, 0, :], start=True, stop=True)
                    te.matmul(b[:, d0 + P:d0 + 2 * P], proj[:, 0, c0:c0 + P], pool_m[:, g, 1, :], start=True, stop=False)
                    last = te.matmul(b[:, d0 + P:d0 + 2 * P], proj[:, 1, c0:c0 + P], pool_m[:, g, 2, :], start=False, stop=True)
                last.then_inc(gemm_done, 1)

            def rows_chunk():
                s = chunk()
                for t in range(NT):
                    b = unit()
                    product(b[:, :], [(act_rows(t, k), weights(s, k * COLS, (k + 1) * COLS)) for k in range(KT)],
                            second=4 if t == 0 else None).then_inc(gemm_done, 1)

            rows_chunk()
            te.wait_ge(rope_ready, 1)
            for t in range(NT):
                for half in range(2):
                    turn([proj[:, t, Q0 + h * HD:Q0 + (h + 1) * HD] for h in range(4 * half, 4 * half + 4)])
            turn([proj[:, t, K0 + j * HD:K0 + (j + 1) * HD] for j in range(KVH) for t in range(NT)])
            rows_chunk()

            def scores(u):
                t, p = u // 4, u % 4
                nk = (t + 1) * P
                b = unit()
                for e in range(2):
                    last = te.matmul(b[:, e * nk:(e + 1) * nk], qT[:, 2 * p + e, t * P:(t + 1) * P], kT[:, p // 2, 0:nk],
                                     start=True, stop=True)
                last.then_inc(gemm_done, 1)

            def turn_probs(u):
                te.wait_ge(probs_ready, u + 1)
                turn([prob[:, u % 4, e, j * P:(j + 1) * P] for e in range(2) for j in range(u // 4 + 1)])

            def values(u, tr):
                t, p = u // 4, u % 4
                if p == 0:
                    small_bank()
                te.wait_ge(tr_read, tr)
                for e in range(2):
                    for j in range(t + 1):
                        last = te.matmul(small[:, (2 * p + e) * HD:(2 * p + e + 1) * HD], pT[:, u % 2, e * (t + 1) + j, :],
                                         proj[:, j, V0 + (p // 2) * HD:V0 + (p // 2 + 1) * HD], start=(j == 0), stop=(j == t))
                last.then_inc(pv_done, 1)

            def attend(first):
                trs = []
                for u in range(first, first + 4):
                    turn_probs(u)
                    trs.append(n.n["tr"])
                    if u > first:
                        values(u - 1, trs[-2])
                values(first + 3, trs[-1])

            te.wait_ge(tr_read, n.at("tr"))
            for u in range(2):
                scores(u)
            for pair in range(2):
                b = unit()
                for g in (2 * pair, 2 * pair + 1):
                    last = te.matmul(b[:, (g % 2) * SEQ:(g % 2 + 1) * SEQ], w_pool[:, g, :], diff[:, g, :], start=True, stop=True)
                last.then_inc(gemm_done, 1)
            for u in range(2, 4):
                scores(u)
            rows_chunk()
            attend(0)
            for u in range(4, 8):
                scores(u)
            rows_chunk()
            attend(4)

            def branch(hi, lo):
                s = chunk()
                for cb in range(2):
                    for t in range(NT):
                        b = unit()
                        product(b[:, :], [((hi[:, k, t * P:(t + 1) * P], lo[:, k, t * P:(t + 1) * P]),
                                           weights(s, (4 * cb + k) * COLS, (4 * cb + k + 1) * COLS)) for k in range(4)],
                                second=0 if cb == 1 and t == 0 else None).then_inc(gemm_done, 1)

            te.wait_ge(pool_lo, 2)
            branch(ypool_hi, ypool_lo)
            te.wait_ge(small_read, n.at("small"))
            for t in range(NT):
                turn([proj[:, t, j * P:(j + 1) * P] for j in range(4)])
            te.wait_ge(tr_read, n.at("tr"))
            branch(yattn_hi, yattn_lo)
            for half in range(2):
                for t in range(NT):
                    te.wait_ge(merged_ready, 2 * half + t + 1)
                    turn([proj[:, t, G0 + (4 * half + j) * P:G0 + (4 * half + j + 1) * P] for j in range(4)])
            te.wait_ge(tr_read, n.at("tr"))
            for cb in range(2):
                rows_chunk()
            turn_rows(0)
            turn_rows(1)
            te.wait_ge(norm_ready, n.step("norm", 4))

            def up(k):
                s = chunk()
                for t in range(NT):
                    b = unit()
                    product(b[:, :], [(act_rows(t, j), weights(s, j * COLS, (j + 1) * COLS)) for j in range(KT)],
                            second=4 if t == 0 else None).then_inc(gemm_done, 1)

            def turn_hidden(k):
                for t in range(NT):
                    te.wait_ge(h_ready, n.step("hidden"))
                    turn([h1[:, k, t, j * P:(j + 1) * P] for j in range(4)])

            def down():
                s = chunk()
                for t in range(NT):
                    b = unit()
                    product(b[:, :], [((h1_hi[:, j, t * P:(t + 1) * P], h1_lo[:, j, t * P:(t + 1) * P]),
                                       weights(s, j * COLS, (j + 1) * COLS)) for j in range(8)],
                            second=4 if t == 0 else None, also=hidden_split).then_inc(gemm_done, 1)

            def hidden_split():
                te.wait_ge(tr_read, n.at("tr"))

            with n.loop(te, 4, chunk=6, unit=8, tr=4, mod=2, small=2, hidden=4):
                up(0)
                mod_product()
                turn_hidden(0)
                up(1)
                mod_columns()
                mod_product()
                turn_hidden(1)
                te.wait_ge(tr_read, n.at("tr", 2))
                down()
                mod_columns()
                down()
            for half in range(2):
                mod_product()
                turn_rows(half)
                mod_gate(2)
            for t in range(NT):
                turn_rows(t)
            te.wait_ge(norm_ready, n.step("norm", 8))
            rotation(3)

            def moving(k):
                return act_hi[:, :, k, :], act_lo[:, :, k, :]

            with n.loop(te, 4, chunk=2, unit=6):
                for f in range(2):
                    s = chunk()
                    for part in (1, 2, 0):
                        b = unit()
                        product(b[:, :].rearrange("p (s t) -> p s t", s=2),
                                [(weights(s, k * 384 + part * P, k * 384 + (part + 1) * P), moving(k)) for k in range(KT)],
                                second=5 if part == 1 else None).then_inc(gemm_done, 1)
            rotation(4)
            te.wait_ge(h_lo, n.step("h", 8))
            for cb in range(2):
                s = chunk()
                for tt in range(2 * NT):
                    b = unit()
                    q, t = tt // NT, slice((tt % NT) * P, (tt % NT + 1) * P)
                    product(b[:, :], [((conv_hi[:, k, q, t], conv_lo[:, k, q, t]), weights(s, k * COLS, (k + 1) * COLS))
                                      for k in range(KT)], second=4 if tt == 0 else None).then_inc(gemm_done, 1)
            for half in range(2):
                mod_product()
                turn_rows(0)
                turn_rows(1)
                mod_gate(2)
            te.wait_ge(norm_ready, n.step("norm", 8))

            def gate_up():
                s = chunk()
                for f in range(2):
                    for part in range(2):
                        b = unit()
                        product(b[:, :].rearrange("p (s t) -> p s t", s=2),
                                [(weights(s, k * COLS + part * 256 + f * P, k * COLS + part * 256 + (f + 1) * P), moving(k))
                                 for k in range(KT)], second=4 if f == part == 0 else None).then_inc(gemm_done, 1)

            def down0(kts):
                te.wait_ge(h_lo, n.step("h", kts))
                s = chunk()
                for cb in range(2):
                    for tt in range(2 * NT):
                        b = unit()
                        q, t = tt // NT, slice((tt % NT) * P, (tt % NT + 1) * P)
                        product(b[:, :], [((h2_hi[:, k, q, t], h2_lo[:, k, q, t]),
                                           weights(s, (kts * cb + k) * COLS, (kts * cb + k + 1) * COLS)) for k in range(kts)],
                                second=0 if cb == 1 and tt == 0 else None).then_inc(gemm_done, 1)

            with n.loop(te, 4, chunk=4, unit=16, mod=1, small=1, h=4):
                gate_up()
                gate_up()
                mod_product()
                down0(4)
                mod_columns()
            gate_up()
            gate_up()
            down0(4)
            gate_up()
            down0(2)
            for half in range(2):
                mod_product()
                turn_rows(0)
                turn_rows(1)
                mod_gate(1)
            te.wait_ge(norm_ready, n.step("norm", 8))
            s = chunk()
            for t in range(NT):
                b = unit()
                product(b[:, :], [(act_rows(t, k), weights(s, k * COLS, (k + 1) * COLS)) for k in range(KT)],
                        second=4 if t == 0 else None).then_inc(gemm_done, 1)
            s = chunk()
            for tt in range(2 * NT):
                b = unit()
                first = 0 if tt < NT else 256
                product(b[:, first:COLS], [(act_rows(tt, k), weights(s, k * COLS + first, (k + 1) * COLS)) for k in range(KT)],
                        second=4 if tt == 0 else None).then_inc(gemm_done, 1)
            b = unit()
            te.wait_ge(wpe_lo, 1)
            for tt in range(2 * NT):
                last = product(b[:, tt * ROPE:(tt + 1) * ROPE],
                               [(act_rows(tt, k), (w_pe_hi[:, k, :], w_pe_lo[:, k, :])) for k in range(KT)])
            last.then_inc(gemm_done, 1)
            mod_product()
            for t in range(NT):
                te.wait_ge(xn_ready, n.step("xn"))
                turn([xn[:, t, j * P:(j + 1) * P] for j in range(4)])
                turn([xn[:, t, j * P:(j + 1) * P] for j in range(4, QKT)])
            mod_gate(1)
            mod_product()
            for q in range(2):
                te.wait_ge(xn_ready, n.step("xn", 2))
                turn([kv_nat[:, 2 * q + t, k * P:(k + 1) * P] for k in range(KVT) for t in range(NT)])
            mod_gate(1)
            te.wait_ge(norm_ready, n.step("norm", 6))
            def heads_group():
                rotation(4)
                s = chunk()
                for t in range(NT):
                    b = unit()
                    product(b[:, 0:GH * QK], [((ql_hi[:, k, t * P:(t + 1) * P], ql_lo[:, k, t * P:(t + 1) * P]),
                                               weights(s, k * GH * QK, (k + 1) * GH * QK)) for k in range(QKT)],
                            second=5 if t == 0 else None).then_inc(gemm_done, 1)
                for tt in range(2 * NT):
                    b = unit()
                    product(b[:, :], [((kvl_hi[:, k, tt * P:(tt + 1) * P], kvl_lo[:, k, tt * P:(tt + 1) * P]),
                                       weights(s, QKT * GH * QK + k * COLS, QKT * GH * QK + (k + 1) * COLS)) for k in range(KVT)]
                            ).then_inc(gemm_done, 1)
                te.wait_ge(tr_read, n.at("tr"))
                te.wait_ge(qk_ready, n.step("qk"))
                for tt in range(2 * NT):
                    turn([kg[:, tt, h, :] for h in range(GH)])
                te.wait_ge(qk_ready, n.step("qk"))
                for t in range(NT):
                    turn([qg[:, t, h, :] for h in range(GH)])
                te.wait_ge(tr_read, n.at("tr"))
                te.wait_ge(gemm_read, n.at("unit"))

                def mla_scores(u):
                    t, h = u // GH, u % GH
                    te.matmul(bank[u % 4][:, :], qgT[:, h, t * P:(t + 1) * P], kgT[:, h, :], start=True, stop=True).then_inc(scores_done, 1)

                def mla_values(u, tr):
                    h = u % GH
                    te.wait_ge(tr_read, tr)
                    for j in range(4):
                        last = te.matmul(small[:, u * VD:(u + 1) * VD], prT[:, u % 2, j, :], vg[:, j, h, :], start=(j == 0), stop=(j == 3))
                    last.then_inc(pv_done, 1)

                small_bank()
                for u in range(3):
                    mla_scores(u)
                trs = []
                for u in range(8):
                    te.wait_ge(probs_ready, 8 + n.step("probs"))
                    turn([pr[:, u % 2, j * P:(j + 1) * P] for j in range(4)])
                    trs.append(n.at("tr"))
                    if u + 3 < 8:
                        mla_scores(u + 3)
                    if u:
                        mla_values(u - 1, trs[u - 1])
                mla_values(7, trs[7])

            with n.loop(te, 2, chunk=2, unit=12, tr=28, small=2, probs=16, qk=4):
                heads_group()
                heads_group()
            te.wait_ge(small_read, n.at("small"))
            for half in range(2):
                for t in range(NT):
                    turn([o_nat[:, t, (4 * half + j) * P:(4 * half + j + 1) * P] for j in range(4)])
            te.wait_ge(tr_read, n.at("tr"))
            rotation(4)
            for cb in range(2):
                rows_chunk()
            turn_rows(0)
            turn_rows(1)
            te.wait_ge(norm_ready, n.step("norm", 4))

            def gate_up1():
                s = chunk()
                for t in range(NT):
                    b = unit()
                    product(b[:, :], [(act_rows(t, j), weights(s, j * COLS, (j + 1) * COLS)) for j in range(KT)],
                            second=4 if t == 0 else None).then_inc(gemm_done, 1)

            def turn_hidden1(p, k, since):
                for t in range(NT):
                    te.wait_ge(gemm_read, n.at("unit", since + 1 - t))
                    turn([h3[:, k, t, j * P:(j + 1) * P] for j in range(2)])

            def down1(p, kts):
                s = chunk()
                for cb in range(2):
                    for t in range(NT):
                        b = unit()
                        product(b[:, :], [((h3_hi[:, p, k, t * P:(t + 1) * P], h3_lo[:, p, k, t * P:(t + 1) * P]),
                                           weights(s, (kts * cb + k) * COLS, (kts * cb + k + 1) * COLS)) for k in range(kts)],
                                second=0 if cb == 1 and t == 0 else None).then_inc(gemm_done, 1)

            def group1(p):
                gate_up1()
                turn_hidden1(1 - p, 1, 2)
                gate_up1()
                turn_hidden1(p, 0, 2)
                te.wait_ge(tr_read, n.at("tr", 2))
                down1(1 - p, 4)

            gate_up1()
            gate_up1()
            turn_hidden1(0, 0, 2)
            with n.loop(te, 2, chunk=6, unit=16, tr=8):
                group1(1)
                group1(0)
            gate_up1()
            turn_hidden1(0, 1, 2)
            te.wait_ge(tr_read, n.at("tr"))
            down1(0, 4)
            turn_hidden1(1, 0, 4)
            te.wait_ge(tr_read, n.at("tr"))
            down1(1, 2)
            assert n.n["chunk"] == STREAM, (n.n["chunk"], STREAM)

        @block.scalar
        def _(act):
            n = Count()

            def split():
                n.step("split")
                c = n.n["split"]
                if c > STREAM:
                    return
                s = (c - 1) % 2
                turns = 16 * ((c + 1) // 2)
                if n.turn is not None:
                    turns = n.turn * (8 * n.per["split"]) + turns
                act.wait_ge(loaded[s], turns)
                if n.n["unit"]:
                    act.wait_ge(gemm_done, n.at("unit"))
                if n.n["mod"]:
                    act.wait_ge(mod_done, n.at("mod"))
                for half in range(2):
                    part = slice(half * HALF, (half + 1) * HALF)
                    act.activation(w_hi[:, s, part], raw[:, s, part], ACT.Copy).then_inc(hi_ready, 1)

            def roots(sources, width):
                for src, junk, k in sources:
                    if n.n["ss"]:
                        act.wait_ge(ss_done, n.at("ss"))
                    act.activation(junk, src, ACT.Square, accum_out=stat[:, SS + k:SS + k + 1]).then_inc(ss_done, 1)
                    n.step("ss")
                act.wait_ge(ss_done, n.at("ss"))
                for src, junk, k in sources:
                    act.activation(stat[:, RT + k:RT + k + 1], stat[:, SS + k:SS + k + 1], ACT.Sqrt,
                                   bias=stat[:, EPSC:EPSC + 1], scale=1.0 / width).then_inc(root_ready, 1)

            def rows_out(dst, src, k):
                act.wait_ge(rstd_ready, n.step("rstd"))
                act.activation(dst, src, ACT.Copy, scale=stat[:, RS + k:RS + k + 1]).then_inc(xn_ready, 1)
                n.step("xn")

            def scaled_hi(dsts, shifted):
                for dst in dsts:
                    n.step("tr")
                    n.step("scaled")
                    if shifted:
                        act.wait_ge(scaled_ready, n.step("shifted"))
                    else:
                        act.wait_ge(tr_read, n.at("tr"))
                    k = (n.n["scaled"] - 1) % 2
                    act.activation(dst, scaled[:, k, 0:int(np.prod(dst.shape[1:]))].rearrange("p (a b) -> p a b", a=dst.shape[1]),
                                   ACT.Copy).then_inc(norm_hi, 1)

            def plain_hi(dst):
                n.step("tr")
                act.wait_ge(tr_done, n.at("tr"))
                k = (n.n["tr"] - 1) % 2
                width = int(np.prod(dst.shape[1:]))
                act.activation(dst, turned[k][:, 0:width].rearrange("p (a b) -> p a b", a=dst.shape[1]), ACT.Copy).then_inc(tr_hi, 1)

            def act_dst(hi, q, half, t):
                return hi[:, q, 4 * half:4 * half + 4, t * P:(t + 1) * P]

            def mod_copy(gate_row=None):
                n.step("mod")
                if n.n["small"]:
                    act.wait_ge(small_done, n.at("small"))
                if gate_row is not None:
                    act.dma_start(mod_row[4:5, :], a["mod_gate_b"][gate_row:gate_row + 1, :]).then_inc(modbias_loaded, 16)
                act.wait_ge(mod_done, n.at("mod"))
                act.activation(mod_row[0:4, :], mod_ps[0:4, :], ACT.Copy).then_inc(mod_row_ready, 1)

            act.dma_start(tab[:, :], a["tab"]).then_inc(const_loaded, 16)
            act.dma_start(cols[:, :], a["cols"]).then_inc(const_loaded, 16)
            act.dma_start(rows[:, :], a["rows"].rearrange("(o n) -> o n", o=1).to_broadcast([P, NROW])).then_inc(const_loaded, 16)
            act.dma_start(x[:, :, :], a["x"].rearrange("(t p) d -> p t d", p=P)).then_inc(x_loaded, 16)
            for t in range(NT):
                act.dma_start(proj[:, t, :], a["b_in"].rearrange("(o n) -> o n", o=1).to_broadcast([P, IN_W])).then_inc(bias_loaded, 16)
            act.dma_start(pool_m[:, :, :, :], a["pool_m"]).then_inc(bias_loaded, 16)
            act.dma_start(mask[:, :], a["mask"]).then_inc(bias_loaded, 16)
            act.dma_start(w_pool[:, :, :], a["w_pool"].rearrange("g c d -> c g d")).then_inc(bias_loaded, 16)
            act.wait_ge(const_loaded, 48)
            act.activation(cond_s[:, :], col("cond", 0, 2 * KT), ACT.Silu).then_inc(cond_silu, 1)
            act.wait_ge(cond_silu, 1)
            act.wait_ge(cond_zero, 2)
            act.activation(cond_w[:, :, 0:3:2], cond_s[:, :].rearrange("p (k s) -> p k s", s=2), ACT.Copy).then_inc(cond_hi, 1)
            act.wait_ge(x_loaded, 16)
            roots([(x[:, t, :], xn[:, t, :], t) for t in range(NT)], D)
            split()
            for t in range(NT):
                rows_out(xn[:, t, :], x[:, t, :], t)
            for t in range(NT):
                split()
                mod_copy()
                scaled_hi([act_dst(act_hi, 0, half, t) for half in range(2)], False)
                n.step("small")
            split()
            mod_copy()
            n.step("small")
            for k in range(3):
                if k == 2:
                    split()
                    mod_copy()
                split()
                n.step("unit", 2)
                if k == 2:
                    n.step("small")
            n.step("unit", 2)

            def gates_sigmoid(k):
                split()
                for t in range(NT):
                    act.wait_ge(gemm_read, n.step("unit"))
                    g = proj[:, t, G0 + k * COLS:G0 + (k + 1) * COLS]
                    act.activation(g, g, ACT.Sigmoid).then_inc(gates_ready, 1)

            def exps(u):
                t, nk = u // 4, (u // 4 + 1) * P
                n.step("unit")
                act.wait_ge(negmax_ready, u + 1)
                if u >= 4:
                    act.wait_ge(tr_done, probs_turned[u - 4])
                for e in range(2):
                    last = act.activation(prob[:, u % 4, e, 0:nk], score[:, u % 2, e, 0:nk], ACT.Exp,
                                          bias=stat[:, NM + 2 * u + e:NM + 2 * u + e + 1],
                                          accum_out=stat[:, LS + 2 * u + e:LS + 2 * u + e + 1])
                last.then_inc(probs_ready, 1)

            probs_turned = {}

            def probs_out(first):
                for u in range(first, first + 4):
                    probs_turned[u] = n.step("tr")
                t = first // 4
                act.wait_ge(sink_in, t + 1)
                act.activation(stat[:, ES + 8 * t:ES + 8 * t + 8], stat[:, ES + 8 * t:ES + 8 * t + 8], ACT.Exp).then_inc(sink_exp, 1)

            gates_sigmoid(0)
            n.step("tr", 5)
            gates_sigmoid(1)
            exps(0)
            exps(1)
            for pair in range(2):
                act.wait_ge(gemm_read, n.step("unit"))
                act.activation(ypool_hi[:, 2 * pair:2 * pair + 2, :], diff[:, 2 * pair:2 * pair + 2, :], ACT.Copy).then_inc(pool_hi, 1)
            exps(2)
            exps(3)
            gates_sigmoid(2)
            probs_out(0)
            for u in range(4, 8):
                exps(u)
            gates_sigmoid(3)
            probs_out(4)
            act.wait_ge(gemm_done, n.at("unit"))
            act.dma_start(g_post1[:, :], a["g_mix_post"].rearrange("(o n) -> o n", o=1).to_broadcast([P, D])).then_inc(post1_loaded, 16)
            split()
            n.step("unit", 4)
            for t in range(NT):
                plain_hi(yattn_hi[:, 0:4, t * P:(t + 1) * P])
            split()
            n.step("unit", 4)
            for half in range(2):
                for t in range(NT):
                    plain_hi(act_dst(act_hi, 0, half, t))
            for cb in range(2):
                split()
                n.step("unit", 2)
            act.wait_ge(gemm_read, n.at("unit"))
            roots([(proj[:, t, 0:D], diff[:, :, :].rearrange("p a b -> p (a b)"), t) for t in range(NT)], D)
            n.step("rstd", 2)
            act.wait_ge(x_ready, n.step("x", 2))
            act.dma_start(ctx[:, :, :], a["ctx"].rearrange("(t p) d -> p t d", p=P)).then_inc(ctx_loaded, 16)
            act.dma_start(g_post2[:, :], a["g_mlp_post"].rearrange("(o n) -> o n", o=1).to_broadcast([P, D])).then_inc(post2_loaded, 16)
            roots([(x[:, t, :], xn[:, t, :], t) for t in range(NT)], D)
            for t in range(NT):
                rows_out(xn[:, t, :], x[:, t, :], t)
            scaled_hi([act_dst(act_hi, 0, half, t) for t in range(NT) for half in range(2)], False)
            act.wait_ge(ctx_loaded, 16)
            roots([(ctx[:, t, :], xn[:, t, :], t) for t in range(NT)], D)
            for t in range(NT):
                rows_out(xn[:, t, :], ctx[:, t, :], t)

            def square_hidden(k):
                split()
                for t in range(NT):
                    act.wait_ge(gemm_read, n.step("unit"))
                    act.activation(h1[:, k, t, :], h1[:, k, t, :], ACT.Square).then_inc(h_ready, 1)

            with n.loop(act, 4, split=6, unit=8, tr=4, mod=2, small=2):
                square_hidden(0)
                split()
                mod_copy()
                for t in range(NT):
                    plain_hi(h1_hi[:, 0:4, t * P:(t + 1) * P])
                square_hidden(1)
                n.step("small")
                split()
                mod_copy()
                for t in range(NT):
                    plain_hi(h1_hi[:, 4:8, t * P:(t + 1) * P])
                split()
                n.step("unit", 2)
                n.step("small")
                split()
                n.step("unit", 2)
            act.wait_ge(gemm_read, n.at("unit"))
            roots([(mlp[:, t, :], h1[:, 0, :, :].rearrange("p a b -> p (a b)"), t) for t in range(NT)], D)
            n.step("rstd", 2)
            for half in range(2):
                split()
                mod_copy(half)
                scaled_hi([act_dst(act_hi, 1, k, half) for k in range(2)], True)
                n.step("small", 2)
            act.wait_ge(x_ready, n.step("x", 2))
            act.wait_ge(tr_done, n.at("tr"))
            roots([(x[:, t, :], xn[:, t, :], t) for t in range(NT)], D)
            for t in range(NT):
                rows_out(xn[:, t, :], x[:, t, :], t)
            scaled_hi([act_dst(act_hi, 0, half, t) for t in range(NT) for half in range(2)], True)
            act.wait_ge(tr_done, n.at("tr"))
            with n.loop(act, 4, split=2, unit=6) as i:
                for f in range(2):
                    split()
                    n.step("unit", 3)
                    act.wait_ge(gemm_read, n.at("unit"))
                    act.activation(conv_hi[:, bass.ds(i * 2 + f, 1), :, :].rearrange("p o s t -> p (o s) t"),
                                   conv_m[:, f, :, :], ACT.Copy).then_inc(h_hi, 1)
            for cb in range(2):
                split()
                n.step("unit", 4)

            def norm_both(gate_row, seqs):
                act.wait_ge(x_ready, n.step("x", 4))
                roots([(res(tt), xn[:, tt % 2, :], tt) for tt in range(2 * NT)], D)
                for q in range(2):
                    split()
                    mod_copy(gate_row + q)
                    if q:
                        act.wait_ge(tr_done, n.at("tr"))
                    for t in range(NT):
                        rows_out(xn[:, t, :], res(NT * q + t), NT * q + t)
                    scaled_hi([act_dst(act_hi, q, half, t) for t in range(NT) for half in range(2)], True)
                    n.step("small", seqs)

            norm_both(2, 2)

            def silu_chunk():
                split()
                for f in range(2):
                    n.step("unit")
                    act.wait_ge(gemm_done, n.at("unit"))
                    b = bank[(2 * f) % 4]
                    act.activation(silu[:, f, :], b[:, :], ACT.Silu).then_inc(silu_ready, 1)
                    n.step("unit")
                    act.wait_ge(gemm_read, n.at("unit"))
                    n.step("hidden")
                    k = (n.n["hidden"] - 1) % 4
                    act.activation(h2_hi[:, k, :, :], h2[:, f, :].rearrange("p (s t) -> p s t", s=2), ACT.Copy).then_inc(h_hi, 1)

            with n.loop(act, 4, split=4, unit=16, mod=1, small=1, hidden=4):
                silu_chunk()
                silu_chunk()
                split()
                mod_copy()
                split()
                n.step("unit", 8)
                n.step("small")
            silu_chunk()
            silu_chunk()
            split()
            n.step("unit", 8)
            silu_chunk()
            split()
            n.step("unit", 8)
            norm_both(4, 1)
            act.wait_ge(xn_ready, n.at("xn"))
            act.dma_start(w_pe[:, :, :], a["w_pe"]).then_inc(pe_loaded, 16)
            split()
            n.step("unit", 2)
            split()
            act.wait_ge(pe_loaded, 16)
            act.activation(w_pe_hi[:, :, :], w_pe[:, :, :], ACT.Copy).then_inc(wpe_hi, 1)
            n.step("unit", 4)
            act.wait_ge(tr_done, n.at("tr"))
            act.wait_ge(gemm_read, n.at("unit"))
            roots([(q_nat[:, t, :], xn[:, t, 0:QL], t) for t in range(NT)], QL)
            roots([(kv_nat[:, tt, :], scaled[:, 0, 0:KVL], 4 + tt) for tt in range(2 * NT)], KVL)
            n.step("unit")
            for t in range(NT):
                rows_out(xn[:, t, 0:QL], q_nat[:, t, :], t)
            for tt in range(2 * NT):
                rows_out(kv_nat[:, tt, :], kv_nat[:, tt, :], 4 + tt)
            act.wait_ge(pe_sum, 1)
            act.activation(stat[:, RT + 8:RT + 12], stat[:, SS + 8:SS + 12], ACT.Sqrt, bias=stat[:, EPSC:EPSC + 1],
                           scale=1.0 / ROPE).then_inc(pe_root, 1)
            split()
            mod_copy(6)
            scaled_hi([dst for t in range(NT) for dst in (ql_hi[:, 0:4, t * P:(t + 1) * P], ql_hi[:, 4:6, t * P:(t + 1) * P])], False)
            n.step("small")
            split()
            mod_copy(7)
            scaled_hi([kvl_hi[:, 0:2, q * SEQ:(q + 1) * SEQ] for q in range(2)], False)
            n.step("small")
            act.wait_ge(tr_done, n.at("tr"))

            def heads_group():
                split()
                for t in range(NT):
                    b = bank[t]
                    act.wait_ge(gemm_done, n.step("unit"))
                    act.activation(qg[:, t, :, :].rearrange("p h d -> p (h d)"), b[:, 0:GH * QK], ACT.Copy).then_inc(gemm_read, 1)
                for tt in range(2 * NT):
                    b = bank[(NT + tt) % 4]
                    act.wait_ge(gemm_done, n.step("unit"))
                    kv = b[:, :].rearrange("p (h d) -> p h d", h=GH)
                    act.activation(kg[:, tt, :, 0:NOPE], kv[:, :, 0:NOPE], ACT.Copy)
                    act.activation(vg[:, tt, :, :], kv[:, :, NOPE:NOPE + VD], ACT.Copy).then_inc(gemm_read, 1)
                act.wait_ge(gemm_read, n.at("unit"))
                act.activation(sq[:, :].rearrange("p (a d) -> p a d", d=NOPE), kg[:, :, :, 0:NOPE].rearrange("p t h d -> p (t h) d"),
                               ACT.Square).then_inc(sq_ready, 1)
                act.wait_ge(gsum_ready, n.step("gsum"))
                act.activation(stat[:, GQ + 16:GQ + 32], stat[:, GQ:GQ + 16], ACT.Sqrt, bias=stat[:, EPSC:EPSC + 1],
                               scale=1.0 / NOPE).then_inc(groot_ready, 1)
                act.activation(sq[:, 0:NT * GH * QK], qg[:, :, :, :].rearrange("p t h d -> p (t h d)"), ACT.Square).then_inc(sq_ready, 1)
                act.wait_ge(gsum_ready, n.step("gsum"))
                act.activation(stat[:, GQ + 16:GQ + 24], stat[:, GQ:GQ + 8], ACT.Sqrt, bias=stat[:, EPSC:EPSC + 1],
                               scale=1.0 / NOPE)
                act.activation(stat[:, GQ + 24:GQ + 32], stat[:, GQ + 8:GQ + 16], ACT.Sqrt, bias=stat[:, EPSC:EPSC + 1],
                               scale=1.0 / ROPE).then_inc(groot_ready, 1)
                for tt in range(2 * NT):
                    act.wait_ge(tr_done, n.step("tr"))
                    k = (n.n["tr"] - 1) % 2
                    act.activation(kgT[:, :, tt * P:(tt + 1) * P], turned[k][0:QK, :].rearrange("p (h t) -> p h t", h=GH),
                                   ACT.Copy).then_inc(tr_read, 1)
                for t in range(NT):
                    act.wait_ge(tr_done, n.step("tr"))
                    k = (n.n["tr"] - 1) % 2
                    act.activation(qgT[:, :, t * P:(t + 1) * P], turned[k][0:QK, :].rearrange("p (h t) -> p h t", h=GH),
                                   ACT.Copy).then_inc(tr_read, 1)
                for u in range(8):
                    act.wait_ge(negmax_ready, 8 + n.step("negmax"))
                    if u >= 2:
                        act.wait_ge(tr_done, n.at("tr", 1))
                    act.activation(pr[:, u % 2, :], bank[u % 4][:, :], ACT.Exp, bias=stat[:, NM + u:NM + u + 1], scale=QK ** -0.5,
                                   accum_out=stat[:, LS + u:LS + u + 1]).then_inc(probs_ready, 1)
                    n.step("tr")

            with n.loop(act, 2, split=2, unit=12, tr=28, gsum=4, negmax=16):
                heads_group()
                heads_group()
            for half in range(2):
                for t in range(NT):
                    plain_hi(act_dst(act_hi, 0, half, t))
            for cb in range(2):
                split()
                n.step("unit", 2)
            act.wait_ge(x_ready, n.step("x", 2))
            roots([(x[:, t, :], xn[:, t, :], t) for t in range(NT)], D)
            for t in range(NT):
                rows_out(xn[:, t, :], x[:, t, :], t)
            scaled_hi([act_dst(act_hi, 0, half, t) for t in range(NT) for half in range(2)], True)

            def silu_rows(k):
                split()
                for t in range(NT):
                    act.wait_ge(gemm_done, n.step("unit"))
                    act.wait_ge(gemm_read, n.at("unit", 2))
                    b = bank[(2 * k + t) % 4]
                    act.activation(silu3[:, t, :], b[:, 0:256], ACT.Silu).then_inc(silu_ready, 1)

            def turned_hi(p, k):
                for t in range(NT):
                    plain_hi(h3_hi[:, p, 2 * k:2 * k + 2, t * P:(t + 1) * P])

            def group1(p):
                silu_rows(0)
                turned_hi(1 - p, 1)
                silu_rows(1)
                turned_hi(p, 0)
                split()
                n.step("unit", 4)

            silu_rows(0)
            silu_rows(1)
            turned_hi(0, 0)
            with n.loop(act, 2, split=6, unit=16, tr=8):
                group1(1)
                group1(0)
            silu_rows(0)
            turned_hi(0, 1)
            split()
            n.step("unit", 4)
            turned_hi(1, 0)
            split()

        @block.vector
        def _(ve):
            n = Count()

            def chained(ins):
                ins.then_inc(dve_chain, 1)
                ve.wait_ge(dve_chain, n.step("chain"))

            def split():
                n.step("split")
                if n.n["split"] > STREAM:
                    return
                s = (n.n["split"] - 1) % 2
                for half in range(2):
                    part = slice(half * HALF, half * HALF + SHARE)
                    ve.wait_ge(hi_ready, 2 * n.at("split") - 1 + half)
                    ve.tensor_tensor(w_lo[:, s, part], raw[:, s, part], w_hi[:, s, part].bitcast(f32),
                                     ALU.subtract).then_inc(lo_ready, 1)

            rot = {"first": 0, "banks": 4}

            def rotation(banks):
                rot["first"], rot["banks"] = n.n["unit"], banks

            def unit():
                ve.wait_ge(gemm_done, n.step("unit"))
                return bank[(n.n["unit"] - 1 - rot["first"]) % rot["banks"]]

            def recips(ks):
                for k in ks:
                    ve.wait_ge(root_ready, n.step("root"))
                    ve.reciprocal(stat[:, RS + k:RS + k + 1], stat[:, RT + k:RT + k + 1]).then_inc(rstd_ready, 1)
                    n.step("rstd")

            def scaled_rows(items):
                def lower(hi, lo):
                    ve.wait_ge(norm_hi, n.step("norm"))
                    k = (n.n["norm"] - 1) % 2
                    src = scaled[:, k, 0:int(np.prod(lo.shape[1:]))].rearrange("p (a b) -> p a b", a=lo.shape[1])
                    ve.tensor_tensor(lo, src, hi.bitcast(f32), ALU.subtract).then_inc(norm_ready, 1)

                before = None
                for gain, shift, hi, lo in items:
                    n.step("scaled")
                    ve.wait_ge(tr_done, n.step("tr"))
                    k, b = (n.n["scaled"] - 1) % 2, (n.n["tr"] - 1) % 2
                    m, w = lo.shape[1], lo.shape[2]
                    dst = scaled[:, k, 0:m * w].rearrange("p (a b) -> p a b", a=m)
                    if n.n["scaled"] > 2:
                        ve.wait_ge(norm_ready, n.at("scaled", 2))
                    src = turned[b][:, 0:m * w].rearrange("p (a b) -> p a b", a=m)
                    ve.tensor_tensor(dst, src, gain.to_broadcast([P, m, w]), ALU.mult).then_inc(tr_read, 1)
                    if shift is not None:
                        ve.wait_ge(tr_read, n.at("tr"))
                        ve.tensor_tensor(dst, dst, shift.to_broadcast([P, m, w]), ALU.add).then_inc(scaled_ready, 1)
                    if before:
                        lower(*before)
                    before = (hi, lo)
                lower(*before)

            def plain_rows(hi, lo):
                n.step("tr")
                ve.wait_ge(tr_hi, n.step("tr_hi"))
                b = (n.n["tr"] - 1) % 2
                m, w = lo.shape[1], lo.shape[2]
                ve.tensor_tensor(lo, turned[b][:, 0:m * w].rearrange("p (a b) -> p a b", a=m), hi.bitcast(f32),
                                 ALU.subtract).then_inc(tr_read, 1)

            def act_dst(buf, q, half, t):
                return buf[:, q, 4 * half:4 * half + 4, t * P:(t + 1) * P]

            def gain_cols(name, j, m):
                return col(name, j, m).rearrange("p (a o) -> p a o", o=1)

            def gained(name, t):
                return [(gain_cols(name, 4 * half, 4), None, act_dst(act_hi, 0, half, t), act_dst(act_lo, 0, half, t)) for half in range(2)]

            def modulated(c, shift_at, q, t):
                return [(coef[:, c, 4 * half:4 * half + 4, q:q + 1], mod_col[:, shift_at + 4 * half:shift_at + 4 * half + 4, q:q + 1],
                         act_dst(act_hi, q, half, t), act_dst(act_lo, q, half, t)) for half in range(2)]

            def coefs(c, name, layer, scale_at):
                chained(ve.scalar_tensor_tensor(coef[:, c, :, :], mod_col[:, scale_at:scale_at + KT, :], 1.0,
                                                gain_cols(name, layer * KT, KT).to_broadcast([P, KT, 2]), ALU.add, ALU.mult))

            def mod_read(chunk, turn=None, step=0):
                n.step("small")
                ve.wait_ge(small_done, n.step("mod_small"))
                if turn is None:
                    dst, b = mod_col[:, 4 * chunk:4 * chunk + 4, :], col("mod_b", 4 * chunk, 4)
                else:
                    dst = mod_col[:, bass.ds(turn * (4 * step) + 4 * chunk, 4), :]
                    b = cols[:, bass.ds(turn * (4 * step) + COL["mod_b"] + 4 * chunk, 4)]
                ve.tensor_tensor(dst, small[:, 0:8].rearrange("p (k s) -> p k s", s=2),
                                 b.rearrange("p (a o) -> p a o", o=1).to_broadcast([P, 4, 2]), ALU.add).then_inc(small_read, 1)

            def gate_read(half, slots):
                for s in slots:
                    n.step("small")
                    ve.wait_ge(small_done, n.step("mod_small"))
                    ve.tensor_copy(gate[:, s, half * COLS:(half + 1) * COLS], small[:, :]).then_inc(small_read, 1)

            def post_norm(src, g):
                for t in range(NT):
                    chained(ve.scalar_tensor_tensor(src(t), src(t), stat[:, RS + t:RS + t + 1], g[:, :], ALU.mult, ALU.mult))
                    ve.tensor_tensor(x[:, t, :], x[:, t, :], src(t), ALU.add).then_inc(x_ready, 1)

            ve.memset(cond_w[:, :, :].bitcast(f32), 0.0).then_inc(cond_zero, 1)
            ve.memset(stat[:, EPSC:EPSC + 1], EPS).then_inc(cond_zero, 1)
            ve.wait_ge(const_loaded, 48)
            ve.tensor_scalar(stat[:, NSINK:NSINK + 8], row("sinks", HEADS), -1.0, None, ALU.mult)
            ve.tensor_tensor(row("kn_nope", NOPE), row("kn_nope", NOPE), row("qn_nope", NOPE), ALU.mult)
            ve.wait_ge(cond_hi, 1)
            ve.tensor_tensor(cond_w[:, :, 1:4:2], cond_s[:, :].rearrange("p (k s) -> p k s", s=2),
                             cond_w[:, :, 0:3:2].bitcast(f32), ALU.subtract).then_inc(cond_ready, 1)
            recips([0, 1])
            split()
            for t in range(NT):
                split()
                scaled_rows(gained("g_mix", t))
                mod_read(t)
            split()
            mod_read(2)
            ve.wait_ge(bias_loaded, 80)
            for k, (c0, width) in enumerate(((0, COLS), (Q0, COLS), (K0, 256))):
                if k == 2:
                    split()
                split()
                for t in range(NT):
                    b = unit()
                    dst = proj[:, t, c0:c0 + width]
                    ve.tensor_tensor(dst, b[:, 0:width], dst, ALU.add).then_inc(gemm_read, 1)
            mod_read(3)
            for pair in range(2):
                b = unit()
                ve.tensor_copy(diff[:, 2 * pair:2 * pair + 2, :].rearrange("p g t -> p (g t)"), b[:, :]).then_inc(gemm_read, 1)
            for t in range(NT):
                heads = proj[:, t, Q0:V0].rearrange("p (h d) -> p h d", d=HD)
                lo, hi = heads[:, :, 0:8], heads[:, :, 8:16]
                c = table("cos1", 8, j=8 * t).rearrange("p (o d) -> p o d", o=1).to_broadcast([P, 10, 8])
                s = table("sin1", 8, j=8 * t).rearrange("p (o d) -> p o d", o=1).to_broadcast([P, 10, 8])
                for j, (src, by) in enumerate(((lo, c), (hi, s), (hi, c), (lo, s))):
                    last = ve.tensor_tensor(rope_t[:, j, t, :, :], src, by, ALU.mult)
                chained(last)
                ve.tensor_tensor(lo, rope_t[:, 0, t, :, :], rope_t[:, 1, t, :, :], ALU.subtract)
                last = ve.tensor_tensor(hi, rope_t[:, 2, t, :, :], rope_t[:, 3, t, :, :], ALU.add)
            last.then_inc(rope_ready, 1)

            def gates_bias(k):
                split()
                for t in range(NT):
                    b = unit()
                    dst = proj[:, t, G0 + k * COLS:G0 + (k + 1) * COLS]
                    ve.tensor_tensor(dst, b[:, :], dst, ALU.add).then_inc(gemm_read, 1)

            gates_bias(0)
            for t in range(NT):
                for half in range(2):
                    ve.wait_ge(tr_done, n.step("tr"))
                    ve.tensor_copy(qT[:, 4 * half:4 * half + 4, t * P:(t + 1) * P],
                                   turned[(n.n["tr"] - 1) % 2][0:HD, :].rearrange("p (h t) -> p h t", h=4)).then_inc(tr_read, 1)
            ve.wait_ge(tr_done, n.step("tr"))
            ve.tensor_copy(kT[:, :, :], turned[(n.n["tr"] - 1) % 2][0:HD, :].rearrange("p (j t) -> p j t", j=KVH)).then_inc(tr_read, 1)
            gates_bias(1)

            def maxima(u):
                t, p = u // 4, u % 4
                nk = (t + 1) * P
                b = unit()
                if u >= 2:
                    ve.wait_ge(probs_ready, u - 1)
                seen = mask[:, (1 - t) * P:(1 - t) * P + nk].rearrange("p (o k) -> p o k", o=1).to_broadcast([P, 2, nk])
                sc = score[:, u % 2, :, 0:nk]
                ve.scalar_tensor_tensor(sc, b[:, 0:2 * nk].rearrange("p (e k) -> p e k", e=2), HD ** -0.5, seen,
                                        ALU.mult, ALU.add).then_inc(gemm_read, 1)
                ve.wait_ge(gemm_read, n.at("unit"))
                chained(ve.tensor_reduce(stat[:, MX:MX + 2], sc, AX.X, ALU.max))
                ve.scalar_tensor_tensor(stat[:, NM + 2 * u:NM + 2 * u + 2], stat[:, MX:MX + 2], -1.0,
                                        stat[:, NSINK + 2 * p:NSINK + 2 * p + 2], ALU.mult, ALU.min).then_inc(negmax_ready, 1)

            def probs_out(first):
                t = first // 4
                ve.wait_ge(negmax_ready, first + 4)
                ve.tensor_tensor(stat[:, ES + 8 * t:ES + 8 * t + 8], row("sinks", HEADS), stat[:, NM + 8 * t:NM + 8 * t + 8],
                                 ALU.add).then_inc(sink_in, 1)
                for u in range(first, first + 4):
                    ve.wait_ge(tr_done, n.step("tr"))
                    if u >= 2:
                        ve.wait_ge(pv_done, u - 1)
                    m = 2 * (t + 1)
                    ve.tensor_copy(pT[:, u % 2, 0:m, :], turned[(n.n["tr"] - 1) % 2][:, 0:m * P].rearrange("p (a b) -> p a b", a=m)
                                   ).then_inc(tr_read, 1)
                ve.wait_ge(sink_exp, t + 1)
                ve.wait_ge(probs_ready, first + 4)
                den = stat[:, RD + 8 * t:RD + 8 * t + 8]
                chained(ve.tensor_tensor(den, stat[:, LS + 8 * t:LS + 8 * t + 8], stat[:, ES + 8 * t:ES + 8 * t + 8], ALU.add))
                chained(ve.reciprocal(den, den))
                ve.wait_ge(pv_done, first + 4)
                n.step("small")
                ve.tensor_tensor(proj[:, t, 0:POOL].rearrange("p (h d) -> p h d", d=HD), small[:, :].rearrange("p (h d) -> p h d", d=HD),
                                 den.rearrange("p (h o) -> p h o", o=1).to_broadcast([P, HEADS, HD]), ALU.mult).then_inc(small_read, 1)

            maxima(0)
            maxima(1)
            for pair in range(2):
                b = unit()
                g = slice(2 * pair, 2 * pair + 2)
                ve.tensor_tensor(diff[:, g, :], b[:, :].rearrange("p (g t) -> p g t", g=2),
                                 gain_cols("pool_scale", 2 * pair, 2).to_broadcast([P, 2, SEQ]), ALU.mult).then_inc(gemm_read, 1)
            maxima(2)
            maxima(3)
            for pair in range(2):
                g = slice(2 * pair, 2 * pair + 2)
                ve.wait_ge(pool_hi, pair + 1)
                ve.tensor_tensor(ypool_lo[:, g, :], diff[:, g, :], ypool_hi[:, g, :].bitcast(f32), ALU.subtract).then_inc(pool_lo, 1)
            gates_bias(2)
            probs_out(0)
            for u in range(4, 8):
                maxima(u)
            gates_bias(3)
            probs_out(4)

            def branch(g0, first):
                split()
                for cb in range(2):
                    for t in range(NT):
                        b = unit()
                        g = proj[:, t, g0 + cb * COLS:g0 + (cb + 1) * COLS]
                        ve.wait_ge(gates_ready, 2 * (first + cb) + t + 1)
                        ve.tensor_tensor(g, g, b[:, :], ALU.mult).then_inc(gemm_read, 1)
                        if first:
                            ve.wait_ge(gemm_read, n.at("unit"))
                            m = proj[:, t, G0 + cb * COLS:G0 + (cb + 1) * COLS]
                            ve.tensor_tensor(m, m, g, ALU.add).then_inc(merged_ready, 1)

            branch(G0, 0)
            for t in range(NT):
                plain_rows(yattn_hi[:, 0:4, t * P:(t + 1) * P], yattn_lo[:, 0:4, t * P:(t + 1) * P])
            branch(G0 + D, 2)
            for half in range(2):
                for t in range(NT):
                    plain_rows(act_dst(act_hi, 0, half, t), act_dst(act_lo, 0, half, t))
            for cb in range(2):
                split()
                for t in range(NT):
                    b = unit()
                    ve.tensor_copy(proj[:, t, cb * COLS:(cb + 1) * COLS], b[:, :]).then_inc(gemm_read, 1)
            recips([0, 1])
            ve.wait_ge(post1_loaded, 16)
            ve.wait_ge(rstd_ready, n.at("rstd"))
            post_norm(lambda t: proj[:, t, 0:D], g_post1)
            n.step("x", 2)
            ve.wait_ge(x_ready, n.at("x"))
            recips([0, 1])
            scaled_rows(gained("g_mlp", 0) + gained("g_mlp", 1))
            recips([0, 1])
            ve.memset(mlp[:, :, :], 0.0).then_inc(dve_chain, 1)
            ve.wait_ge(dve_chain, n.step("chain"))

            def rectify(k):
                split()
                for t in range(NT):
                    b = unit()
                    ve.tensor_scalar(h1[:, k, t, :], b[:, :], 0.0, None, ALU.max).then_inc(gemm_read, 1)

            def down_rows(cb):
                split()
                for t in range(NT):
                    b = unit()
                    dst = mlp[:, t, cb * COLS:(cb + 1) * COLS]
                    ve.tensor_tensor(dst, b[:, :], dst, ALU.add).then_inc(gemm_read, 1)

            with n.loop(ve, 4, split=6, unit=8, tr=4, tr_hi=4, small=2, mod_small=2) as i:
                for k in range(2):
                    rectify(k)
                    if k:
                        mod_read(4, i, 2)
                    split()
                    for t in range(NT):
                        plain_rows(h1_hi[:, 4 * k:4 * k + 4, t * P:(t + 1) * P], h1_lo[:, 4 * k:4 * k + 4, t * P:(t + 1) * P])
                down_rows(0)
                mod_read(5, i, 2)
                down_rows(1)
            recips([0, 1])
            ve.wait_ge(post2_loaded, 16)
            ve.wait_ge(rstd_ready, n.at("rstd"))
            post_norm(lambda t: mlp[:, t, :], g_post2)
            n.step("x", 2)
            ve.wait_ge(small_read, n.at("small"))
            coefs(0, "norm_mix", 0, 8)
            for half in range(2):
                split()
                scaled_rows(modulated(0, 0, 1, half))
                gate_read(half, (0, 1))
            recips([0, 1])
            scaled_rows(modulated(0, 0, 0, 0) + modulated(0, 0, 0, 1))
            ve.wait_ge(tr_done, n.at("tr"))
            ve.memset(z_pad[:, :, 0:1], 0.0)
            chained(ve.memset(z_pad[:, :, SEQ + 1:SEQ + 2], 0.0))
            rotation(3)

            def tap(name, i, f):
                return cols[:, bass.ds(i * 2 + COL[name] + f, 1)]

            with n.loop(ve, 4, split=2, unit=6, h=2, chain=6) as i:
                for f in range(2):
                    split()
                    b = unit()
                    ve.tensor_copy(c_sb[:, :, :].rearrange("p s t -> p (s t)"), b[:, :]).then_inc(gemm_read, 1)
                    ve.wait_ge(gemm_read, n.at("unit"))
                    b = unit()
                    ve.tensor_tensor(z_pad[:, :, 1:SEQ + 1], c_sb[:, :, :], b[:, :].rearrange("p (s t) -> p s t", s=2),
                                     ALU.mult).then_inc(gemm_read, 1)
                    ve.wait_ge(gemm_read, n.at("unit"))
                    chained(ve.tensor_scalar(conv_y[:, :, :], z_pad[:, :, 1:SEQ + 1], tap("conv_k1", i, f), tap("conv_b", i, f),
                                             ALU.mult, ALU.add))
                    chained(ve.scalar_tensor_tensor(conv_y[:, :, :], z_pad[:, :, 0:SEQ], tap("conv_k0", i, f), conv_y[:, :, :],
                                                    ALU.mult, ALU.add))
                    chained(ve.scalar_tensor_tensor(conv_y[:, :, :], z_pad[:, :, 2:SEQ + 2], tap("conv_k2", i, f), conv_y[:, :, :],
                                                    ALU.mult, ALU.add))
                    b = unit()
                    ve.tensor_tensor(conv_m[:, f, :, :], conv_y[:, :, :], b[:, :].rearrange("p (s t) -> p s t", s=2),
                                     ALU.mult).then_inc(gemm_read, 1)
                    ve.wait_ge(h_hi, n.step("h"))
                    ve.tensor_tensor(conv_lo[:, bass.ds(i * 2 + f, 1), :, :].rearrange("p o s t -> p (o s) t"), conv_m[:, f, :, :],
                                     conv_hi[:, bass.ds(i * 2 + f, 1), :, :].rearrange("p o s t -> p (o s) t").bitcast(f32),
                                     ALU.subtract).then_inc(h_lo, 1)
            rotation(4)

            def add_gated(tt, cb, g, last):
                b = unit()
                k = n.n["unit"] % 2
                r = res(tt)[:, cb * COLS:(cb + 1) * COLS]
                ve.tensor_tensor(gated[:, k, :], b[:, :], gate[:, g, cb * COLS:(cb + 1) * COLS], ALU.mult).then_inc(gemm_read, 1)
                ve.wait_ge(gemm_read, n.at("unit"))
                ins = ve.tensor_tensor(r, r, gated[:, k, :], ALU.add)
                if last:
                    ins.then_inc(x_ready, 1)
                else:
                    ins.then_inc(dve_chain, 1)
                    n.step("chain")

            for cb in range(2):
                split()
                for tt in range(2 * NT):
                    add_gated(tt, cb, tt // NT, cb == 1)
            n.step("x", 4)

            def norm_both(c, layer, gain, shift_at, slots):
                coefs(c, gain, layer, shift_at + 8)
                recips(range(4))
                for q in range(2):
                    split()
                    scaled_rows(modulated(c, shift_at, q, 0) + modulated(c, shift_at, q, 1))
                    gate_read(q, slots)

            norm_both(1, 0, "norm_ffn", 16, (0, 1))

            def hidden_chunk():
                split()
                for f in range(2):
                    n.step("unit")
                    b = unit()
                    ve.wait_ge(silu_ready, n.step("silu"))
                    ve.tensor_tensor(h2[:, f, :], silu[:, f, :], b[:, :], ALU.mult).then_inc(gemm_read, 2)
                    ve.wait_ge(h_hi, 8 + n.step("hidden"))
                    k = (n.n["hidden"] - 1) % 4
                    ve.tensor_tensor(h2_lo[:, k, :, :], h2[:, f, :].rearrange("p (s t) -> p s t", s=2), h2_hi[:, k, :, :].bitcast(f32),
                                     ALU.subtract).then_inc(h_lo, 1)

            def down_gated(final=False):
                split()
                for cb in range(2):
                    for tt in range(2 * NT):
                        add_gated(tt, cb, tt // NT, final and cb == 1)

            with n.loop(ve, 4, split=4, unit=16, small=1, mod_small=1, silu=4, hidden=4, chain=8) as i:
                hidden_chunk()
                hidden_chunk()
                split()
                down_gated()
                mod_read(12, i, 1)
            hidden_chunk()
            hidden_chunk()
            down_gated()
            hidden_chunk()
            down_gated(final=True)
            n.step("x", 4)
            ve.wait_ge(small_read, n.at("small"))
            norm_both(2, 1, "norm_mix", 32, (0,))
            split()
            for t in range(NT):
                b = unit()
                ve.tensor_copy(q_nat[:, t, 0:COLS], b[:, :]).then_inc(gemm_read, 1)
            split()
            for tt in range(2 * NT):
                b = unit()
                if tt < NT:
                    ve.tensor_copy(q_nat[:, tt, COLS:QL], b[:, 0:256])
                ve.tensor_copy(kv_nat[:, tt, :], b[:, 256:COLS]).then_inc(gemm_read, 1)
            ve.wait_ge(wpe_hi, 1)
            ve.tensor_tensor(w_pe_lo[:, :, :], w_pe[:, :, :], w_pe_hi[:, :, :].bitcast(f32), ALU.subtract).then_inc(wpe_lo, 1)
            recips([0, 1] + list(range(4, 8)))
            b = unit()
            ve.tensor_copy(pe[:, :, :].rearrange("p t d -> p (t d)"), b[:, 0:2 * NT * ROPE]).then_inc(gemm_read, 1)
            ve.wait_ge(gemm_read, n.at("unit"))
            chained(ve.tensor_tensor(pe_t[:, :, :], pe[:, :, :], pe[:, :, :], ALU.mult))
            ve.tensor_reduce(stat[:, SS + 8:SS + 12], pe_t[:, :, :], AX.X, ALU.add).then_inc(pe_sum, 1)
            ve.wait_ge(pe_root, 1)
            chained(ve.reciprocal(stat[:, RS + 8:RS + 12], stat[:, RT + 8:RT + 12]))
            chained(ve.tensor_tensor(pe[:, :, :], pe[:, :, :],
                                     stat[:, RS + 8:RS + 12].rearrange("p (t o) -> p t o", o=1).to_broadcast([P, 2 * NT, ROPE]), ALU.mult))
            chained(ve.tensor_tensor(pe[:, :, :], pe[:, :, :],
                                     row("kn_rope", ROPE).rearrange("p (o d) -> p o d", o=1).to_broadcast([P, 2 * NT, ROPE]), ALU.mult))

            def halves(ap, k):
                return ap.rearrange("p h (a k d) -> p h a k d", a=2, k=2)[:, :, :, k, :]

            def rotate(src, tmp, t, heads):
                def tabs(name):
                    return table(name, ROPE, j=ROPE * t).rearrange("p (o d) -> p o d", o=1)

                for k in range(2):
                    s = halves(tabs("sinm"), k).to_broadcast([P, heads, 2, 8])
                    last = ve.tensor_tensor(halves(tmp, k), halves(src, 1 - k), s, ALU.mult)
                chained(last)
                chained(ve.tensor_tensor(src, src, tabs("cosm").to_broadcast([P, heads, ROPE]), ALU.mult))
                return ve.tensor_tensor(src, src, tmp, ALU.add)

            for t in range(NT):
                chained(rotate(pe[:, t:t + 1, :], pe_t[:, t:t + 1, :], t, 1))
            split()
            scaled_rows([item for t in range(NT) for item in (
                (gain_cols("q_norm", 0, 4), None, ql_hi[:, 0:4, t * P:(t + 1) * P], ql_lo[:, 0:4, t * P:(t + 1) * P]),
                (gain_cols("q_norm", 4, 2), None, ql_hi[:, 4:6, t * P:(t + 1) * P], ql_lo[:, 4:6, t * P:(t + 1) * P]))])
            gate_read(0, (1,))
            split()
            scaled_rows([(gain_cols("kv_norm", 0, 2), None, kvl_hi[:, 0:2, q * SEQ:(q + 1) * SEQ], kvl_lo[:, 0:2, q * SEQ:(q + 1) * SEQ])
                         for q in range(2)])
            gate_read(1, (1,))
            for tt in range(2 * NT):
                last = ve.tensor_copy(kg[:, tt, :, NOPE:QK], pe[:, tt:tt + 1, :].to_broadcast([P, GH, ROPE]))
            chained(last)

            def heads_group(i, g):
                split()
                n.step("unit", 6)
                KH = 2 * NT * GH
                ve.wait_ge(sq_ready, n.step("sq"))
                ve.tensor_reduce(stat[:, GQ:GQ + KH], sq[:, :].rearrange("p (a d) -> p a d", d=NOPE), AX.X, ALU.add).then_inc(gsum_ready, 1)
                ve.wait_ge(groot_ready, n.step("groot"))
                chained(ve.reciprocal(stat[:, GQ + 32:GQ + 32 + KH], stat[:, GQ + 16:GQ + 16 + KH]))
                kn = kg[:, :, :, 0:NOPE].rearrange("p t h d -> p (t h) d")
                ve.tensor_tensor(kn, kn, stat[:, GQ + 32:GQ + 32 + KH].rearrange("p (a o) -> p a o", o=1).to_broadcast([P, KH, NOPE]),
                                 ALU.mult).then_inc(qk_ready, 1)
                QH = NT * GH
                qf = qg[:, :, :, :].rearrange("p t h d -> p (t h) d")
                sf = sq[:, 0:QH * QK].rearrange("p (a d) -> p a d", d=QK)
                ve.wait_ge(sq_ready, n.step("sq"))
                ve.tensor_reduce(stat[:, GQ:GQ + QH], sf[:, :, 0:NOPE], AX.X, ALU.add)
                ve.tensor_reduce(stat[:, GQ + QH:GQ + 2 * QH], sf[:, :, NOPE:QK], AX.X, ALU.add).then_inc(gsum_ready, 1)
                ve.wait_ge(groot_ready, n.step("groot"))
                chained(ve.reciprocal(stat[:, GQ + 32:GQ + 32 + 2 * QH], stat[:, GQ + 16:GQ + 16 + 2 * QH]))
                for first, c0, c1 in ((0, 0, NOPE), (QH, NOPE, QK)):
                    r = stat[:, GQ + 32 + first:GQ + 32 + first + QH].rearrange("p (a o) -> p a o", o=1)
                    last = ve.tensor_tensor(qf[:, :, c0:c1], qf[:, :, c0:c1], r.to_broadcast([P, QH, c1 - c0]), ALU.mult)
                chained(last)
                ve.tensor_tensor(qf[:, :, 0:NOPE], qf[:, :, 0:NOPE],
                                 row("kn_nope", NOPE).rearrange("p (o d) -> p o d", o=1).to_broadcast([P, QH, NOPE]), ALU.mult)
                chained(ve.tensor_tensor(qf[:, :, NOPE:QK], qf[:, :, NOPE:QK],
                                         row("qn_rope", ROPE).rearrange("p (o d) -> p o d", o=1).to_broadcast([P, QH, ROPE]), ALU.mult))
                for t in range(NT):
                    last = rotate(qg[:, t, :, NOPE:QK], qr_t[:, t, :, :], t, GH)
                last.then_inc(qk_ready, 1)
                n.step("tr", 6)

                def mla_max(u):
                    ve.wait_ge(scores_done, n.step("scores"))
                    chained(ve.tensor_reduce(stat[:, MX + u:MX + u + 1], bank[u % 4][:, :], AX.X, ALU.max))
                    ve.tensor_scalar(stat[:, NM + u:NM + u + 1], stat[:, MX + u:MX + u + 1], -QK ** -0.5, None, ALU.mult).then_inc(negmax_ready, 1)

                for u in range(2):
                    mla_max(u)
                for u in range(8):
                    if u + 2 < 8:
                        mla_max(u + 2)
                    ve.wait_ge(tr_done, n.step("tr"))
                    n.step("pv")
                    if u >= 2:
                        ve.wait_ge(pv_done, 8 + n.at("pv", 2))
                    ve.tensor_copy(prT[:, u % 2, :, :], turned[(n.n["tr"] - 1) % 2][:, :].rearrange("p (a b) -> p a b", a=4)).then_inc(tr_read, 1)
                rd = stat[:, RD:RD + 8]
                ve.wait_ge(probs_ready, 8 + n.step("probs", 8))
                chained(ve.reciprocal(rd, stat[:, LS:LS + 8]))
                ve.wait_ge(pv_done, 8 + n.at("pv"))
                n.step("small")
                for t in range(NT):
                    dst = o_nat[:, t, bass.ds(i * (2 * GH * VD) + g * GH * VD, GH * VD)].rearrange("p (h d) -> p h d", d=VD)
                    last = ve.tensor_tensor(dst, small[:, t * GH * VD:(t + 1) * GH * VD].rearrange("p (h d) -> p h d", d=VD),
                                            rd[:, t * GH:(t + 1) * GH].rearrange("p (h o) -> p h o", o=1).to_broadcast([P, GH, VD]), ALU.mult)
                last.then_inc(small_read, 1)

            with n.loop(ve, 2, split=2, unit=12, tr=28, scores=16, small=2, sq=4, groot=4, probs=16, pv=16, chain=2 * 17) as i:
                heads_group(i, 0)
                heads_group(i, 1)
            for half in range(2):
                for t in range(NT):
                    plain_rows(act_dst(act_hi, 0, half, t), act_dst(act_lo, 0, half, t))
            rotation(4)
            for cb in range(2):
                split()
                for t in range(NT):
                    add_gated(t, cb, 0, cb == 1)
            n.step("x", 2)
            coefs(3, "norm_ffn", 1, 56)
            recips([0, 1])
            scaled_rows(modulated(3, 48, 0, 0) + modulated(3, 48, 0, 1))

            def hidden_rows(k):
                split()
                for t in range(NT):
                    b = unit()
                    ve.wait_ge(silu_ready, n.step("silu"))
                    ve.tensor_tensor(h3[:, k, t, :], silu3[:, t, :], b[:, 256:COLS], ALU.mult).then_inc(gemm_read, 1)

            def turn_hidden1(p, k):
                for t in range(NT):
                    where = (slice(None), p, slice(2 * k, 2 * k + 2), slice(t * P, (t + 1) * P))
                    plain_rows(h3_hi[where], h3_lo[where])

            def down1(final=False):
                split()
                for cb in range(2):
                    for t in range(NT):
                        add_gated(t, cb, 1, final and cb == 1)

            def group1(p):
                hidden_rows(0)
                turn_hidden1(1 - p, 1)
                hidden_rows(1)
                turn_hidden1(p, 0)
                down1()

            hidden_rows(0)
            hidden_rows(1)
            turn_hidden1(0, 0)
            with n.loop(ve, 2, split=6, unit=16, tr=8, tr_hi=8, silu=8, chain=8):
                group1(1)
                group1(0)
            hidden_rows(0)
            turn_hidden1(0, 1)
            down1()
            turn_hidden1(1, 0)
            down1(final=True)


def _rows_first(w, kts):
    return w.reshape(kts, P, w.shape[1]).transpose(1, 0, 2).reshape(P, -1)


def _blocks(w):
    return [_rows_first(w[:, c:c + COLS], KT) for c in range(0, w.shape[1], COLS)]


def _down(w):
    kts = w.shape[0] // P
    return w.reshape(kts, P, 2, COLS).transpose(1, 2, 0, 3).reshape(P, -1)


def _tables():
    ident = np.eye(P, dtype=np.float32)
    rel = np.arange(P)[:, None] + P - np.arange(2 * P)[None, :]
    mask = np.where((rel >= 0) & (rel < P), 0.0, -1e30).astype(np.float32)

    def token_rows(t):
        return t.astype(np.float32).reshape(NT, P, -1).transpose(1, 0, 2).reshape(P, -1)

    inv1 = (500000.0 ** (-np.arange(0, ROT, 2, dtype=np.float32).astype(np.float64) / ROT)).astype(np.float32)
    ang1 = (np.arange(SEQ, dtype=np.float32)[:, None] * inv1[None, :]).astype(np.float64)
    inv2 = (10000.0 ** (-np.arange(0, ROPE // 2, 2).astype(np.float64) / (ROPE // 2))).astype(np.float32)
    grid = 64
    r = (np.arange(SEQ) // grid).astype(np.float32)[:, None] * inv2
    c = (np.arange(SEQ) % grid).astype(np.float32)[:, None] * inv2
    ang2 = np.concatenate([r, r, c, c], axis=1).astype(np.float64)
    sign = np.tile(np.repeat([-1.0, 1.0], 8), 2)
    sel_col = np.zeros((P, 2), np.float32)
    sel_col[0:2, 0] = sel_col[2:4, 1] = 1.0
    sel_row = np.zeros((P, 2, P), np.float32)
    sel_row[0:2, 0] = sel_row[2:4, 1] = sel_row[4] = 1.0
    return mask, np.concatenate([ident, token_rows(np.cos(ang1)), token_rows(np.sin(ang1)), token_rows(np.cos(ang2)),
                           token_rows(np.sin(ang2) * sign), sel_col, sel_row.reshape(P, 2 * P)], axis=1)


def _pool_matrices():
    s, t = np.arange(SEQ)[:, None], np.arange(SEQ)[None, :]
    out = np.zeros((P, len(POOL_WINDOWS), 3, P), np.float32)
    for g, w in enumerate(POOL_WINDOWS):
        m = ((s <= t) & (t - s < w)) / np.minimum(t + 1, w) - (s == t)
        for j, (a, b) in enumerate(((0, 0), (0, 1), (1, 1))):
            out[:, g, j] = m[a * P:(a + 1) * P, b * P:(b + 1) * P]
    return out


def kernel(**inputs):
    import concourse.bacc as bacc
    from concourse.bass_utils import run_bass_kernel_spmd

    v = {name: np.asarray(value) for name, value in inputs.items()}

    def columns(vec):
        return vec.reshape(-1, P).T

    mod_w, mod_b = v["mod_w_2"], v["mod_b_2"]
    kinds = (0, 1, 3, 4)
    mod_cols = [_rows_first(mod_w[l][:, k * D + h * COLS:k * D + (h + 1) * COLS], KT) for l in range(2) for k in kinds for h in range(2)]
    gates = [(l, k) for l in range(2) for k in (2, 5)]
    mod_gates = [[_rows_first(mod_w[l][:, k * D + h * COLS:k * D + (h + 1) * COLS], KT) for h in range(2)] for l, k in gates]
    w_in = v["w_in"][0]
    mlp = []
    up, down = _blocks(v["w_up"][0]), v["w_down"][0]
    for i in range(4):
        d = down[i * D:(i + 1) * D]
        mlp += [up[2 * i], mod_cols[4 + 2 * i], up[2 * i + 1], mod_cols[5 + 2 * i], _rows_first(d[:, 0:COLS], KT), _rows_first(d[:, COLS:D], KT)]
    conv = v["conv_w_in_2"][0].reshape(D, 3, KT, P)
    ffn = []
    for l in range(2):
        wg, wu, wd = v["ffn_w_gate_2"][l], v["ffn_w_up_2"][l], v["ffn_w_down_2"][l]
        gu = [_rows_first(np.concatenate([wg[:, j:j + 256], wu[:, j:j + 256]], axis=1), KT) for j in range(0, FH, 256)]
        dn = [_down(wd[i * COLS:(i + 1) * COLS]) for i in range(6)]
        seq = []
        for i in range(5):
            if l == 0:
                seq += [gu[2 * i], gu[2 * i + 1]] + ([mod_cols[12 + i]] if i < 4 else []) + [dn[i]]
            else:
                seq += [gu[2 * i], gu[2 * i + 1]] + ([dn[i - 1]] if i else [])
        ffn.append((seq + [gu[10]] + ([dn[4]] if l else []), [dn[5]]))
    mla_in = v["mla_w_in_2"][0]
    q_up, kv_up = v["mla_w_q_up_2"][0], v["mla_w_kv_up_2"][0]
    mla_up = [np.concatenate([_rows_first(q_up[:, g * GH * QK:(g + 1) * GH * QK], QKT), _rows_first(kv_up[:, g * COLS:(g + 1) * COLS], KVT)], axis=1)
              for g in range(MH // GH)]
    stream = {
        "mod_head": mod_cols[0:3], "w_in": _blocks(w_in[:, 0:K0]), "mod_last": mod_cols[3:4], "w_kv": [_rows_first(w_in[:, K0:G0], KT)],
        "w_gates": _blocks(w_in[:, G0:]), "w_branch": [_down(v["w_branch_pool"][0]), _down(v["w_branch_attn"][0])],
        "w_out": _blocks(v["w_out"][0]), "mlp": mlp, "mod_gate0": mod_gates[0],
        "conv_in": [_rows_first(conv[:, :, f, :].reshape(D, 3 * P), KT) for f in range(KT)], "conv_out": _blocks(v["conv_w_out_2"][0]),
        "mod_gate1": mod_gates[1], "ffn0": ffn[0][0], "ffn0_half": ffn[0][1], "mod_gate2": mod_gates[2],
        "mla_in": _blocks(mla_in[:, 0:QL + KVL]), "mod_gate3": mod_gates[3], "mla_up": mla_up, "mla_out": _blocks(v["mla_w_out_2"][0]),
        "ffn1": ffn[1][0], "ffn1_half": ffn[1][1],
    }
    arrays = {}
    for name, n, width in SECTIONS:
        arrays[name] = np.stack(stream[name])
        assert arrays[name].shape == (n, P, width), (name, arrays[name].shape)
    arrays["x"] = v["x"][0]
    arrays["ctx"] = v["ctx_2"][0]
    arrays["cols"] = np.concatenate(
        [columns(v[k]) for k in ("g_mix_pre", "g_mlp_pre", "pool_scale", "norm_mix_g_2", "norm_ffn_g_2", "mla_q_norm_g_2", "mla_kv_norm_g_2")]
        + [columns(v["conv_k_2"][0, j]) for j in range(3)] + [columns(v["conv_b_2"])]
        + [np.stack([columns(v["c_2"]), columns(v["c_ctx_2"])], axis=2).reshape(P, 2 * KT)]
        + [columns(mod_b[l, k * D:(k + 1) * D]) for l in range(2) for k in kinds], axis=1)
    arrays["rows"] = np.concatenate([v[k].reshape(-1) for k in (
        "attn_sinks", "mla_qn_nope_g_2", "mla_qn_rope_g_2", "mla_kn_nope_g_2", "mla_kn_rope_g_2")])
    arrays["mask"], arrays["tab"] = _tables()
    arrays["pool_m"] = _pool_matrices()
    arrays["w_pool"] = v["w_pool"][0]
    arrays["b_in"] = v["b_in"][0]
    arrays["g_mix_post"] = v["g_mix_post"][0]
    arrays["g_mlp_post"] = v["g_mlp_post"][0]
    arrays["mod_gate_b"] = np.concatenate([mod_b[l, k * D:(k + 1) * D].reshape(2, COLS) for l, k in gates])
    arrays["w_pe"] = mla_in[:, QL + KVL:].reshape(KT, P, ROPE).transpose(1, 0, 2)

    f32 = mybir.dt.float32
    nc = bacc.Bacc("TRN2", target_bir_lowering=False, num_devices=1)
    feeds, args = {}, {}
    for name, value in arrays.items():
        feeds["in_" + name] = np.ascontiguousarray(value)
        args[name] = nc.dram_tensor("in_" + name, value.shape, f32, kind="ExternalInput").ap()
    out = nc.dram_tensor("out_x", (SEQ, D), f32, kind="ExternalOutput").ap()
    build(nc, args, out)
    result = run_bass_kernel_spmd(nc, [feeds], core_ids=[0])
    return result.results[0]["out_x"].reshape(1, SEQ, D)
```

```python
import contextlib
from collections import Counter

import concourse.bass as bass
import numpy as np
from concourse import mybir

P = 128
D = 1024
KT = D // P
SEQ = 256
NT = SEQ // P
CHUNK = 4096
COLS = 512
EPS = 1e-6

POOL_WINDOWS = (2, 4, 8, 16)
POOL = 512
HEADS = 8
HD = 64
KVH = 2
IN_W = 3328
Q0, K0, V0, G0 = POOL, POOL + HEADS * HD, POOL + HEADS * HD + KVH * HD, POOL + HEADS * HD + 2 * KVH * HD
ROT = 16
FF = 4096

FH = 2816
MH = 16
GH = 4
NOPE, ROPE, VD = 64, 32, 64
QK = NOPE + ROPE
QL, KVL = 768, 256
QKT, KVT = QL // P, KVL // P
KEYS = 2 * SEQ

SECTIONS = (
    ("w_in", 2, 4096), ("w_kv", 1, 2048), ("w_gates", 4, 4096), ("w_branch", 4, 4096), ("w_out", 2, 4096), ("mod_scale", 2, 4096),
    ("mlp", 24, 4096), ("mod_gate0", 2, 4096), ("conv_in", 8, 3072), ("conv_out", 2, 4096),
    ("mod_gate1", 2, 4096), ("ffn0", 20, 4096), ("ffn0_half", 1, 2048),
    ("mod_gate2", 2, 4096), ("mla_in", 2, 4096), ("mod_gate3", 2, 4096), ("mla_up", 4, 3328), ("mla_out", 2, 4096),
    ("ffn1", 16, 4096), ("ffn1_half", 1, 2048),
)
STREAM = sum(n for _, n, _ in SECTIONS)
X_UPDATES = 16

COL_NAMES = (("g_mix", KT), ("g_mlp", KT), ("pool_scale", 4), ("norm_mix", 2 * KT), ("norm_ffn", 2 * KT),
             ("q_norm", QKT), ("kv_norm", KVT), ("conv_k0", KT), ("conv_k1", KT), ("conv_k2", KT), ("conv_b", KT),
             ("cond", 2 * KT), ("mod_b", 64))
COL, _at = {}, 0
for _name, _n in COL_NAMES:
    COL[_name] = _at
    _at += _n
NCOL = _at

ROW_NAMES = (("sinks", HEADS), ("qn_nope", NOPE), ("qn_rope", ROPE), ("kn_nope", NOPE), ("kn_rope", ROPE))
ROW, _at = {}, 0
for _name, _n in ROW_NAMES:
    ROW[_name] = _at
    _at += _n
NROW = _at

TAB_NAMES = (("ident", P), ("cos1", NT * 8), ("sin1", NT * 8), ("cosm", NT * ROPE), ("sinm", NT * ROPE),
             ("sel_col", 2), ("sel_row", 2 * P))
TAB, _at = {}, 0
for _name, _n in TAB_NAMES:
    TAB[_name] = _at
    _at += _n
NTAB = _at


class Count:

    def __init__(self):
        self.n, self.turn, self.per = Counter(), None, {}

    def at(self, name, back=0):
        value = self.n[name] - back
        assert value >= 0, name
        if self.turn is not None and self.per.get(name):
            assert value > 0, name
            return self.turn * self.per[name] + value
        return value

    def step(self, name, k=1):
        self.n[name] += k
        return self.at(name)

    @contextlib.contextmanager
    def loop(self, eng, turns, **per):
        start = Counter(self.n)
        with eng.Fori(0, turns) as i:
            self.turn, self.per = i, per
            yield i
        for name in set(self.n) | set(per):
            assert self.n[name] - start[name] == per.get(name, 0), (name, self.n[name] - start[name], per)
            self.n[name] = start[name] + turns * per.get(name, 0)
        self.turn, self.per = None, {}


def build(nc, a, out):
    f32, f32r = mybir.dt.float32, mybir.dt.float32r
    ACT, ALU, AX = mybir.ActivationFunctionType, mybir.AluOpType, mybir.AxisListType

    base = -(-nc.sbuf_base // 64) * 64

    def at(name, shape, offset, dtype=f32):
        return nc.alloc_sbuf_tensor_at(name, shape, dtype, offset=base + offset)

    K = 1024
    raw = at("raw", [P, 2, CHUNK], 0)
    w_hi = at("w_hi", [P, 2, CHUNK], 32 * K, f32r)
    w_lo = at("w_lo", [P, 2, CHUNK], 64 * K, f32r)
    x = at("x", [P, NT, D], 96 * K)
    ACT0 = 104 * K
    act_hi = at("act_hi", [P, 2, KT, SEQ], ACT0, f32r)
    act_lo = at("act_lo", [P, 2, KT, SEQ], ACT0 + 16 * K, f32r)
    XN0 = 136 * K
    xn = at("xn", [P, 2, D], XN0)
    scaled = at("scaled", [P, 2, COLS], XN0 + 8 * K)
    junk = at("junk", [P, D], ACT0 + 8 * K)
    M0 = XN0 + 12 * K
    cols = at("cols", [P, NCOL], M0)
    ROWS0 = M0 + -(-4 * NCOL // 32) * 32
    rows = at("rows", [P, NROW], ROWS0)
    TAB0 = ROWS0 + -(-4 * NROW // 32) * 32
    tab = at("tab", [P, NTAB], TAB0)
    M1 = TAB0 + -(-4 * NTAB // 32) * 32
    cond_w = at("cond_w", [P, KT, P], M1, f32r)
    cond_s = at("cond_s", [P, 2 * KT], M1 + 4 * K)
    mod_row = at("mod_row", [5, COLS], M1 + 4 * K + 64)
    mod_col = at("mod_col", [P, 64, 2], M1 + 6 * K + 64)
    stat = at("stat", [P, 160], M1 + 6 * K + 64 + 512)
    coef = at("coef", [P, 4, KT, 2], M1 + 6 * K + 64 + 512 + 640)
    PH = M1 + 6 * K + 64 + 512 + 640 + 256
    END = nc.sbuf_usable_end - base
    assert PH + 48 * K <= END, (PH, END)

    proj = at("proj", [P, NT, IN_W], PH)
    w_pool = at("w_pool", [P, 4, P], PH + 26 * K)
    diff = at("diff", [P, 4, SEQ], PH + 28 * K)
    qT = at("qT", [HD, HEADS, SEQ], PH + 32 * K)
    g_post1 = at("g_post1", [P, D], PH + 32 * K)
    kT = at("kT", [HD, KVH, SEQ], PH + 40 * K)
    pT = at("pT", [P, 2, 4, P], PH + 42 * K)
    mask = at("mask", [P, 2 * P], PH + 46 * K)
    ypool_hi = at("ypool_hi", [P, 4, SEQ], ACT0 + 8 * K, f32r)
    ypool_lo = at("ypool_lo", [P, 4, SEQ], ACT0 + 12 * K, f32r)
    yattn_hi = at("yattn_hi", [P, 4, SEQ], ACT0 + 24 * K, f32r)
    yattn_lo = at("yattn_lo", [P, 4, SEQ], ACT0 + 28 * K, f32r)
    pool_m = at("pool_m", [P, 4, 3, P], ACT0 + 24 * K)
    score = at("score", [P, 2, 2, 2 * P], XN0)
    prob = at("prob", [P, 4, 2, 2 * P], XN0 + 4 * K)
    rope_t = at("rope_t", [P, 4, NT, 10, 8], XN0)
    ctx = at("ctx", [P, NT, D], PH)
    h1_hi = at("h1_hi", [P, 8, SEQ], PH + 8 * K, f32r)
    h1_lo = at("h1_lo", [P, 8, SEQ], PH + 16 * K, f32r)
    mlp = at("mlp", [P, NT, D], PH + 24 * K)
    h1 = at("h1", [P, 2, NT, COLS], PH + 32 * K)
    g_post2 = at("g_post2", [P, D], PH + 40 * K)
    gate = at("gate", [P, 2, D], PH + 8 * K)
    conv_hi = at("conv_hi", [P, KT, 2, SEQ], PH + 16 * K, f32r)
    conv_lo = at("conv_lo", [P, KT, 2, SEQ], PH + 32 * K, f32r)
    c_sb = at("c_sb", [P, 2, SEQ], XN0)
    z_pad = at("z_pad", [P, 2, SEQ + 2], XN0 + 2 * K)
    conv_y = at("conv_y", [P, 2, SEQ], XN0 + 4 * K + 64)
    conv_m = at("conv_m", [P, 2, 2, SEQ], XN0 + 6 * K + 64)
    h2_hi = at("h2_hi", [P, 4, 2, SEQ], PH + 16 * K, f32r)
    h2_lo = at("h2_lo", [P, 4, 2, SEQ], PH + 24 * K, f32r)
    silu = at("silu", [P, 2, COLS], PH + 32 * K)
    h2 = at("h2", [P, 2, COLS], PH + 36 * K)
    gated = at("gated", [P, 2, COLS], XN0 + 8 * K)
    ql_hi = at("ql_hi", [P, QKT, SEQ], PH + 16 * K, f32r)
    ql_lo = at("ql_lo", [P, QKT, SEQ], PH + 22 * K, f32r)
    kvl_hi = at("kvl_hi", [P, KVT, KEYS], PH + 28 * K, f32r)
    kvl_lo = at("kvl_lo", [P, KVT, KEYS], PH + 32 * K, f32r)
    q_nat = at("q_nat", [P, NT, QL], PH + 36 * K)
    kv_nat = at("kv_nat", [P, 2 * NT, KVL], PH + 42 * K)
    pe = at("pe", [P, 2 * NT, ROPE], PH + 46 * K)
    pe_t = at("pe_t", [P, 2 * NT, ROPE], PH + 46 * K + 512)
    w_pe = at("w_pe", [P, KT, ROPE], PH)
    w_pe_hi = at("w_pe_hi", [P, KT, ROPE], PH + 1 * K, f32r)
    w_pe_lo = at("w_pe_lo", [P, KT, ROPE], PH + 2 * K, f32r)
    o_nat = at("o_nat", [P, NT, D], PH)
    qg = at("qg", [P, NT, GH, QK], PH + 36 * K)
    sq = at("sq", [P, 2 * NT * GH * NOPE], PH + 39 * K)
    qr_t = at("qr_t", [P, NT, GH, ROPE], PH + 43 * K)
    kg = at("kg", [P, 2 * NT, GH, QK], ACT0)
    vg = at("vg", [P, 2 * NT, GH, VD], ACT0 + 6 * K)
    qgT = at("qgT", [QK, GH, SEQ], ACT0 + 10 * K)
    kgT = at("kgT", [QK, GH, KEYS], ACT0 + 14 * K)
    pr = at("pr", [P, 2, KEYS], XN0)
    prT = at("prT", [P, 2, 4, P], XN0 + 4 * K)
    h3_hi = at("h3_hi", [P, 2, 4, SEQ], PH + 16 * K, f32r)
    h3_lo = at("h3_lo", [P, 2, 4, SEQ], PH + 24 * K, f32r)
    silu3 = at("silu3", [P, 2, 256], PH + 32 * K)
    h3 = at("h3", [P, 2, NT, 256], PH + 34 * K)

    def res(tt):
        return x[:, tt, :] if tt < NT else ctx[:, tt - NT, :]

    def col(name, j, n=1):
        return cols[:, COL[name] + j:COL[name] + j + n]

    def row(name, n):
        return rows[:, ROW[name]:ROW[name] + n]

    def table(name, n, parts=P, j=0):
        return tab[0:parts, TAB[name] + j:TAB[name] + j + n]

    ident = table("ident", P)

    SS, RT, RS = 0, 16, 32
    NM, LS, ES, RD = 48, 64, 80, 96
    MX, NSINK, EPSC = 112, 120, 128
    GQ = 0

    bank = [nc.alloc_psum_tensor(f"bank{i}", [P, COLS], f32) for i in range(4)]
    turned = [nc.alloc_psum_tensor(f"turned{i}", [P, COLS], f32) for i in range(2)]
    mod_ps = nc.alloc_psum_tensor("mod_ps", [P, COLS], f32)
    small = nc.alloc_psum_tensor("small", [P, COLS], f32)

    S = nc.alloc_semaphore
    loaded = [S("loaded0"), S("loaded1")]
    hi_ready = S("hi_ready")
    lo_ready = S("lo_ready")
    lo_ready_pool = S("lo_ready_pool")
    const_loaded = S("const_loaded")
    x_loaded = [S("x_loaded0"), S("x_loaded1")]
    bias_loaded = S("bias_loaded")
    ctx_loaded = S("ctx_loaded")
    post1_loaded = S("post1_loaded")
    post2_loaded = S("post2_loaded")
    pe_loaded = S("pe_loaded")
    modbias_loaded = S("modbias_loaded")
    out_done = S("out_done")
    gemm_done = S("gemm_done")
    gemm_read = S("gemm_read")
    tr_done = S("tr_done")
    tr_read = S("tr_read")
    tr_hi = S("tr_hi")
    mod_done = S("mod_done")
    mod_row_ready = S("mod_row_ready")
    small_done = S("small_done")
    small_read = S("small_read")
    cond_silu = S("cond_silu")
    cond_hi = S("cond_hi")
    cond_zero = S("cond_zero")
    cond_ready = S("cond_ready")
    ss_done = S("ss_done")
    root_ready = S("root_ready")
    rstd_ready = S("rstd_ready")
    xn_ready = S("xn_ready")
    norm_hi = S("norm_hi")
    norm_ready = S("norm_ready")
    x_ready = S("x_ready")
    dve_chain = S("dve_chain")
    gates_ready = S("gates_ready")
    rope_ready = S("rope_ready")
    negmax_ready = S("negmax_ready")
    probs_ready = S("probs_ready")
    scores_done = S("scores_done")
    pv_done = S("pv_done")
    sink_in = S("sink_in")
    sink_exp = S("sink_exp")
    pool_hi = S("pool_hi")
    pool_lo = S("pool_lo")
    merged_ready = S("merged_ready")
    h_ready = S("h_ready")
    silu_ready = S("silu_ready")
    h_hi = S("h_hi")
    h_lo = S("h_lo")
    wpe_hi = S("wpe_hi")
    wpe_lo = S("wpe_lo")
    pe_root = S("pe_root")
    pe_sum = S("pe_sum")
    sq_ready = S("sq_ready")
    gsum_ready = S("gsum_ready")
    groot_ready = S("groot_ready")
    qk_ready = S("qk_ready")

    HALF = CHUNK // 2
    SHARE = 1408

    with nc.Block() as block:

        @block.sync
        def _(sp):
            n = Count()

            def load(section, k, width):
                c = n.step("chunk")
                slot = (n.n["chunk"] - 1) % 2
                if n.n["chunk"] > 2:
                    sp.wait_ge(lo_ready, 2 * n.at("chunk", 2))
                    sp.wait_ge(lo_ready_pool, 2 * n.at("chunk", 2))
                src = a[section][k] if isinstance(k, int) else a[section][bass.ds(k, 1)].rearrange("o p n -> (o p) n")
                sp.dma_start(raw[:, slot, 0:width], src).then_inc(loaded[slot], 16)

            for t in range(NT):
                sp.dma_start(x[:, t, :], a["x"][t * P:(t + 1) * P, :]).then_inc(x_loaded[t], 16)
            sp.dma_start(tab[:, :], a["tab"]).then_inc(const_loaded, 16)
            sp.dma_start(cols[:, :], a["cols"]).then_inc(const_loaded, 16)
            sp.dma_start(rows[:, :], a["rows"].rearrange("(o n) -> o n", o=1).to_broadcast([P, NROW])).then_inc(const_loaded, 16)
            for section, chunks, width in SECTIONS:
                first = 0
                while first < chunks and (chunks < 8 or n.n["chunk"] < 2):
                    load(section, first, width)
                    first += 1
                turns = (chunks - first) // 2
                if turns:
                    with n.loop(sp, turns, chunk=2) as i:
                        load(section, i * 2 + first, width)
                        load(section, i * 2 + first + 1, width)
                if (chunks - first) % 2:
                    load(section, chunks - 1, width)
            for t in range(NT):
                sp.wait_ge(x_ready, X_UPDATES)
                sp.dma_start(out[t * P:(t + 1) * P, :], x[:, t, :]).then_inc(out_done, 16)
            sp.wait_ge(out_done, 16 * NT)

        @block.gpsimd
        def _(pool):
            n = Count()

            def split():
                n.step("chunk")
                s = (n.n["chunk"] - 1) % 2
                for half in range(2):
                    part = slice(half * HALF + SHARE, (half + 1) * HALF)
                    pool.wait_ge(hi_ready, n.step("half"))
                    pool.tensor_tensor(w_lo[:, s, part], raw[:, s, part], w_hi[:, s, part].bitcast(f32),
                                       ALU.subtract).then_inc(lo_ready_pool, 1)

            with n.loop(pool, STREAM // 2, chunk=2, half=4):
                split()
                split()
            if STREAM % 2:
                split()

        @block.tensor
        def _(te):
            n = Count()

            def chunk():
                n.step("chunk")
                split_half(1)
                return (n.n["chunk"] - 1) % 2

            def split_half(back):
                te.wait_ge(lo_ready, 2 * n.at("chunk") - back)
                te.wait_ge(lo_ready_pool, 2 * n.at("chunk") - back)

            def weights(s, j0, j1):
                return w_hi[:, s, j0:j1], w_lo[:, s, j0:j1]

            rot = {"first": 0, "banks": 4}

            def rotation(banks):
                if n.n["unit"]:
                    te.wait_ge(gemm_read, n.at("unit"))
                rot["first"], rot["banks"] = n.n["unit"], banks

            def unit():
                n.step("unit")
                if n.n["unit"] > rot["banks"]:
                    te.wait_ge(gemm_read, n.at("unit", rot["banks"]))
                return bank[(n.n["unit"] - 1 - rot["first"]) % rot["banks"]]

            def product(dst, terms, second=None, also=None, before_last=None):
                for j, ((sh, sl), (mh, ml)) in enumerate(terms):
                    if before_last and j == len(terms) - 1:
                        before_last()
                    if j == second:
                        split_half(0)
                        if also:
                            also()
                    te.matmul(dst, sh, mh, start=(j == 0), stop=False)
                    te.matmul(dst, sh, ml, start=False, stop=False)
                    last = te.matmul(dst, sl, mh, start=False, stop=(j == len(terms) - 1))
                return last

            def act_rows(tt, k):
                t = slice((tt % NT) * P, (tt % NT + 1) * P)
                return act_hi[:, tt // NT, k, t], act_lo[:, tt // NT, k, t]

            def turn(pieces):
                n.step("tr")
                if n.n["tr"] > 2:
                    te.wait_ge(tr_read, n.at("tr", 2))
                dst = turned[(n.n["tr"] - 1) % 2]
                for j, src in enumerate(pieces):
                    m = src.shape[-1]
                    last = te.transpose(dst[0:m, j * P:(j + 1) * P], src, ident)
                last.then_inc(tr_done, 1)

            def turn_rows(buf):
                te.wait_ge(xn_ready, n.step("xn"))
                for half in range(2):
                    turn([xn[:, buf, (4 * half + j) * P:(4 * half + j + 1) * P] for j in range(4)])

            def mod_product():
                s = chunk()
                m = n.step("mod")
                if n.n["mod"] > 1:
                    te.wait_ge(mod_row_ready, n.at("mod", 1))
                for k in range(KT):
                    if k == KT // 2:
                        split_half(0)
                    h, l = weights(s, k * COLS, (k + 1) * COLS)
                    te.matmul(mod_ps[:, :], cond_w[:, k, :], h, start=(k == 0), stop=False)
                    last = te.matmul(mod_ps[:, :], cond_w[:, k, :], l, start=False, stop=(k == KT - 1))
                last.then_inc(mod_done, 1)

            def small_bank():
                n.step("small")
                if n.n["small"] > 1:
                    te.wait_ge(small_read, n.at("small", 1))

            def mod_columns():
                te.wait_ge(mod_row_ready, n.at("mod"))
                small_bank()
                for j in range(4):
                    last = te.matmul(small[:, 2 * j:2 * j + 2], mod_row[0:4, j * P:(j + 1) * P], table("sel_col", 2, 4),
                                     start=True, stop=True)
                last.then_inc(small_done, 1)

            def gate_rows(s, back=0):
                if s == 0:
                    te.wait_ge(mod_row_ready, n.at("mod", back))
                    te.wait_ge(modbias_loaded, 16 * n.step("gate"))
                small_bank()
                te.matmul(small[:, :], table("sel_row", P, 5, s * P), mod_row[0:5, :], start=True, stop=True).then_inc(small_done, 1)

            def mod_gate(seqs):
                for s in range(seqs):
                    gate_rows(s)

            te.wait_ge(const_loaded, 16 * 3)
            turn_rows(0)
            turn_rows(1)
            for k, width in enumerate((COLS, COLS, 256)):
                s = chunk()
                for t in range(NT):
                    if k == 0:
                        te.wait_ge(norm_ready, n.step("norm", 2))
                    b = unit()
                    product(b[:, 0:width], [(act_rows(t, k), weights(s, k * width, (k + 1) * width)) for k in range(KT)],
                            second=0 if width < COLS else 4 if t == 0 else None).then_inc(gemm_done, 1)
            te.wait_ge(gemm_read, n.at("unit"))
            for pair in range(2):
                b = unit()
                for g in (2 * pair, 2 * pair + 1):
                    d0, c0 = (g % 2) * SEQ, g * P
                    te.matmul(b[:, d0:d0 + P], proj[:, 0, c0:c0 + P], pool_m[:, g, 0, :], start=True, stop=True)
                    te.matmul(b[:, d0 + P:d0 + 2 * P], proj[:, 0, c0:c0 + P], pool_m[:, g, 1, :], start=True, stop=False)
                    last = te.matmul(b[:, d0 + P:d0 + 2 * P], proj[:, 1, c0:c0 + P], pool_m[:, g, 2, :], start=False, stop=True)
                last.then_inc(gemm_done, 1)

            def rows_chunk():
                s = chunk()
                for t in range(NT):
                    b = unit()
                    product(b[:, :], [(act_rows(t, k), weights(s, k * COLS, (k + 1) * COLS)) for k in range(KT)],
                            second=4 if t == 0 else None).then_inc(gemm_done, 1)

            rows_chunk()
            te.wait_ge(rope_ready, 1)
            for t in range(NT):
                for half in range(2):
                    turn([proj[:, t, Q0 + h * HD:Q0 + (h + 1) * HD] for h in range(4 * half, 4 * half + 4)])
            turn([proj[:, t, K0 + j * HD:K0 + (j + 1) * HD] for j in range(KVH) for t in range(NT)])
            rows_chunk()

            def scores(u):
                t, p = u // 4, u % 4
                nk = (t + 1) * P
                b = unit()
                for e in range(2):
                    last = te.matmul(b[:, e * nk:(e + 1) * nk], qT[:, 2 * p + e, t * P:(t + 1) * P], kT[:, p // 2, 0:nk],
                                     start=True, stop=True)
                last.then_inc(gemm_done, 1)

            def turn_probs(u):
                te.wait_ge(probs_ready, u + 1)
                turn([prob[:, u % 4, e, j * P:(j + 1) * P] for e in range(2) for j in range(u // 4 + 1)])

            def values(u, tr):
                t, p = u // 4, u % 4
                if p == 0:
                    small_bank()
                te.wait_ge(tr_read, tr)
                for e in range(2):
                    for j in range(t + 1):
                        last = te.matmul(small[:, (2 * p + e) * HD:(2 * p + e + 1) * HD], pT[:, u % 2, e * (t + 1) + j, :],
                                         proj[:, j, V0 + (p // 2) * HD:V0 + (p // 2 + 1) * HD], start=(j == 0), stop=(j == t))
                last.then_inc(pv_done, 1)

            def attend(first):
                trs = []
                for u in range(first, first + 4):
                    turn_probs(u)
                    trs.append(n.n["tr"])
                    if u > first:
                        values(u - 1, trs[-2])
                values(first + 3, trs[-1])

            te.wait_ge(tr_read, n.at("tr"))
            for u in range(2):
                scores(u)
            for pair in range(2):
                b = unit()
                for g in (2 * pair, 2 * pair + 1):
                    last = te.matmul(b[:, (g % 2) * SEQ:(g % 2 + 1) * SEQ], w_pool[:, g, :], diff[:, g, :], start=True, stop=True)
                last.then_inc(gemm_done, 1)
            for u in range(2, 4):
                scores(u)
            rows_chunk()
            attend(0)
            for u in range(4, 8):
                scores(u)
            rows_chunk()
            attend(4)

            def branch(hi, lo):
                s = chunk()
                for cb in range(2):
                    for t in range(NT):
                        b = unit()
                        product(b[:, :], [((hi[:, k, t * P:(t + 1) * P], lo[:, k, t * P:(t + 1) * P]),
                                           weights(s, (4 * cb + k) * COLS, (4 * cb + k + 1) * COLS)) for k in range(4)],
                                second=0 if cb == 1 and t == 0 else None).then_inc(gemm_done, 1)

            te.wait_ge(pool_lo, 2)
            branch(ypool_hi, ypool_lo)
            te.wait_ge(small_read, n.at("small"))
            for t in range(NT):
                turn([proj[:, t, j * P:(j + 1) * P] for j in range(4)])
            te.wait_ge(cond_ready, 1)
            mod_product()
            te.wait_ge(tr_read, n.at("tr"))
            branch(yattn_hi, yattn_lo)
            mod_columns()
            for half in range(2):
                for t in range(NT):
                    te.wait_ge(merged_ready, 2 * half + t + 1)
                    turn([proj[:, t, G0 + (4 * half + j) * P:G0 + (4 * half + j + 1) * P] for j in range(4)])
            mod_product()
            te.wait_ge(tr_read, n.at("tr"))
            rows_chunk()
            mod_columns()
            rows_chunk()
            mod_product()
            turn_rows(0)
            mod_columns()
            mod_product()
            turn_rows(1)

            def up(k, first=False):
                s = chunk()
                for t in range(NT):
                    if first:
                        te.wait_ge(norm_ready, n.step("norm", 2))
                    b = unit()
                    product(b[:, :], [(act_rows(t, j), weights(s, j * COLS, (j + 1) * COLS)) for j in range(KT)],
                            second=4 if t == 0 else None).then_inc(gemm_done, 1)
                    if first and t == 0:
                        mod_columns()

            def turn_hidden(k):
                for t in range(NT):
                    te.wait_ge(h_ready, n.step("hidden"))
                    turn([h1[:, k, t, j * P:(j + 1) * P] for j in range(4)])

            def down():
                s = chunk()
                for t in range(NT):
                    b = unit()
                    product(b[:, :], [((h1_hi[:, j, t * P:(t + 1) * P], h1_lo[:, j, t * P:(t + 1) * P]),
                                       weights(s, j * COLS, (j + 1) * COLS)) for j in range(8)],
                            second=4 if t == 0 else None, also=hidden_split).then_inc(gemm_done, 1)

            def hidden_split():
                te.wait_ge(tr_read, n.at("tr"))

            def mlp_turn(first=False):
                up(0, first)
                mod_product()
                turn_hidden(0)
                up(1)
                mod_columns()
                mod_product()
                turn_hidden(1)
                te.wait_ge(tr_read, n.at("tr", 2))
                down()
                mod_columns()
                if first:
                    turn_rows(0)
                down()
                if first:
                    turn_rows(1)

            mlp_turn(first=True)
            with n.loop(te, 3, chunk=6, unit=8, tr=4, mod=2, small=2, hidden=4):
                mlp_turn()
            mod_product()
            mod_product()

            def moving(k):
                return act_hi[:, :, k, :], act_lo[:, :, k, :]

            def conv_weights(s, part):
                return [weights(s, k * 384 + part * P, k * 384 + (part + 1) * P) for k in range(KT)]

            def conv_in():
                s = chunk()
                for part in (1, 2, 0):
                    b = unit()
                    product(b[:, :].rearrange("p (s t) -> p s t", s=2), [(w, moving(k)) for k, w in enumerate(conv_weights(s, part))],
                            second=5 if part == 1 else None).then_inc(gemm_done, 1)

            rotation(3)
            te.wait_ge(norm_ready, n.step("norm", 4))
            s = chunk()
            for j, part in enumerate((1, 2, 0)):
                b = unit()
                product(b[:, SEQ:2 * SEQ], [(w, (act_hi[:, 1, k, :], act_lo[:, 1, k, :])) for k, w in enumerate(conv_weights(s, part))],
                        second=5 if part == 1 else None)
                if j < 2:
                    turn_rows(j)
                    gate_rows(j, 1)
            te.wait_ge(norm_ready, n.step("norm", 4))
            for j, part in enumerate((1, 2, 0)):
                product(bank[j][:, 0:SEQ], [(w, (act_hi[:, 0, k, :], act_lo[:, 0, k, :])) for k, w in enumerate(conv_weights(s, part))]
                        ).then_inc(gemm_done, 1)
                if j < 2:
                    gate_rows(j)
            conv_in()
            with n.loop(te, 3, chunk=2, unit=6):
                conv_in()
                conv_in()
            rotation(4)

            def features(kts):
                n.step("h", kts)
                te.wait_ge(h_lo, n.at("h", 1))

            def last_feature():
                te.wait_ge(h_lo, n.at("h"))

            def conv_out(s, tt, first):
                b = unit()
                q, t = tt // NT, slice((tt % NT) * P, (tt % NT + 1) * P)
                product(b[:, :], [((conv_hi[:, k, q, t], conv_lo[:, k, q, t]), weights(s, k * COLS, (k + 1) * COLS))
                                  for k in range(KT)], second=4 if tt == 0 else None,
                        before_last=last_feature if first else None).then_inc(gemm_done, 1)

            def norm_both(rows_unit, lag):
                for tt in range(2 * NT):
                    rows_unit(tt)
                    if 0 <= tt - lag < NT and tt < 3:
                        turn_rows(tt - lag)
                mod_product()
                if lag == 2:
                    turn_rows(1)
                mod_product()
                te.wait_ge(norm_ready, n.step("norm", 4))

            features(8)
            s = chunk()
            for tt in range(2 * NT):
                conv_out(s, tt, tt == 0)
            s = chunk()
            norm_both(lambda tt: conv_out(s, tt, False), 1)

            def gate_up(apart=False):
                s = chunk()
                for f in range(2):
                    for part in range(2):
                        b = unit()
                        cols_of = [weights(s, k * COLS + part * 256 + f * P, k * COLS + part * 256 + (f + 1) * P) for k in range(KT)]
                        half = 4 if f == part == 0 else None
                        if apart:
                            product(b[:, 0:SEQ], [(cols_of[k], (act_hi[:, 0, k, :], act_lo[:, 0, k, :])) for k in range(KT)], second=half)
                            if f == 0:
                                turn_rows(part)
                                gate_rows(part, 1)
                            else:
                                gate_rows(part)
                        else:
                            product(b[:, :].rearrange("p (s t) -> p s t", s=2), [(cols_of[k], moving(k)) for k in range(KT)],
                                    second=half).then_inc(gemm_done, 1)
                if apart:
                    te.wait_ge(norm_ready, n.step("norm", 4))
                    for f in range(2):
                        for part in range(2):
                            cols_of = [weights(s, k * COLS + part * 256 + f * P, k * COLS + part * 256 + (f + 1) * P) for k in range(KT)]
                            product(bank[2 * f + part][:, SEQ:2 * SEQ], [(cols_of[k], (act_hi[:, 1, k, :], act_lo[:, 1, k, :])) for k in range(KT)]
                                    ).then_inc(gemm_done, 1)

            def down0(s, kts, cb, tt):
                b = unit()
                q, t = tt // NT, slice((tt % NT) * P, (tt % NT + 1) * P)
                product(b[:, :], [((h2_hi[:, k, q, t], h2_lo[:, k, q, t]),
                                   weights(s, (kts * cb + k) * COLS, (kts * cb + k + 1) * COLS)) for k in range(kts)],
                        second=0 if cb == 1 and tt == 0 else None,
                        before_last=last_feature if cb == tt == 0 else None).then_inc(gemm_done, 1)

            def down0_all():
                features(4)
                s = chunk()
                for cb in range(2):
                    for tt in range(2 * NT):
                        down0(s, 4, cb, tt)

            gate_up(apart=True)
            mod_product()
            gate_up()
            mod_columns()
            down0_all()
            with n.loop(te, 3, chunk=4, unit=16, mod=1, small=1, h=4):
                gate_up()
                mod_product()
                gate_up()
                mod_columns()
                down0_all()
            gate_up()
            gate_up()
            down0_all()
            gate_up()
            features(2)
            s = chunk()

            def down0_rows(tt):
                down0(s, 2, 0, tt)
                down0(s, 2, 1, tt)

            norm_both(down0_rows, 2)
            s = chunk()
            for t in range(NT):
                b = unit()
                product(b[:, :], [(act_rows(t, k), weights(s, k * COLS, (k + 1) * COLS)) for k in range(KT)],
                        second=4 if t == 0 else None).then_inc(gemm_done, 1)
                turn_rows(t)
                if t == 0:
                    gate_rows(0, 1)
            s = chunk()
            for tt in range(2 * NT):
                b = unit()
                if tt == NT:
                    te.wait_ge(norm_ready, n.step("norm", 4))
                first = 0 if tt < NT else 256
                product(b[:, first:COLS], [(act_rows(tt, k), weights(s, k * COLS + first, (k + 1) * COLS)) for k in range(KT)],
                        second=4 if tt == 0 else None).then_inc(gemm_done, 1)
                if tt == 0:
                    gate_rows(0)
            b = unit()
            te.wait_ge(wpe_lo, 1)
            for tt in range(2 * NT):
                last = product(b[:, tt * ROPE:(tt + 1) * ROPE],
                               [(act_rows(tt, k), (w_pe_hi[:, k, :], w_pe_lo[:, k, :])) for k in range(KT)])
            last.then_inc(gemm_done, 1)
            mod_product()
            for t in range(NT):
                te.wait_ge(xn_ready, n.step("xn"))
                turn([xn[:, t, j * P:(j + 1) * P] for j in range(4)])
                turn([xn[:, t, j * P:(j + 1) * P] for j in range(4, QKT)])
            mod_gate(1)
            mod_product()
            for q in range(2):
                te.wait_ge(xn_ready, n.step("xn", 2))
                turn([kv_nat[:, 2 * q + t, k * P:(k + 1) * P] for k in range(KVT) for t in range(NT)])
            mod_gate(1)
            te.wait_ge(norm_ready, n.step("norm", 6))
            def heads_group():
                rotation(4)
                s = chunk()
                for t in range(NT):
                    b = unit()
                    product(b[:, 0:GH * QK], [((ql_hi[:, k, t * P:(t + 1) * P], ql_lo[:, k, t * P:(t + 1) * P]),
                                               weights(s, k * GH * QK, (k + 1) * GH * QK)) for k in range(QKT)],
                            second=5 if t == 0 else None).then_inc(gemm_done, 1)
                for tt in range(2 * NT):
                    b = unit()
                    product(b[:, :], [((kvl_hi[:, k, tt * P:(tt + 1) * P], kvl_lo[:, k, tt * P:(tt + 1) * P]),
                                       weights(s, QKT * GH * QK + k * COLS, QKT * GH * QK + (k + 1) * COLS)) for k in range(KVT)]
                            ).then_inc(gemm_done, 1)
                te.wait_ge(tr_read, n.at("tr"))
                te.wait_ge(qk_ready, n.step("qk"))
                for tt in range(2 * NT):
                    turn([kg[:, tt, h, :] for h in range(GH)])
                te.wait_ge(qk_ready, n.step("qk"))
                for t in range(NT):
                    turn([qg[:, t, h, :] for h in range(GH)])
                te.wait_ge(tr_read, n.at("tr"))
                te.wait_ge(gemm_read, n.at("unit"))

                def mla_scores(u):
                    t, h = u // GH, u % GH
                    te.matmul(bank[u % 4][:, :], qgT[:, h, t * P:(t + 1) * P], kgT[:, h, :], start=True, stop=True).then_inc(scores_done, 1)

                def mla_values(u, tr):
                    h = u % GH
                    te.wait_ge(tr_read, tr)
                    for j in range(4):
                        last = te.matmul(small[:, u * VD:(u + 1) * VD], prT[:, u % 2, j, :], vg[:, j, h, :], start=(j == 0), stop=(j == 3))
                    last.then_inc(pv_done, 1)

                small_bank()
                for u in range(3):
                    mla_scores(u)
                trs = []
                for u in range(8):
                    te.wait_ge(probs_ready, 8 + n.step("probs"))
                    turn([pr[:, u % 2, j * P:(j + 1) * P] for j in range(4)])
                    trs.append(n.at("tr"))
                    if u + 3 < 8:
                        mla_scores(u + 3)
                    if u:
                        mla_values(u - 1, trs[u - 1])
                mla_values(7, trs[7])

            with n.loop(te, 2, chunk=2, unit=12, tr=28, small=2, probs=16, qk=4):
                heads_group()
                heads_group()
            te.wait_ge(small_read, n.at("small"))
            for half in range(2):
                for t in range(NT):
                    turn([o_nat[:, t, (4 * half + j) * P:(4 * half + j + 1) * P] for j in range(4)])
            te.wait_ge(tr_read, n.at("tr"))
            rotation(4)
            for cb in range(2):
                rows_chunk()
            turn_rows(0)
            turn_rows(1)

            def gate_up1(first=False):
                s = chunk()
                for t in range(NT):
                    if first:
                        te.wait_ge(norm_ready, n.step("norm", 2))
                    b = unit()
                    product(b[:, :], [(act_rows(t, j), weights(s, j * COLS, (j + 1) * COLS)) for j in range(KT)],
                            second=4 if t == 0 else None).then_inc(gemm_done, 1)

            def turn_hidden1(p, k, since):
                for t in range(NT):
                    te.wait_ge(gemm_read, n.at("unit", since + 1 - t))
                    turn([h3[:, k, t, j * P:(j + 1) * P] for j in range(2)])

            def down1(p, kts):
                s = chunk()
                for cb in range(2):
                    for t in range(NT):
                        b = unit()
                        product(b[:, :], [((h3_hi[:, p, k, t * P:(t + 1) * P], h3_lo[:, p, k, t * P:(t + 1) * P]),
                                           weights(s, (kts * cb + k) * COLS, (kts * cb + k + 1) * COLS)) for k in range(kts)],
                                second=0 if cb == 1 and t == 0 else None).then_inc(gemm_done, 1)

            def group1(p):
                gate_up1()
                turn_hidden1(1 - p, 1, 2)
                gate_up1()
                turn_hidden1(p, 0, 2)
                te.wait_ge(tr_read, n.at("tr", 2))
                down1(1 - p, 4)

            gate_up1(first=True)
            gate_up1()
            turn_hidden1(0, 0, 2)
            with n.loop(te, 2, chunk=6, unit=16, tr=8):
                group1(1)
                group1(0)
            gate_up1()
            turn_hidden1(0, 1, 2)
            te.wait_ge(tr_read, n.at("tr"))
            down1(0, 4)
            turn_hidden1(1, 0, 4)
            te.wait_ge(tr_read, n.at("tr"))
            down1(1, 2)
            assert n.n["chunk"] == STREAM, (n.n["chunk"], STREAM)

        @block.scalar
        def _(act):
            n = Count()

            def split():
                n.step("split")
                c = n.n["split"]
                if c > STREAM:
                    return
                s = (c - 1) % 2
                turns = 16 * ((c + 1) // 2)
                if n.turn is not None:
                    turns = n.turn * (8 * n.per["split"]) + turns
                act.wait_ge(loaded[s], turns)
                if n.n["unit"]:
                    act.wait_ge(gemm_done, n.at("unit"))
                if n.n["mod"]:
                    act.wait_ge(mod_done, n.at("mod"))
                for half in range(2):
                    part = slice(half * HALF, (half + 1) * HALF)
                    act.activation(w_hi[:, s, part], raw[:, s, part], ACT.Copy).then_inc(hi_ready, 1)

            def roots(sources, width):
                for src, junk, k in sources:
                    if n.n["ss"]:
                        act.wait_ge(ss_done, n.at("ss"))
                    act.activation(junk, src, ACT.Square, accum_out=stat[:, SS + k:SS + k + 1]).then_inc(ss_done, 1)
                    n.step("ss")
                act.wait_ge(ss_done, n.at("ss"))
                for src, junk, k in sources:
                    act.activation(stat[:, RT + k:RT + k + 1], stat[:, SS + k:SS + k + 1], ACT.Sqrt,
                                   bias=stat[:, EPSC:EPSC + 1], scale=1.0 / width).then_inc(root_ready, 1)

            def rows_out(dst, src, k):
                act.wait_ge(rstd_ready, n.step("rstd"))
                act.activation(dst, src, ACT.Copy, scale=stat[:, RS + k:RS + k + 1]).then_inc(xn_ready, 1)
                n.step("xn")

            def scaled_hi(dsts):
                for dst in dsts:
                    n.step("tr")
                    n.step("scaled")
                    act.wait_ge(tr_read, n.at("tr"))
                    k = (n.n["scaled"] - 1) % 2
                    act.activation(dst, scaled[:, k, 0:int(np.prod(dst.shape[1:]))].rearrange("p (a b) -> p a b", a=dst.shape[1]),
                                   ACT.Copy).then_inc(norm_hi, 1)

            def plain_hi(dst):
                n.step("tr")
                act.wait_ge(tr_done, n.at("tr"))
                k = (n.n["tr"] - 1) % 2
                width = int(np.prod(dst.shape[1:]))
                act.activation(dst, turned[k][:, 0:width].rearrange("p (a b) -> p a b", a=dst.shape[1]), ACT.Copy).then_inc(tr_hi, 1)

            def act_dst(hi, q, half, t):
                return hi[:, q, 4 * half:4 * half + 4, t * P:(t + 1) * P]

            def gate_bias(gate_row):
                if n.n["small"]:
                    act.wait_ge(small_done, n.at("small"))
                act.dma_start(mod_row[4:5, :], a["mod_gate_b"][gate_row:gate_row + 1, :]).then_inc(modbias_loaded, 16)

            def mod_copy(gate_row=None):
                n.step("mod")
                if n.n["small"]:
                    act.wait_ge(small_done, n.at("small"))
                if gate_row is not None:
                    gate_bias(gate_row)
                act.wait_ge(mod_done, n.at("mod"))
                act.activation(mod_row[0:4, :], mod_ps[0:4, :], ACT.Copy).then_inc(mod_row_ready, 1)

            act.wait_ge(cond_zero, 2)
            for t in range(NT):
                act.wait_ge(x_loaded[t], 16)
                roots([(x[:, t, :], xn[:, t, :], t)], D)
            for t in range(NT):
                rows_out(xn[:, t, :], x[:, t, :], t)
            scaled_hi([act_dst(act_hi, 0, half, 0) for half in range(2)])
            split()
            act.dma_start(proj[:, 1, :], a["b_in"].rearrange("(o n) -> o n", o=1).to_broadcast([P, IN_W])).then_inc(bias_loaded, 16)
            act.dma_start(pool_m[:, :, :, :], a["pool_m"]).then_inc(bias_loaded, 16)
            act.dma_start(mask[:, :], a["mask"]).then_inc(bias_loaded, 16)
            act.dma_start(w_pool[:, :, :], a["w_pool"].rearrange("g c d -> c g d")).then_inc(bias_loaded, 16)
            scaled_hi([act_dst(act_hi, 0, half, 1) for half in range(2)])
            act.wait_ge(const_loaded, 48)
            act.activation(cond_s[:, :], col("cond", 0, 2 * KT), ACT.Silu).then_inc(cond_silu, 1)
            act.wait_ge(cond_silu, 1)
            act.activation(cond_w[:, :, 0:3:2], cond_s[:, :].rearrange("p (k s) -> p k s", s=2), ACT.Copy).then_inc(cond_hi, 1)
            for k in range(3):
                split()
                n.step("unit", 2)
            n.step("unit", 2)

            def gates_sigmoid(k):
                split()
                for t in range(NT):
                    act.wait_ge(gemm_read, n.step("unit"))
                    g = proj[:, t, G0 + k * COLS:G0 + (k + 1) * COLS]
                    act.activation(g, g, ACT.Sigmoid).then_inc(gates_ready, 1)

            def exps(u):
                t, nk = u // 4, (u // 4 + 1) * P
                n.step("unit")
                act.wait_ge(negmax_ready, u + 1)
                if u >= 4:
                    act.wait_ge(tr_done, probs_turned[u - 4])
                for e in range(2):
                    last = act.activation(prob[:, u % 4, e, 0:nk], score[:, u % 2, e, 0:nk], ACT.Exp,
                                          bias=stat[:, NM + 2 * u + e:NM + 2 * u + e + 1],
                                          accum_out=stat[:, LS + 2 * u + e:LS + 2 * u + e + 1])
                last.then_inc(probs_ready, 1)

            probs_turned = {}

            def probs_out(first):
                for u in range(first, first + 4):
                    probs_turned[u] = n.step("tr")
                t = first // 4
                act.wait_ge(sink_in, t + 1)
                act.activation(stat[:, ES + 8 * t:ES + 8 * t + 8], stat[:, ES + 8 * t:ES + 8 * t + 8], ACT.Exp).then_inc(sink_exp, 1)

            gates_sigmoid(0)
            n.step("tr", 5)
            gates_sigmoid(1)
            exps(0)
            exps(1)
            for pair in range(2):
                act.wait_ge(gemm_read, n.step("unit"))
                act.activation(ypool_hi[:, 2 * pair:2 * pair + 2, :], diff[:, 2 * pair:2 * pair + 2, :], ACT.Copy).then_inc(pool_hi, 1)
            exps(2)
            exps(3)
            gates_sigmoid(2)
            probs_out(0)
            for u in range(4, 8):
                exps(u)
            gates_sigmoid(3)
            probs_out(4)
            act.wait_ge(gemm_done, n.at("unit"))
            act.dma_start(g_post1[:, :], a["g_mix_post"].rearrange("(o n) -> o n", o=1).to_broadcast([P, D])).then_inc(post1_loaded, 16)
            split()
            n.step("unit", 4)
            for t in range(NT):
                plain_hi(yattn_hi[:, 0:4, t * P:(t + 1) * P])
            split()
            mod_copy()
            split()
            n.step("unit", 4)
            n.step("small")
            for half in range(2):
                for t in range(NT):
                    plain_hi(act_dst(act_hi, 0, half, t))
            split()
            mod_copy()
            split()
            n.step("unit", 2)
            n.step("small")
            split()
            n.step("unit", 2)

            def root_before(src, scratch, t):
                act.wait_ge(gemm_read, n.at("unit", 1 - t))
                roots([(src(t), scratch, t)], D)
                n.step("rstd")

            def root_after(t):
                act.wait_ge(x_ready, n.step("x"))
                roots([(x[:, t, :], xn[:, t, :], t)], D)

            def high(q, t):
                scaled_hi([act_dst(act_hi, q, half, t) for half in range(2)])

            def mixed(t):
                return proj[:, t, 0:D]

            diff_rows = diff[:, :, :].rearrange("p a b -> p (a b)")
            root_before(mixed, diff_rows, 0)
            root_after(0)
            root_before(mixed, diff_rows, 1)
            rows_out(xn[:, 0, :], x[:, 0, :], 0)
            mod_copy()
            split()
            root_after(1)
            act.dma_start(ctx[:, :, :], a["ctx"].rearrange("(t p) d -> p t d", p=P)).then_inc(ctx_loaded, 16)
            act.dma_start(g_post2[:, :], a["g_mlp_post"].rearrange("(o n) -> o n", o=1).to_broadcast([P, D])).then_inc(post2_loaded, 16)
            rows_out(xn[:, 1, :], x[:, 1, :], 1)
            high(0, 0)
            split()
            n.step("small")
            mod_copy()
            high(0, 1)
            n.step("small")

            def square_hidden(k):
                split()
                for t in range(NT):
                    act.wait_ge(gemm_read, n.step("unit"))
                    act.activation(h1[:, k, t, :], h1[:, k, t, :], ACT.Square).then_inc(h_ready, 1)

            def mlp_turn(first=False):
                square_hidden(0)
                split()
                mod_copy()
                for t in range(NT):
                    plain_hi(h1_hi[:, 0:4, t * P:(t + 1) * P])
                square_hidden(1)
                n.step("small")
                split()
                mod_copy()
                for t in range(NT):
                    plain_hi(h1_hi[:, 4:8, t * P:(t + 1) * P])
                split()
                n.step("unit", 2)
                n.step("small")
                if first:
                    act.wait_ge(ctx_loaded, 16)
                    roots([(ctx[:, t, :], xn[:, t, :], t) for t in range(NT)], D)
                    for t in range(NT):
                        rows_out(xn[:, t, :], ctx[:, t, :], t)
                    high(1, 0)
                split()
                n.step("unit", 2)
                if first:
                    high(1, 1)

            mlp_turn(first=True)
            with n.loop(act, 3, split=6, unit=8, tr=4, mod=2, small=2):
                mlp_turn()
            def mlp_rows(t):
                return mlp[:, t, :]

            h1_rows = h1[:, 0, :, :].rearrange("p a b -> p (a b)")
            gate_bias(0)
            root_before(mlp_rows, h1_rows, 0)
            split()
            mod_copy()
            root_before(mlp_rows, h1_rows, 1)
            root_after(0)
            split()
            rows_out(xn[:, 0, :], x[:, 0, :], 0)
            root_after(1)
            rows_out(xn[:, 1, :], x[:, 1, :], 1)
            high(0, 0)
            n.step("small", 2)
            mod_copy(1)
            high(0, 1)
            n.step("small", 2)
            act.wait_ge(tr_done, n.at("tr"))
            with n.loop(act, 4, split=2, unit=6) as i:
                for f in range(2):
                    split()
                    n.step("unit", 3)
                    act.wait_ge(gemm_read, n.at("unit"))
                    act.activation(conv_hi[:, bass.ds(i * 2 + f, 1), :, :].rearrange("p o s t -> p (o s) t"),
                                   conv_m[:, f, :, :], ACT.Copy).then_inc(h_hi, 1)
            for cb in range(2):
                split()
                n.step("unit", 4)

            def norm_both(gate_row, seqs, lag, ahead):
                def root(tt):
                    act.wait_ge(x_ready, n.step("x"))
                    roots([(res(tt), junk[:, :], tt)], D)

                def high(t):
                    scaled_hi([act_dst(act_hi, 0, half, t) for half in range(2)])

                gate_bias(gate_row)
                for t in range(NT):
                    root(t)
                    rows_out(xn[:, t, :], res(t), t)
                if lag == 1:
                    high(0)
                    root(2)
                    high(1)
                else:
                    root(2)
                    high(0)
                split()
                act.wait_ge(tr_done, n.at("tr"))
                rows_out(xn[:, 0, :], res(2), 2)
                mod_copy()
                if lag == 2:
                    high(1)
                split()
                root(3)
                act.wait_ge(tr_done, n.at("tr"))
                rows_out(xn[:, 1, :], res(3), 3)
                scaled_hi([act_dst(act_hi, 1, half, 0) for half in range(2)])
                n.step("small", seqs)
                if ahead:
                    mod_copy(gate_row + 1)
                    split()
                scaled_hi([act_dst(act_hi, 1, half, 1) for half in range(2)])
                if not ahead:
                    mod_copy(gate_row + 1)
                n.step("small", seqs)

            norm_both(2, 2, 1, False)

            def silu_chunk(early=False):
                split()
                for f in range(2):
                    n.step("unit")
                    act.wait_ge(gemm_done, n.at("unit"))
                    b = bank[(2 * f) % 4]
                    act.activation(silu[:, f, :], b[:, :], ACT.Silu).then_inc(silu_ready, 1)
                    n.step("unit")
                    if early and f:
                        split()
                    act.wait_ge(gemm_read, n.at("unit"))
                    n.step("hidden")
                    k = (n.n["hidden"] - 1) % 4
                    act.activation(h2_hi[:, k, :, :], h2[:, f, :].rearrange("p (s t) -> p s t", s=2), ACT.Copy).then_inc(h_hi, 1)

            with n.loop(act, 4, split=4, unit=16, mod=1, small=1, hidden=4):
                silu_chunk(early=True)
                mod_copy()
                silu_chunk()
                n.step("small")
                split()
                n.step("unit", 8)
            silu_chunk()
            silu_chunk()
            split()
            n.step("unit", 8)
            silu_chunk()
            split()
            n.step("unit", 8)
            norm_both(4, 1, 2, True)
            act.wait_ge(xn_ready, n.at("xn"))
            act.dma_start(w_pe[:, :, :], a["w_pe"]).then_inc(pe_loaded, 16)
            n.step("unit", 2)
            split()
            act.wait_ge(pe_loaded, 16)
            act.activation(w_pe_hi[:, :, :], w_pe[:, :, :], ACT.Copy).then_inc(wpe_hi, 1)
            n.step("unit", 4)
            act.wait_ge(tr_done, n.at("tr"))
            act.wait_ge(gemm_read, n.at("unit"))
            roots([(q_nat[:, t, :], xn[:, t, 0:QL], t) for t in range(NT)], QL)
            roots([(kv_nat[:, tt, :], scaled[:, 0, 0:KVL], 4 + tt) for tt in range(2 * NT)], KVL)
            n.step("unit")
            for t in range(NT):
                rows_out(xn[:, t, 0:QL], q_nat[:, t, :], t)
            for tt in range(2 * NT):
                rows_out(kv_nat[:, tt, :], kv_nat[:, tt, :], 4 + tt)
            act.wait_ge(pe_sum, 1)
            act.activation(stat[:, RT + 8:RT + 12], stat[:, SS + 8:SS + 12], ACT.Sqrt, bias=stat[:, EPSC:EPSC + 1],
                           scale=1.0 / ROPE).then_inc(pe_root, 1)
            split()
            mod_copy(6)
            scaled_hi([dst for t in range(NT) for dst in (ql_hi[:, 0:4, t * P:(t + 1) * P], ql_hi[:, 4:6, t * P:(t + 1) * P])])
            n.step("small")
            split()
            mod_copy(7)
            scaled_hi([kvl_hi[:, 0:2, q * SEQ:(q + 1) * SEQ] for q in range(2)])
            n.step("small")
            act.wait_ge(tr_done, n.at("tr"))

            def heads_group():
                split()
                for t in range(NT):
                    b = bank[t]
                    act.wait_ge(gemm_done, n.step("unit"))
                    act.activation(qg[:, t, :, :].rearrange("p h d -> p (h d)"), b[:, 0:GH * QK], ACT.Copy).then_inc(gemm_read, 1)
                for tt in range(2 * NT):
                    b = bank[(NT + tt) % 4]
                    act.wait_ge(gemm_done, n.step("unit"))
                    kv = b[:, :].rearrange("p (h d) -> p h d", h=GH)
                    act.activation(kg[:, tt, :, 0:NOPE], kv[:, :, 0:NOPE], ACT.Copy)
                    act.activation(vg[:, tt, :, :], kv[:, :, NOPE:NOPE + VD], ACT.Copy).then_inc(gemm_read, 1)
                act.wait_ge(gemm_read, n.at("unit"))
                act.activation(sq[:, :].rearrange("p (a d) -> p a d", d=NOPE), kg[:, :, :, 0:NOPE].rearrange("p t h d -> p (t h) d"),
                               ACT.Square).then_inc(sq_ready, 1)
                act.wait_ge(gsum_ready, n.step("gsum"))
                act.activation(stat[:, GQ + 16:GQ + 32], stat[:, GQ:GQ + 16], ACT.Sqrt, bias=stat[:, EPSC:EPSC + 1],
                               scale=1.0 / NOPE).then_inc(groot_ready, 1)
                act.activation(sq[:, 0:NT * GH * QK], qg[:, :, :, :].rearrange("p t h d -> p (t h d)"), ACT.Square).then_inc(sq_ready, 1)
                act.wait_ge(gsum_ready, n.step("gsum"))
                act.activation(stat[:, GQ + 16:GQ + 24], stat[:, GQ:GQ + 8], ACT.Sqrt, bias=stat[:, EPSC:EPSC + 1],
                               scale=1.0 / NOPE)
                act.activation(stat[:, GQ + 24:GQ + 32], stat[:, GQ + 8:GQ + 16], ACT.Sqrt, bias=stat[:, EPSC:EPSC + 1],
                               scale=1.0 / ROPE).then_inc(groot_ready, 1)
                for tt in range(2 * NT):
                    act.wait_ge(tr_done, n.step("tr"))
                    k = (n.n["tr"] - 1) % 2
                    act.activation(kgT[:, :, tt * P:(tt + 1) * P], turned[k][0:QK, :].rearrange("p (h t) -> p h t", h=GH),
                                   ACT.Copy).then_inc(tr_read, 1)
                for t in range(NT):
                    act.wait_ge(tr_done, n.step("tr"))
                    k = (n.n["tr"] - 1) % 2
                    act.activation(qgT[:, :, t * P:(t + 1) * P], turned[k][0:QK, :].rearrange("p (h t) -> p h t", h=GH),
                                   ACT.Copy).then_inc(tr_read, 1)
                for u in range(8):
                    act.wait_ge(negmax_ready, 8 + n.step("negmax"))
                    if u >= 2:
                        act.wait_ge(tr_done, n.at("tr", 1))
                    act.activation(pr[:, u % 2, :], bank[u % 4][:, :], ACT.Exp, bias=stat[:, NM + u:NM + u + 1], scale=QK ** -0.5,
                                   accum_out=stat[:, LS + u:LS + u + 1]).then_inc(probs_ready, 1)
                    n.step("tr")

            with n.loop(act, 2, split=2, unit=12, tr=28, gsum=4, negmax=16):
                heads_group()
                heads_group()
            for half in range(2):
                for t in range(NT):
                    plain_hi(act_dst(act_hi, 0, half, t))
            for cb in range(2):
                split()
                n.step("unit", 2)
            for t in range(NT):
                root_after(t)
                rows_out(xn[:, t, :], x[:, t, :], t)
            scaled_hi([act_dst(act_hi, 0, half, t) for t in range(NT) for half in range(2)])

            def silu_rows(k):
                split()
                for t in range(NT):
                    act.wait_ge(gemm_done, n.step("unit"))
                    act.wait_ge(gemm_read, n.at("unit", 2))
                    b = bank[(2 * k + t) % 4]
                    act.activation(silu3[:, t, :], b[:, 0:256], ACT.Silu).then_inc(silu_ready, 1)

            def turned_hi(p, k):
                for t in range(NT):
                    plain_hi(h3_hi[:, p, 2 * k:2 * k + 2, t * P:(t + 1) * P])

            def group1(p):
                silu_rows(0)
                turned_hi(1 - p, 1)
                silu_rows(1)
                turned_hi(p, 0)
                split()
                n.step("unit", 4)

            silu_rows(0)
            silu_rows(1)
            turned_hi(0, 0)
            with n.loop(act, 2, split=6, unit=16, tr=8):
                group1(1)
                group1(0)
            silu_rows(0)
            turned_hi(0, 1)
            split()
            n.step("unit", 4)
            turned_hi(1, 0)
            split()

        @block.vector
        def _(ve):
            n = Count()

            def chained(ins):
                ins.then_inc(dve_chain, 1)
                ve.wait_ge(dve_chain, n.step("chain"))

            def split():
                n.step("split")
                if n.n["split"] > STREAM:
                    return
                s = (n.n["split"] - 1) % 2
                for half in range(2):
                    part = slice(half * HALF, half * HALF + SHARE)
                    ve.wait_ge(hi_ready, 2 * n.at("split") - 1 + half)
                    ve.tensor_tensor(w_lo[:, s, part], raw[:, s, part], w_hi[:, s, part].bitcast(f32),
                                     ALU.subtract).then_inc(lo_ready, 1)

            rot = {"first": 0, "banks": 4}

            def rotation(banks):
                rot["first"], rot["banks"] = n.n["unit"], banks

            def unit():
                ve.wait_ge(gemm_done, n.step("unit"))
                return bank[(n.n["unit"] - 1 - rot["first"]) % rot["banks"]]

            def recips(ks):
                for k in ks:
                    ve.wait_ge(root_ready, n.step("root"))
                    ve.reciprocal(stat[:, RS + k:RS + k + 1], stat[:, RT + k:RT + k + 1]).then_inc(rstd_ready, 1)
                    n.step("rstd")

            def scaled_rows(items):
                def lower(hi, lo):
                    ve.wait_ge(norm_hi, n.step("norm"))
                    k = (n.n["norm"] - 1) % 2
                    src = scaled[:, k, 0:int(np.prod(lo.shape[1:]))].rearrange("p (a b) -> p a b", a=lo.shape[1])
                    ve.tensor_tensor(lo, src, hi.bitcast(f32), ALU.subtract).then_inc(norm_ready, 1)

                before = None
                for gain, shift, hi, lo in items:
                    n.step("scaled")
                    ve.wait_ge(tr_done, n.step("tr"))
                    k, b = (n.n["scaled"] - 1) % 2, (n.n["tr"] - 1) % 2
                    m, w = lo.shape[1], lo.shape[2]
                    dst = scaled[:, k, 0:m * w].rearrange("p (a b) -> p a b", a=m)
                    if n.n["scaled"] > 2:
                        ve.wait_ge(norm_ready, n.at("scaled", 2))
                    src = turned[b][:, 0:m * w].rearrange("p (a b) -> p a b", a=m)
                    if shift is None:
                        last = ve.tensor_tensor(dst, src, gain.to_broadcast([P, m, w]), ALU.mult)
                    else:
                        for j in range(m):
                            last = ve.tensor_scalar(dst[:, j, :], src[:, j, :], gain[:, j, :], shift[:, j, :], ALU.mult, ALU.add)
                    last.then_inc(tr_read, 1)
                    if before:
                        lower(*before)
                    before = (hi, lo)
                lower(*before)

            def plain_rows(hi, lo):
                n.step("tr")
                ve.wait_ge(tr_hi, n.step("tr_hi"))
                b = (n.n["tr"] - 1) % 2
                m, w = lo.shape[1], lo.shape[2]
                ve.tensor_tensor(lo, turned[b][:, 0:m * w].rearrange("p (a b) -> p a b", a=m), hi.bitcast(f32),
                                 ALU.subtract).then_inc(tr_read, 1)

            def act_dst(buf, q, half, t):
                return buf[:, q, 4 * half:4 * half + 4, t * P:(t + 1) * P]

            def gain_cols(name, j, m):
                return col(name, j, m).rearrange("p (a o) -> p a o", o=1)

            def gained(name, t):
                return [(gain_cols(name, 4 * half, 4), None, act_dst(act_hi, 0, half, t), act_dst(act_lo, 0, half, t)) for half in range(2)]

            def modulated(c, shift_at, q, t):
                return [(coef[:, c, 4 * half:4 * half + 4, q:q + 1], mod_col[:, shift_at + 4 * half:shift_at + 4 * half + 4, q:q + 1],
                         act_dst(act_hi, q, half, t), act_dst(act_lo, q, half, t)) for half in range(2)]

            def coefs(c, name, layer, scale_at):
                chained(ve.scalar_tensor_tensor(coef[:, c, :, :], mod_col[:, scale_at:scale_at + KT, :], 1.0,
                                                gain_cols(name, layer * KT, KT).to_broadcast([P, KT, 2]), ALU.add, ALU.mult))

            def mod_read(chunk, turn=None, step=0):
                n.step("small")
                ve.wait_ge(small_done, n.step("mod_small"))
                if turn is None:
                    dst, b = mod_col[:, 4 * chunk:4 * chunk + 4, :], col("mod_b", 4 * chunk, 4)
                else:
                    dst = mod_col[:, bass.ds(turn * (4 * step) + 4 * chunk, 4), :]
                    b = cols[:, bass.ds(turn * (4 * step) + COL["mod_b"] + 4 * chunk, 4)]
                ve.tensor_tensor(dst, small[:, 0:8].rearrange("p (k s) -> p k s", s=2),
                                 b.rearrange("p (a o) -> p a o", o=1).to_broadcast([P, 4, 2]), ALU.add).then_inc(small_read, 1)

            def gate_read(half, slots):
                for s in slots:
                    n.step("small")
                    ve.wait_ge(small_done, n.step("mod_small"))
                    ve.tensor_copy(gate[:, s, half * COLS:(half + 1) * COLS], small[:, :]).then_inc(small_read, 1)

            def post_norm(src, g, t):
                recips([t])
                ve.wait_ge(rstd_ready, n.at("rstd"))
                chained(ve.scalar_tensor_tensor(src, src, stat[:, RS + t:RS + t + 1], g[:, :], ALU.mult, ALU.mult))
                ve.tensor_tensor(x[:, t, :], x[:, t, :], src, ALU.add).then_inc(x_ready, 1)
                n.step("x")

            ve.memset(cond_w[:, :, :].bitcast(f32), 0.0).then_inc(cond_zero, 1)
            ve.memset(stat[:, EPSC:EPSC + 1], EPS).then_inc(cond_zero, 1)
            recips([0, 1])
            ve.wait_ge(const_loaded, 48)
            ve.tensor_scalar(stat[:, NSINK:NSINK + 8], row("sinks", HEADS), -1.0, None, ALU.mult)
            ve.tensor_tensor(row("kn_nope", NOPE), row("kn_nope", NOPE), row("qn_nope", NOPE), ALU.mult)
            scaled_rows(gained("g_mix", 0))
            split()
            scaled_rows(gained("g_mix", 1))
            ve.wait_ge(cond_hi, 1)
            ve.tensor_tensor(cond_w[:, :, 1:4:2], cond_s[:, :].rearrange("p (k s) -> p k s", s=2),
                             cond_w[:, :, 0:3:2].bitcast(f32), ALU.subtract).then_inc(cond_ready, 1)
            for k, (c0, width) in enumerate(((0, COLS), (Q0, COLS), (K0, 256))):
                split()
                if k == 0:
                    ve.wait_ge(bias_loaded, 64)
                for t in range(NT):
                    b = unit()
                    ve.tensor_tensor(proj[:, t, c0:c0 + width], b[:, 0:width], proj[:, 1, c0:c0 + width], ALU.add).then_inc(gemm_read, 1)
            for pair in range(2):
                b = unit()
                ve.tensor_copy(diff[:, 2 * pair:2 * pair + 2, :].rearrange("p g t -> p (g t)"), b[:, :]).then_inc(gemm_read, 1)
            for t in range(NT):
                heads = proj[:, t, Q0:V0].rearrange("p (h d) -> p h d", d=HD)
                lo, hi = heads[:, :, 0:8], heads[:, :, 8:16]
                c = table("cos1", 8, j=8 * t).rearrange("p (o d) -> p o d", o=1).to_broadcast([P, 10, 8])
                s = table("sin1", 8, j=8 * t).rearrange("p (o d) -> p o d", o=1).to_broadcast([P, 10, 8])
                for j, (src, by) in enumerate(((lo, c), (hi, s), (hi, c), (lo, s))):
                    last = ve.tensor_tensor(rope_t[:, j, t, :, :], src, by, ALU.mult)
                chained(last)
                ve.tensor_tensor(lo, rope_t[:, 0, t, :, :], rope_t[:, 1, t, :, :], ALU.subtract)
                last = ve.tensor_tensor(hi, rope_t[:, 2, t, :, :], rope_t[:, 3, t, :, :], ALU.add)
            last.then_inc(rope_ready, 1)

            def gates_bias(k):
                split()
                for t in range(NT):
                    b = unit()
                    g = slice(G0 + k * COLS, G0 + (k + 1) * COLS)
                    ve.tensor_tensor(proj[:, t, g], b[:, :], proj[:, 1, g], ALU.add).then_inc(gemm_read, 1)

            gates_bias(0)
            for t in range(NT):
                for half in range(2):
                    ve.wait_ge(tr_done, n.step("tr"))
                    ve.tensor_copy(qT[:, 4 * half:4 * half + 4, t * P:(t + 1) * P],
                                   turned[(n.n["tr"] - 1) % 2][0:HD, :].rearrange("p (h t) -> p h t", h=4)).then_inc(tr_read, 1)
            ve.wait_ge(tr_done, n.step("tr"))
            ve.tensor_copy(kT[:, :, :], turned[(n.n["tr"] - 1) % 2][0:HD, :].rearrange("p (j t) -> p j t", j=KVH)).then_inc(tr_read, 1)
            gates_bias(1)

            def maxima(u):
                t, p = u // 4, u % 4
                nk = (t + 1) * P
                b = unit()
                if u >= 2:
                    ve.wait_ge(probs_ready, u - 1)
                seen = mask[:, (1 - t) * P:(1 - t) * P + nk].rearrange("p (o k) -> p o k", o=1).to_broadcast([P, 2, nk])
                sc = score[:, u % 2, :, 0:nk]
                ve.scalar_tensor_tensor(sc, b[:, 0:2 * nk].rearrange("p (e k) -> p e k", e=2), HD ** -0.5, seen,
                                        ALU.mult, ALU.add).then_inc(gemm_read, 1)
                ve.wait_ge(gemm_read, n.at("unit"))
                chained(ve.tensor_reduce(stat[:, MX:MX + 2], sc, AX.X, ALU.max))
                ve.scalar_tensor_tensor(stat[:, NM + 2 * u:NM + 2 * u + 2], stat[:, MX:MX + 2], -1.0,
                                        stat[:, NSINK + 2 * p:NSINK + 2 * p + 2], ALU.mult, ALU.min).then_inc(negmax_ready, 1)

            def probs_out(first):
                t = first // 4
                ve.wait_ge(negmax_ready, first + 4)
                ve.tensor_tensor(stat[:, ES + 8 * t:ES + 8 * t + 8], row("sinks", HEADS), stat[:, NM + 8 * t:NM + 8 * t + 8],
                                 ALU.add).then_inc(sink_in, 1)
                for u in range(first, first + 4):
                    ve.wait_ge(tr_done, n.step("tr"))
                    if u >= 2:
                        ve.wait_ge(pv_done, u - 1)
                    m = 2 * (t + 1)
                    ve.tensor_copy(pT[:, u % 2, 0:m, :], turned[(n.n["tr"] - 1) % 2][:, 0:m * P].rearrange("p (a b) -> p a b", a=m)
                                   ).then_inc(tr_read, 1)
                ve.wait_ge(sink_exp, t + 1)
                ve.wait_ge(probs_ready, first + 4)
                den = stat[:, RD + 8 * t:RD + 8 * t + 8]
                chained(ve.tensor_tensor(den, stat[:, LS + 8 * t:LS + 8 * t + 8], stat[:, ES + 8 * t:ES + 8 * t + 8], ALU.add))
                chained(ve.reciprocal(den, den))
                ve.wait_ge(pv_done, first + 4)
                n.step("small")
                ve.tensor_tensor(proj[:, t, 0:POOL].rearrange("p (h d) -> p h d", d=HD), small[:, :].rearrange("p (h d) -> p h d", d=HD),
                                 den.rearrange("p (h o) -> p h o", o=1).to_broadcast([P, HEADS, HD]), ALU.mult).then_inc(small_read, 1)

            maxima(0)
            maxima(1)
            for pair in range(2):
                b = unit()
                g = slice(2 * pair, 2 * pair + 2)
                ve.tensor_tensor(diff[:, g, :], b[:, :].rearrange("p (g t) -> p g t", g=2),
                                 gain_cols("pool_scale", 2 * pair, 2).to_broadcast([P, 2, SEQ]), ALU.mult).then_inc(gemm_read, 1)
            maxima(2)
            maxima(3)
            for pair in range(2):
                g = slice(2 * pair, 2 * pair + 2)
                ve.wait_ge(pool_hi, pair + 1)
                ve.tensor_tensor(ypool_lo[:, g, :], diff[:, g, :], ypool_hi[:, g, :].bitcast(f32), ALU.subtract).then_inc(pool_lo, 1)
            gates_bias(2)
            probs_out(0)
            for u in range(4, 8):
                maxima(u)
            gates_bias(3)
            probs_out(4)

            def branch(g0, first):
                split()
                for cb in range(2):
                    for t in range(NT):
                        b = unit()
                        g = proj[:, t, g0 + cb * COLS:g0 + (cb + 1) * COLS]
                        ve.wait_ge(gates_ready, 2 * (first + cb) + t + 1)
                        ve.tensor_tensor(g, g, b[:, :], ALU.mult).then_inc(gemm_read, 1)
                        if first:
                            ve.wait_ge(gemm_read, n.at("unit"))
                            m = proj[:, t, G0 + cb * COLS:G0 + (cb + 1) * COLS]
                            ve.tensor_tensor(m, m, g, ALU.add).then_inc(merged_ready, 1)

            branch(G0, 0)
            for t in range(NT):
                plain_rows(yattn_hi[:, 0:4, t * P:(t + 1) * P], yattn_lo[:, 0:4, t * P:(t + 1) * P])
            split()
            branch(G0 + D, 2)
            mod_read(0)
            for half in range(2):
                for t in range(NT):
                    plain_rows(act_dst(act_hi, 0, half, t), act_dst(act_lo, 0, half, t))
            split()

            def mixed_rows(cb, t):
                b = unit()
                ve.tensor_copy(proj[:, t, cb * COLS:(cb + 1) * COLS], b[:, :]).then_inc(gemm_read, 1)
                ve.wait_ge(gemm_read, n.at("unit"))

            split()
            for t in range(NT):
                mixed_rows(0, t)
            mod_read(1)
            split()
            ve.wait_ge(post1_loaded, 16)
            mixed_rows(1, 0)
            post_norm(proj[:, 0, 0:D], g_post1, 0)
            mixed_rows(1, 1)
            recips([0])
            post_norm(proj[:, 1, 0:D], g_post1, 1)
            split()
            recips([1])
            scaled_rows(gained("g_mlp", 0))
            mod_read(2)
            split()
            scaled_rows(gained("g_mlp", 1))
            mod_read(3)
            ve.wait_ge(small_read, n.at("small"))
            coefs(0, "norm_mix", 0, 8)
            ve.memset(mlp[:, :, :], 0.0).then_inc(dve_chain, 1)
            ve.wait_ge(dve_chain, n.step("chain"))

            def rectify(k):
                split()
                for t in range(NT):
                    b = unit()
                    ve.tensor_scalar(h1[:, k, t, :], b[:, :], 0.0, None, ALU.max).then_inc(gemm_read, 1)

            def down_rows(cb):
                split()
                for t in range(NT):
                    b = unit()
                    dst = mlp[:, t, cb * COLS:(cb + 1) * COLS]
                    ve.tensor_tensor(dst, b[:, :], dst, ALU.add).then_inc(gemm_read, 1)

            def mlp_turn(i=None):
                at_chunk, step = (4, 0) if i is None else (6, 2)
                for k in range(2):
                    rectify(k)
                    if k:
                        mod_read(at_chunk, i, step)
                    split()
                    for t in range(NT):
                        plain_rows(h1_hi[:, 4 * k:4 * k + 4, t * P:(t + 1) * P], h1_lo[:, 4 * k:4 * k + 4, t * P:(t + 1) * P])
                if i is None:
                    recips([0, 1])
                down_rows(0)
                mod_read(at_chunk + 1, i, step)
                if i is None:
                    scaled_rows(modulated(0, 0, 1, 0))
                down_rows(1)
                if i is None:
                    scaled_rows(modulated(0, 0, 1, 1))

            mlp_turn()
            with n.loop(ve, 3, split=6, unit=8, tr=4, tr_hi=4, small=2, mod_small=2) as i:
                mlp_turn(i)
            ve.wait_ge(post2_loaded, 16)
            post_norm(mlp[:, 0, :], g_post2, 0)
            split()
            post_norm(mlp[:, 1, :], g_post2, 1)
            recips([0])
            split()
            recips([1])
            for t in range(NT):
                scaled_rows(modulated(0, 0, 0, t))
                gate_read(0, (t,))
            gate_read(1, (0, 1))
            ve.wait_ge(tr_done, n.at("tr"))
            ve.memset(z_pad[:, :, 0:1], 0.0)
            chained(ve.memset(z_pad[:, :, SEQ + 1:SEQ + 2], 0.0))
            rotation(3)

            def tap(name, i, f):
                return cols[:, bass.ds(i * 2 + COL[name] + f, 1)]

            with n.loop(ve, 4, split=2, unit=6, h=2, chain=6) as i:
                for f in range(2):
                    split()
                    b = unit()
                    ve.tensor_copy(c_sb[:, :, :].rearrange("p s t -> p (s t)"), b[:, :]).then_inc(gemm_read, 1)
                    ve.wait_ge(gemm_read, n.at("unit"))
                    b = unit()
                    ve.tensor_tensor(z_pad[:, :, 1:SEQ + 1], c_sb[:, :, :], b[:, :].rearrange("p (s t) -> p s t", s=2),
                                     ALU.mult).then_inc(gemm_read, 1)
                    ve.wait_ge(gemm_read, n.at("unit"))
                    chained(ve.tensor_scalar(conv_y[:, :, :], z_pad[:, :, 1:SEQ + 1], tap("conv_k1", i, f), tap("conv_b", i, f),
                                             ALU.mult, ALU.add))
                    chained(ve.scalar_tensor_tensor(conv_y[:, :, :], z_pad[:, :, 0:SEQ], tap("conv_k0", i, f), conv_y[:, :, :],
                                                    ALU.mult, ALU.add))
                    chained(ve.scalar_tensor_tensor(conv_y[:, :, :], z_pad[:, :, 2:SEQ + 2], tap("conv_k2", i, f), conv_y[:, :, :],
                                                    ALU.mult, ALU.add))
                    b = unit()
                    ve.tensor_tensor(conv_m[:, f, :, :], conv_y[:, :, :], b[:, :].rearrange("p (s t) -> p s t", s=2),
                                     ALU.mult).then_inc(gemm_read, 1)
                    ve.wait_ge(h_hi, n.step("h"))
                    ve.tensor_tensor(conv_lo[:, bass.ds(i * 2 + f, 1), :, :].rearrange("p o s t -> p (o s) t"), conv_m[:, f, :, :],
                                     conv_hi[:, bass.ds(i * 2 + f, 1), :, :].rearrange("p o s t -> p (o s) t").bitcast(f32),
                                     ALU.subtract).then_inc(h_lo, 1)
            rotation(4)

            def add_gated(tt, cb, g, last):
                b = unit()
                k = n.n["unit"] % 2
                r = res(tt)[:, cb * COLS:(cb + 1) * COLS]
                ve.tensor_tensor(gated[:, k, :], b[:, :], gate[:, g, cb * COLS:(cb + 1) * COLS], ALU.mult).then_inc(gemm_read, 1)
                ve.wait_ge(gemm_read, n.at("unit"))
                ins = ve.tensor_tensor(r, r, gated[:, k, :], ALU.add)
                if last:
                    ins.then_inc(x_ready, 1)
                else:
                    ins.then_inc(dve_chain, 1)
                    n.step("chain")

            split()
            for tt in range(2 * NT):
                add_gated(tt, 0, tt // NT, False)
            split()

            def norm_both(add, c, layer, gain, shift_at, slots, lag, ahead):
                coefs(c, gain, layer, shift_at + 8)
                def summed(tt):
                    ve.wait_ge(norm_ready, n.at("norm"))
                    add(tt)
                    ve.wait_ge(x_ready, n.step("x"))

                def normed(t):
                    scaled_rows(modulated(c, shift_at, 0, t))

                summed(0)
                if lag == 1:
                    recips([0])
                    summed(1)
                    recips([1])
                    normed(0)
                    summed(2)
                    normed(1)
                else:
                    summed(1)
                    recips([0])
                    summed(2)
                    recips([1])
                    normed(0)
                summed(3)
                recips([2])
                split()
                if lag == 2:
                    normed(1)
                split()
                recips([3])
                for t in range(NT):
                    scaled_rows(modulated(c, shift_at, 1, t))
                    gate_read(0, slots[t::NT])
                    if ahead and t == 0:
                        split()
            norm_both(lambda tt: add_gated(tt, 1, tt // NT, True), 1, 0, "norm_ffn", 16, (0, 1), 1, False)
            gate_read(1, (0, 1))

            def hidden_chunk(early=False):
                split()
                for f in range(2):
                    n.step("unit")
                    b = unit()
                    ve.wait_ge(silu_ready, n.step("silu"))
                    ve.tensor_tensor(h2[:, f, :], silu[:, f, :], b[:, :], ALU.mult).then_inc(gemm_read, 2)
                    if early and f:
                        split()
                    ve.wait_ge(h_hi, 8 + n.step("hidden"))
                    k = (n.n["hidden"] - 1) % 4
                    ve.tensor_tensor(h2_lo[:, k, :, :], h2[:, f, :].rearrange("p (s t) -> p s t", s=2), h2_hi[:, k, :, :].bitcast(f32),
                                     ALU.subtract).then_inc(h_lo, 1)

            def down_gated():
                split()
                for cb in range(2):
                    for tt in range(2 * NT):
                        add_gated(tt, cb, tt // NT, False)

            with n.loop(ve, 4, split=4, unit=16, small=1, mod_small=1, silu=4, hidden=4, chain=8) as i:
                hidden_chunk(early=True)
                hidden_chunk()
                mod_read(12, i, 1)
                down_gated()
            hidden_chunk()
            hidden_chunk()
            down_gated()
            hidden_chunk()
            split()

            def down_rows0(tt):
                for cb in range(2):
                    add_gated(tt, cb, tt // NT, cb == 1)

            ve.wait_ge(small_read, n.at("small"))
            norm_both(down_rows0, 2, 1, "norm_mix", 32, (0,), 2, True)
            for t in range(NT):
                b = unit()
                ve.tensor_copy(q_nat[:, t, 0:COLS], b[:, :]).then_inc(gemm_read, 1)
            split()
            for tt in range(2 * NT):
                b = unit()
                if tt < NT:
                    ve.tensor_copy(q_nat[:, tt, COLS:QL], b[:, 0:256])
                ve.tensor_copy(kv_nat[:, tt, :], b[:, 256:COLS]).then_inc(gemm_read, 1)
                if tt == 0:
                    gate_read(1, (0,))
            ve.wait_ge(wpe_hi, 1)
            ve.tensor_tensor(w_pe_lo[:, :, :], w_pe[:, :, :], w_pe_hi[:, :, :].bitcast(f32), ALU.subtract).then_inc(wpe_lo, 1)
            recips([0, 1] + list(range(4, 8)))
            b = unit()
            ve.tensor_copy(pe[:, :, :].rearrange("p t d -> p (t d)"), b[:, 0:2 * NT * ROPE]).then_inc(gemm_read, 1)
            ve.wait_ge(gemm_read, n.at("unit"))
            chained(ve.tensor_tensor(pe_t[:, :, :], pe[:, :, :], pe[:, :, :], ALU.mult))
            ve.tensor_reduce(stat[:, SS + 8:SS + 12], pe_t[:, :, :], AX.X, ALU.add).then_inc(pe_sum, 1)
            ve.wait_ge(pe_root, 1)
            chained(ve.reciprocal(stat[:, RS + 8:RS + 12], stat[:, RT + 8:RT + 12]))
            chained(ve.tensor_tensor(pe[:, :, :], pe[:, :, :],
                                     stat[:, RS + 8:RS + 12].rearrange("p (t o) -> p t o", o=1).to_broadcast([P, 2 * NT, ROPE]), ALU.mult))
            chained(ve.tensor_tensor(pe[:, :, :], pe[:, :, :],
                                     row("kn_rope", ROPE).rearrange("p (o d) -> p o d", o=1).to_broadcast([P, 2 * NT, ROPE]), ALU.mult))

            def halves(ap, k):
                return ap.rearrange("p h (a k d) -> p h a k d", a=2, k=2)[:, :, :, k, :]

            def rotate(src, tmp, t, heads):
                def tabs(name):
                    return table(name, ROPE, j=ROPE * t).rearrange("p (o d) -> p o d", o=1)

                for k in range(2):
                    s = halves(tabs("sinm"), k).to_broadcast([P, heads, 2, 8])
                    last = ve.tensor_tensor(halves(tmp, k), halves(src, 1 - k), s, ALU.mult)
                chained(last)
                chained(ve.tensor_tensor(src, src, tabs("cosm").to_broadcast([P, heads, ROPE]), ALU.mult))
                return ve.tensor_tensor(src, src, tmp, ALU.add)

            for t in range(NT):
                chained(rotate(pe[:, t:t + 1, :], pe_t[:, t:t + 1, :], t, 1))
            split()
            scaled_rows([item for t in range(NT) for item in (
                (gain_cols("q_norm", 0, 4), None, ql_hi[:, 0:4, t * P:(t + 1) * P], ql_lo[:, 0:4, t * P:(t + 1) * P]),
                (gain_cols("q_norm", 4, 2), None, ql_hi[:, 4:6, t * P:(t + 1) * P], ql_lo[:, 4:6, t * P:(t + 1) * P]))])
            gate_read(0, (1,))
            split()
            scaled_rows([(gain_cols("kv_norm", 0, 2), None, kvl_hi[:, 0:2, q * SEQ:(q + 1) * SEQ], kvl_lo[:, 0:2, q * SEQ:(q + 1) * SEQ])
                         for q in range(2)])
            gate_read(1, (1,))
            for tt in range(2 * NT):
                last = ve.tensor_copy(kg[:, tt, :, NOPE:QK], pe[:, tt:tt + 1, :].to_broadcast([P, GH, ROPE]))
            chained(last)

            def heads_group(i, g):
                split()
                n.step("unit", 6)
                KH = 2 * NT * GH
                ve.wait_ge(sq_ready, n.step("sq"))
                ve.tensor_reduce(stat[:, GQ:GQ + KH], sq[:, :].rearrange("p (a d) -> p a d", d=NOPE), AX.X, ALU.add).then_inc(gsum_ready, 1)
                ve.wait_ge(groot_ready, n.step("groot"))
                chained(ve.reciprocal(stat[:, GQ + 32:GQ + 32 + KH], stat[:, GQ + 16:GQ + 16 + KH]))
                kn = kg[:, :, :, 0:NOPE].rearrange("p t h d -> p (t h) d")
                ve.tensor_tensor(kn, kn, stat[:, GQ + 32:GQ + 32 + KH].rearrange("p (a o) -> p a o", o=1).to_broadcast([P, KH, NOPE]),
                                 ALU.mult).then_inc(qk_ready, 1)
                QH = NT * GH
                qf = qg[:, :, :, :].rearrange("p t h d -> p (t h) d")
                sf = sq[:, 0:QH * QK].rearrange("p (a d) -> p a d", d=QK)
                ve.wait_ge(sq_ready, n.step("sq"))
                ve.tensor_reduce(stat[:, GQ:GQ + QH], sf[:, :, 0:NOPE], AX.X, ALU.add)
                ve.tensor_reduce(stat[:, GQ + QH:GQ + 2 * QH], sf[:, :, NOPE:QK], AX.X, ALU.add).then_inc(gsum_ready, 1)
                ve.wait_ge(groot_ready, n.step("groot"))
                chained(ve.reciprocal(stat[:, GQ + 32:GQ + 32 + 2 * QH], stat[:, GQ + 16:GQ + 16 + 2 * QH]))
                for first, c0, c1 in ((0, 0, NOPE), (QH, NOPE, QK)):
                    r = stat[:, GQ + 32 + first:GQ + 32 + first + QH].rearrange("p (a o) -> p a o", o=1)
                    last = ve.tensor_tensor(qf[:, :, c0:c1], qf[:, :, c0:c1], r.to_broadcast([P, QH, c1 - c0]), ALU.mult)
                chained(last)
                ve.tensor_tensor(qf[:, :, 0:NOPE], qf[:, :, 0:NOPE],
                                 row("kn_nope", NOPE).rearrange("p (o d) -> p o d", o=1).to_broadcast([P, QH, NOPE]), ALU.mult)
                chained(ve.tensor_tensor(qf[:, :, NOPE:QK], qf[:, :, NOPE:QK],
                                         row("qn_rope", ROPE).rearrange("p (o d) -> p o d", o=1).to_broadcast([P, QH, ROPE]), ALU.mult))
                for t in range(NT):
                    last = rotate(qg[:, t, :, NOPE:QK], qr_t[:, t, :, :], t, GH)
                last.then_inc(qk_ready, 1)
                n.step("tr", 6)

                def mla_max(u):
                    ve.wait_ge(scores_done, n.step("scores"))
                    chained(ve.tensor_reduce(stat[:, MX + u:MX + u + 1], bank[u % 4][:, :], AX.X, ALU.max))
                    ve.tensor_scalar(stat[:, NM + u:NM + u + 1], stat[:, MX + u:MX + u + 1], -QK ** -0.5, None, ALU.mult).then_inc(negmax_ready, 1)

                for u in range(2):
                    mla_max(u)
                for u in range(8):
                    if u + 2 < 8:
                        mla_max(u + 2)
                    ve.wait_ge(tr_done, n.step("tr"))
                    n.step("pv")
                    if u >= 2:
                        ve.wait_ge(pv_done, 8 + n.at("pv", 2))
                    ve.tensor_copy(prT[:, u % 2, :, :], turned[(n.n["tr"] - 1) % 2][:, :].rearrange("p (a b) -> p a b", a=4)).then_inc(tr_read, 1)
                rd = stat[:, RD:RD + 8]
                ve.wait_ge(probs_ready, 8 + n.step("probs", 8))
                chained(ve.reciprocal(rd, stat[:, LS:LS + 8]))
                ve.wait_ge(pv_done, 8 + n.at("pv"))
                n.step("small")
                for t in range(NT):
                    dst = o_nat[:, t, bass.ds(i * (2 * GH * VD) + g * GH * VD, GH * VD)].rearrange("p (h d) -> p h d", d=VD)
                    last = ve.tensor_tensor(dst, small[:, t * GH * VD:(t + 1) * GH * VD].rearrange("p (h d) -> p h d", d=VD),
                                            rd[:, t * GH:(t + 1) * GH].rearrange("p (h o) -> p h o", o=1).to_broadcast([P, GH, VD]), ALU.mult)
                last.then_inc(small_read, 1)

            with n.loop(ve, 2, split=2, unit=12, tr=28, scores=16, small=2, sq=4, groot=4, probs=16, pv=16, chain=2 * 17) as i:
                heads_group(i, 0)
                heads_group(i, 1)
            for half in range(2):
                for t in range(NT):
                    plain_rows(act_dst(act_hi, 0, half, t), act_dst(act_lo, 0, half, t))
            rotation(4)
            coefs(3, "norm_ffn", 1, 56)
            for cb in range(2):
                split()
                for t in range(NT):
                    add_gated(t, cb, 0, cb == 1)
                    if cb:
                        recips([t])
            ve.wait_ge(x_ready, n.step("x", 2))
            scaled_rows(modulated(3, 48, 0, 0) + modulated(3, 48, 0, 1))

            def hidden_rows(k):
                split()
                for t in range(NT):
                    b = unit()
                    ve.wait_ge(silu_ready, n.step("silu"))
                    ve.tensor_tensor(h3[:, k, t, :], silu3[:, t, :], b[:, 256:COLS], ALU.mult).then_inc(gemm_read, 1)

            def turn_hidden1(p, k):
                for t in range(NT):
                    where = (slice(None), p, slice(2 * k, 2 * k + 2), slice(t * P, (t + 1) * P))
                    plain_rows(h3_hi[where], h3_lo[where])

            def down1(final=False):
                split()
                for cb in range(2):
                    for t in range(NT):
                        add_gated(t, cb, 1, final and cb == 1)

            def group1(p):
                hidden_rows(0)
                turn_hidden1(1 - p, 1)
                hidden_rows(1)
                turn_hidden1(p, 0)
                down1()

            hidden_rows(0)
            hidden_rows(1)
            turn_hidden1(0, 0)
            with n.loop(ve, 2, split=6, unit=16, tr=8, tr_hi=8, silu=8, chain=8):
                group1(1)
                group1(0)
            hidden_rows(0)
            turn_hidden1(0, 1)
            down1()
            turn_hidden1(1, 0)
            down1(final=True)


def _rows_first(w, kts):
    return w.reshape(kts, P, w.shape[1]).transpose(1, 0, 2).reshape(P, -1)


def _blocks(w):
    return [_rows_first(w[:, c:c + COLS], KT) for c in range(0, w.shape[1], COLS)]


def _down(w):
    kts = w.shape[0] // P
    return w.reshape(kts, P, 2, COLS).transpose(1, 2, 0, 3).reshape(P, -1)


def _tables():
    ident = np.eye(P, dtype=np.float32)
    rel = np.arange(P)[:, None] + P - np.arange(2 * P)[None, :]
    mask = np.where((rel >= 0) & (rel < P), 0.0, -1e30).astype(np.float32)

    def token_rows(t):
        return t.astype(np.float32).reshape(NT, P, -1).transpose(1, 0, 2).reshape(P, -1)

    inv1 = (500000.0 ** (-np.arange(0, ROT, 2, dtype=np.float32).astype(np.float64) / ROT)).astype(np.float32)
    ang1 = (np.arange(SEQ, dtype=np.float32)[:, None] * inv1[None, :]).astype(np.float64)
    inv2 = (10000.0 ** (-np.arange(0, ROPE // 2, 2).astype(np.float64) / (ROPE // 2))).astype(np.float32)
    grid = 64
    r = (np.arange(SEQ) // grid).astype(np.float32)[:, None] * inv2
    c = (np.arange(SEQ) % grid).astype(np.float32)[:, None] * inv2
    ang2 = np.concatenate([r, r, c, c], axis=1).astype(np.float64)
    sign = np.tile(np.repeat([-1.0, 1.0], 8), 2)
    sel_col = np.zeros((P, 2), np.float32)
    sel_col[0:2, 0] = sel_col[2:4, 1] = 1.0
    sel_row = np.zeros((P, 2, P), np.float32)
    sel_row[0:2, 0] = sel_row[2:4, 1] = sel_row[4] = 1.0
    return mask, np.concatenate([ident, token_rows(np.cos(ang1)), token_rows(np.sin(ang1)), token_rows(np.cos(ang2)),
                           token_rows(np.sin(ang2) * sign), sel_col, sel_row.reshape(P, 2 * P)], axis=1)


def _pool_matrices():
    s, t = np.arange(SEQ)[:, None], np.arange(SEQ)[None, :]
    out = np.zeros((P, len(POOL_WINDOWS), 3, P), np.float32)
    for g, w in enumerate(POOL_WINDOWS):
        m = ((s <= t) & (t - s < w)) / np.minimum(t + 1, w) - (s == t)
        for j, (a, b) in enumerate(((0, 0), (0, 1), (1, 1))):
            out[:, g, j] = m[a * P:(a + 1) * P, b * P:(b + 1) * P]
    return out


def kernel(**inputs):
    import concourse.bacc as bacc
    from concourse.bass_utils import run_bass_kernel_spmd

    v = {name: np.asarray(value) for name, value in inputs.items()}

    def columns(vec):
        return vec.reshape(-1, P).T

    mod_w, mod_b = v["mod_w_2"], v["mod_b_2"]
    kinds = (0, 1, 3, 4)
    mod_cols = [_rows_first(mod_w[l][:, k * D + h * COLS:k * D + (h + 1) * COLS], KT) for l in range(2) for k in kinds for h in range(2)]
    gates = [(l, k) for l in range(2) for k in (2, 5)]
    mod_gates = [[_rows_first(mod_w[l][:, k * D + h * COLS:k * D + (h + 1) * COLS], KT) for h in range(2)] for l, k in gates]
    w_in = v["w_in"][0]
    mlp = []
    up, down = _blocks(v["w_up"][0]), v["w_down"][0]
    for i in range(4):
        d = down[i * D:(i + 1) * D]
        mlp += [up[2 * i], mod_cols[4 + 2 * i], up[2 * i + 1], mod_cols[5 + 2 * i], _rows_first(d[:, 0:COLS], KT), _rows_first(d[:, COLS:D], KT)]
    conv = v["conv_w_in_2"][0].reshape(D, 3, KT, P)
    ffn = []
    for l in range(2):
        wg, wu, wd = v["ffn_w_gate_2"][l], v["ffn_w_up_2"][l], v["ffn_w_down_2"][l]
        gu = [_rows_first(np.concatenate([wg[:, j:j + 256], wu[:, j:j + 256]], axis=1), KT) for j in range(0, FH, 256)]
        dn = [_down(wd[i * COLS:(i + 1) * COLS]) for i in range(6)]
        seq = []
        for i in range(5):
            if l == 0:
                seq += [gu[2 * i]] + ([mod_cols[12 + i]] if i < 4 else []) + [gu[2 * i + 1], dn[i]]
            else:
                seq += [gu[2 * i], gu[2 * i + 1]] + ([dn[i - 1]] if i else [])
        ffn.append((seq + [gu[10]] + ([dn[4]] if l else []), [dn[5]]))
    mla_in = v["mla_w_in_2"][0]
    q_up, kv_up = v["mla_w_q_up_2"][0], v["mla_w_kv_up_2"][0]
    mla_up = [np.concatenate([_rows_first(q_up[:, g * GH * QK:(g + 1) * GH * QK], QKT), _rows_first(kv_up[:, g * COLS:(g + 1) * COLS], KVT)], axis=1)
              for g in range(MH // GH)]
    stream = {
        "w_in": _blocks(w_in[:, 0:K0]), "w_kv": [_rows_first(w_in[:, K0:G0], KT)],
        "w_gates": _blocks(w_in[:, G0:]), "w_branch": [_down(v["w_branch_pool"][0]), mod_cols[0], _down(v["w_branch_attn"][0]), mod_cols[1]],
        "w_out": _blocks(v["w_out"][0]), "mod_scale": mod_cols[2:4], "mlp": mlp, "mod_gate0": mod_gates[0],
        "conv_in": [_rows_first(conv[:, :, f, :].reshape(D, 3 * P), KT) for f in range(KT)], "conv_out": _blocks(v["conv_w_out_2"][0]),
        "mod_gate1": mod_gates[1], "ffn0": ffn[0][0], "ffn0_half": ffn[0][1], "mod_gate2": mod_gates[2],
        "mla_in": _blocks(mla_in[:, 0:QL + KVL]), "mod_gate3": mod_gates[3], "mla_up": mla_up, "mla_out": _blocks(v["mla_w_out_2"][0]),
        "ffn1": ffn[1][0], "ffn1_half": ffn[1][1],
    }
    arrays = {}
    for name, n, width in SECTIONS:
        arrays[name] = np.stack(stream[name])
        assert arrays[name].shape == (n, P, width), (name, arrays[name].shape)
    arrays["x"] = v["x"][0]
    arrays["ctx"] = v["ctx_2"][0]
    arrays["cols"] = np.concatenate(
        [columns(v[k]) for k in ("g_mix_pre", "g_mlp_pre", "pool_scale", "norm_mix_g_2", "norm_ffn_g_2", "mla_q_norm_g_2", "mla_kv_norm_g_2")]
        + [columns(v["conv_k_2"][0, j]) for j in range(3)] + [columns(v["conv_b_2"])]
        + [np.stack([columns(v["c_2"]), columns(v["c_ctx_2"])], axis=2).reshape(P, 2 * KT)]
        + [columns(mod_b[l, k * D:(k + 1) * D]) for l in range(2) for k in kinds], axis=1)
    arrays["rows"] = np.concatenate([v[k].reshape(-1) for k in (
        "attn_sinks", "mla_qn_nope_g_2", "mla_qn_rope_g_2", "mla_kn_nope_g_2", "mla_kn_rope_g_2")])
    arrays["mask"], arrays["tab"] = _tables()
    arrays["pool_m"] = _pool_matrices()
    arrays["w_pool"] = v["w_pool"][0]
    arrays["b_in"] = v["b_in"][0]
    arrays["g_mix_post"] = v["g_mix_post"][0]
    arrays["g_mlp_post"] = v["g_mlp_post"][0]
    arrays["mod_gate_b"] = np.concatenate([mod_b[l, k * D:(k + 1) * D].reshape(2, COLS) for l, k in gates])
    arrays["w_pe"] = mla_in[:, QL + KVL:].reshape(KT, P, ROPE).transpose(1, 0, 2)

    f32 = mybir.dt.float32
    nc = bacc.Bacc("TRN2", target_bir_lowering=False, num_devices=1)
    feeds, args = {}, {}
    for name, value in arrays.items():
        feeds["in_" + name] = np.ascontiguousarray(value)
        args[name] = nc.dram_tensor("in_" + name, value.shape, f32, kind="ExternalInput").ap()
    out = nc.dram_tensor("out_x", (SEQ, D), f32, kind="ExternalOutput").ap()
    build(nc, args, out)
    result = run_bass_kernel_spmd(nc, [feeds], core_ids=[0])
    return result.results[0]["out_x"].reshape(1, SEQ, D)
```

```python
import contextlib
from collections import Counter

import concourse.bass as bass
import numpy as np
from concourse import mybir

P = 128
D = 1024
KT = D // P
SEQ = 256
NT = SEQ // P
CHUNK = 4096
COLS = 512
EPS = 1e-6

POOL_WINDOWS = (2, 4, 8, 16)
POOL = 512
HEADS = 8
HD = 64
KVH = 2
IN_W = 3328
Q0, K0, V0, G0 = POOL, POOL + HEADS * HD, POOL + HEADS * HD + KVH * HD, POOL + HEADS * HD + 2 * KVH * HD
ROT = 16

FH = 2816
MH = 16
GH = 4
NOPE, ROPE, VD = 64, 32, 64
QK = NOPE + ROPE
QL, KVL = 768, 256
QKT, KVT = QL // P, KVL // P
KEYS = 2 * SEQ

SECTIONS = (
    ("w_in", 2, 4096), ("w_kv", 1, 2048), ("w_gates", 4, 4096), ("w_branch", 4, 4096), ("w_out", 2, 4096), ("mod_scale", 2, 4096),
    ("mlp", 24, 4096), ("mod_gate0", 2, 4096), ("conv_in", 8, 3072), ("conv_out", 2, 4096),
    ("mod_gate1", 2, 4096), ("ffn0_first", 1, 4096), ("ffn0_half", 1, 2048), ("ffn0", 19, 4096),
    ("mod_gate2", 2, 4096), ("mla_in", 2, 4096), ("mod_gate3", 1, 4096), ("mla_q", 4, 2304), ("mla_kv", 4, 1024),
    ("mod_gate3_half", 1, 4096), ("mla_out", 2, 4096),
    ("ffn1", 16, 4096), ("ffn1_half", 1, 2048),
)
STREAM = sum(n for _, n, _ in SECTIONS)
X_UPDATES = 16

COL_NAMES = (("g_mix", KT), ("g_mlp", KT), ("pool_scale", 4), ("norm_mix", 2 * KT), ("norm_ffn", 2 * KT),
             ("q_norm", QKT), ("kv_norm", KVT), ("conv_k0", KT), ("conv_k1", KT), ("conv_k2", KT), ("conv_b", KT),
             ("cond", 2 * KT), ("mod_b", 64))
COL, _at = {}, 0
for _name, _n in COL_NAMES:
    COL[_name] = _at
    _at += _n
NCOL = _at

ROW_NAMES = (("sinks", HEADS), ("qn_nope", NOPE), ("qn_rope", ROPE), ("kn_nope", NOPE), ("kn_rope", ROPE))
ROW, _at = {}, 0
for _name, _n in ROW_NAMES:
    ROW[_name] = _at
    _at += _n
NROW = _at

TAB_NAMES = (("ident", P), ("cos1", NT * 8), ("sin1", NT * 8), ("cosm", NT * ROPE), ("sinm", NT * ROPE),
             ("sel_col", 2), ("sel_row", 2 * P))
TAB, _at = {}, 0
for _name, _n in TAB_NAMES:
    TAB[_name] = _at
    _at += _n
NTAB = _at


class Count:

    def __init__(self):
        self.n, self.turn, self.per = Counter(), None, {}

    def at(self, name, back=0):
        value = self.n[name] - back
        assert value >= 0, name
        if self.turn is not None and self.per.get(name):
            assert value > 0, name
            return self.turn * self.per[name] + value
        return value

    def step(self, name, k=1):
        self.n[name] += k
        return self.at(name)

    @contextlib.contextmanager
    def loop(self, eng, turns, **per):
        start = Counter(self.n)
        with eng.Fori(0, turns) as i:
            self.turn, self.per = i, per
            yield i
        for name in set(self.n) | set(per):
            assert self.n[name] - start[name] == per.get(name, 0), (name, self.n[name] - start[name], per)
            self.n[name] = start[name] + turns * per.get(name, 0)
        self.turn, self.per = None, {}


def build(nc, a, out):
    f32, f32r = mybir.dt.float32, mybir.dt.float32r
    ACT, ALU, AX = mybir.ActivationFunctionType, mybir.AluOpType, mybir.AxisListType

    base = -(-nc.sbuf_base // 64) * 64

    def at(name, shape, offset, dtype=f32):
        return nc.alloc_sbuf_tensor_at(name, shape, dtype, offset=base + offset)

    K = 1024
    raw = at("raw", [P, 2, CHUNK], 0)
    w_hi = at("w_hi", [P, 2, CHUNK], 32 * K, f32r)
    w_lo = at("w_lo", [P, 2, CHUNK], 64 * K, f32r)
    x = at("x", [P, NT, D], 96 * K)
    ACT0 = 104 * K
    act_hi = at("act_hi", [P, 2, KT, SEQ], ACT0, f32r)
    act_lo = at("act_lo", [P, 2, KT, SEQ], ACT0 + 16 * K, f32r)
    XN0 = 136 * K
    xn = at("xn", [P, 2, D], XN0)
    scaled = at("scaled", [P, 2, COLS], XN0 + 8 * K)
    junk = at("junk", [P, D], ACT0 + 8 * K)
    M0 = XN0 + 12 * K
    cols = at("cols", [P, NCOL], M0)
    ROWS0 = M0 + -(-4 * NCOL // 32) * 32
    rows = at("rows", [P, NROW], ROWS0)
    TAB0 = ROWS0 + -(-4 * NROW // 32) * 32
    tab = at("tab", [P, NTAB], TAB0)
    M1 = TAB0 + -(-4 * NTAB // 32) * 32
    cond_w = at("cond_w", [P, KT, P], M1, f32r)
    cond_s = at("cond_s", [P, 2 * KT], M1 + 4 * K)
    mod_row = at("mod_row", [5, COLS], M1 + 4 * K + 64)
    mod_col = at("mod_col", [P, 64, 2], M1 + 6 * K + 64)
    stat = at("stat", [P, 160], M1 + 6 * K + 64 + 512)
    coef = at("coef", [P, 4, KT, 2], M1 + 6 * K + 64 + 512 + 640)
    PH = M1 + 6 * K + 64 + 512 + 640 + 256
    END = nc.sbuf_usable_end - base
    assert PH + 48 * K <= END, (PH, END)

    proj = at("proj", [P, NT, IN_W], PH)
    w_pool = at("w_pool", [P, 4, P], PH + 26 * K)
    diff = at("diff", [P, 4, SEQ], PH + 28 * K)
    qT = at("qT", [HD, HEADS, SEQ], PH + 32 * K)
    g_post1 = at("g_post1", [P, D], PH + 32 * K)
    kT = at("kT", [HD, KVH, SEQ], PH + 40 * K)
    pT = at("pT", [P, 2, 4, P], PH + 42 * K)
    mask = at("mask", [P, 2 * P], PH + 46 * K)
    ypool_hi = at("ypool_hi", [P, 4, SEQ], ACT0 + 8 * K, f32r)
    ypool_lo = at("ypool_lo", [P, 4, SEQ], ACT0 + 12 * K, f32r)
    yattn_hi = at("yattn_hi", [P, 4, SEQ], ACT0 + 24 * K, f32r)
    yattn_lo = at("yattn_lo", [P, 4, SEQ], ACT0 + 28 * K, f32r)
    pool_m = at("pool_m", [P, 4, 3, P], ACT0 + 24 * K)
    score = at("score", [P, 2, 2, 2 * P], XN0)
    prob = at("prob", [P, 4, 2, 2 * P], XN0 + 4 * K)
    rope_t = at("rope_t", [P, 4, NT, 10, 8], XN0)
    ctx = at("ctx", [P, NT, D], PH)
    h1_hi = at("h1_hi", [P, 8, SEQ], PH + 8 * K, f32r)
    h1_lo = at("h1_lo", [P, 8, SEQ], PH + 16 * K, f32r)
    mlp = at("mlp", [P, NT, D], PH + 24 * K)
    h1 = at("h1", [P, 2, NT, COLS], PH + 32 * K)
    g_post2 = at("g_post2", [P, D], PH + 40 * K)
    gate = at("gate", [P, 2, D], PH + 8 * K)
    conv_hi = at("conv_hi", [P, KT, 2, SEQ], PH + 16 * K, f32r)
    conv_lo = at("conv_lo", [P, KT, 2, SEQ], PH + 32 * K, f32r)
    c_sb = at("c_sb", [P, 2, SEQ], XN0)
    z_pad = at("z_pad", [P, 2, SEQ + 2], XN0 + 2 * K)
    conv_y = at("conv_y", [P, 2, SEQ], XN0 + 4 * K + 64)
    conv_m = at("conv_m", [P, 2, 2, SEQ], XN0 + 6 * K + 64)
    h2_hi = at("h2_hi", [P, 4, 2, SEQ], PH + 16 * K, f32r)
    h2_lo = at("h2_lo", [P, 4, 2, SEQ], PH + 24 * K, f32r)
    silu = at("silu", [P, 2, COLS], PH + 32 * K)
    h2 = at("h2", [P, 2, COLS], PH + 36 * K)
    gated = at("gated", [P, 2, COLS], XN0 + 8 * K)
    ql_hi = at("ql_hi", [P, QKT, SEQ], PH + 16 * K, f32r)
    ql_lo = at("ql_lo", [P, QKT, SEQ], PH + 22 * K, f32r)
    kvl_hi = at("kvl_hi", [P, KVT, KEYS], PH + 28 * K, f32r)
    kvl_lo = at("kvl_lo", [P, KVT, KEYS], PH + 32 * K, f32r)
    q_nat = at("q_nat", [P, NT, QL], PH + 36 * K)
    kv_nat = at("kv_nat", [P, 2 * NT, KVL], PH + 42 * K)
    pe = at("pe", [P, 2 * NT, ROPE], PH + 46 * K)
    pe_t = at("pe_t", [P, 2 * NT, ROPE], PH + 46 * K + 512)
    w_pe = at("w_pe", [P, KT, ROPE], PH)
    w_pe_hi = at("w_pe_hi", [P, KT, ROPE], PH + 1 * K, f32r)
    w_pe_lo = at("w_pe_lo", [P, KT, ROPE], PH + 2 * K, f32r)
    o_nat = at("o_nat", [P, NT, D], PH)
    qg = at("qg", [P, NT, GH, QK], PH + 36 * K)
    sq = at("sq", [P, 2 * NT * GH * NOPE], PH + 39 * K)
    qr_t = at("qr_t", [P, NT, GH, ROPE], PH + 43 * K)
    kg = at("kg", [P, 2 * NT, GH, QK], ACT0)
    vg = at("vg", [P, 2 * NT, GH, VD], ACT0 + 6 * K)
    v_next = at("v_next", [P, 2 * NT, GH, VD], ACT0 + 22 * K)
    qgT = at("qgT", [QK, GH, SEQ], ACT0 + 10 * K)
    kgT = at("kgT", [QK, GH, KEYS], ACT0 + 14 * K)
    pr = at("pr", [P, 2, KEYS], XN0)
    prT = at("prT", [P, 2, 4, P], XN0 + 4 * K)
    h3_hi = at("h3_hi", [P, 2, 4, SEQ], PH + 16 * K, f32r)
    h3_lo = at("h3_lo", [P, 2, 4, SEQ], PH + 24 * K, f32r)
    silu3 = at("silu3", [P, 2, 256], PH + 32 * K)
    h3 = at("h3", [P, 2, NT, 256], PH + 34 * K)

    def res(tt):
        return x[:, tt, :] if tt < NT else ctx[:, tt - NT, :]

    def col(name, j, n=1):
        return cols[:, COL[name] + j:COL[name] + j + n]

    def row(name, n):
        return rows[:, ROW[name]:ROW[name] + n]

    def table(name, n, parts=P, j=0):
        return tab[0:parts, TAB[name] + j:TAB[name] + j + n]

    ident = table("ident", P)

    SS, RT, RS = 0, 16, 32
    NM, LS, ES, RD = 48, 64, 80, 96
    MX, NSINK, EPSC = 112, 120, 128
    GQ = 0

    bank = [nc.alloc_psum_tensor(f"bank{i}", [P, COLS], f32) for i in range(4)]
    turned = [nc.alloc_psum_tensor(f"turned{i}", [P, COLS], f32) for i in range(2)]
    mod_ps = nc.alloc_psum_tensor("mod_ps", [P, COLS], f32)
    small = nc.alloc_psum_tensor("small", [P, COLS], f32)

    S = nc.alloc_semaphore
    loaded = [S("loaded0"), S("loaded1")]
    hi_ready = S("hi_ready")
    lo_ready = S("lo_ready")
    lo_ready_pool = S("lo_ready_pool")
    const_loaded = S("const_loaded")
    x_loaded = [S("x_loaded0"), S("x_loaded1")]
    bias_loaded = S("bias_loaded")
    ctx_loaded = S("ctx_loaded")
    post1_loaded = S("post1_loaded")
    post2_loaded = S("post2_loaded")
    pe_loaded = S("pe_loaded")
    modbias_loaded = S("modbias_loaded")
    out_done = S("out_done")
    gemm_done = S("gemm_done")
    gemm_read = S("gemm_read")
    tr_done = S("tr_done")
    tr_read = S("tr_read")
    tr_hi = S("tr_hi")
    mod_done = S("mod_done")
    mod_row_ready = S("mod_row_ready")
    small_done = S("small_done")
    small_read = S("small_read")
    cond_silu = S("cond_silu")
    cond_hi = S("cond_hi")
    cond_zero = S("cond_zero")
    cond_ready = S("cond_ready")
    ss_done = S("ss_done")
    root_ready = S("root_ready")
    rstd_ready = S("rstd_ready")
    xn_ready = S("xn_ready")
    norm_hi = S("norm_hi")
    norm_ready = S("norm_ready")
    x_ready = S("x_ready")
    dve_chain = S("dve_chain")
    gates_ready = S("gates_ready")
    rope_ready = S("rope_ready")
    negmax_ready = S("negmax_ready")
    probs_ready = S("probs_ready")
    scores_done = S("scores_done")
    pv_done = S("pv_done")
    sink_in = S("sink_in")
    sink_exp = S("sink_exp")
    pool_hi = S("pool_hi")
    pool_lo = S("pool_lo")
    merged_ready = S("merged_ready")
    h_ready = S("h_ready")
    hidden_ready = S("hidden_ready")
    silu_ready = S("silu_ready")
    h_hi = S("h_hi")
    h_lo = S("h_lo")
    wpe_hi = S("wpe_hi")
    wpe_lo = S("wpe_lo")
    pe_root = S("pe_root")
    pe_sum = S("pe_sum")
    sq_ready = S("sq_ready")
    gsum_ready = S("gsum_ready")
    groot_ready = S("groot_ready")
    qk_ready = S("qk_ready")
    v_ready = S("v_ready")

    WQ, WKV = QKT * GH * QK, KVT * COLS

    def halves_of(width):
        half = width // 2
        return [(h * half, h * half + half * 11 // 16, (h + 1) * half) for h in range(2)]

    with nc.Block() as block:

        @block.sync
        def _(sp):
            n = Count()

            def load(section, k, width):
                c = n.step("chunk")
                slot = (n.n["chunk"] - 1) % 2
                if n.n["chunk"] > 2:
                    sp.wait_ge(lo_ready, 2 * n.at("chunk", 2))
                    sp.wait_ge(lo_ready_pool, 2 * n.at("chunk", 2))
                src = a[section][k] if isinstance(k, int) else a[section][bass.ds(k, 1)].rearrange("o p n -> (o p) n")
                sp.dma_start(raw[:, slot, 0:width], src).then_inc(loaded[slot], 16)

            for t in range(NT):
                sp.dma_start(x[:, t, :], a["x"][t * P:(t + 1) * P, :]).then_inc(x_loaded[t], 16)
            sp.dma_start(tab[:, :], a["tab"]).then_inc(const_loaded, 16)
            sp.dma_start(cols[:, :], a["cols"]).then_inc(const_loaded, 16)
            sp.dma_start(rows[:, :], a["rows"].rearrange("(o n) -> o n", o=1).to_broadcast([P, NROW])).then_inc(const_loaded, 16)
            for section, chunks, width in SECTIONS:
                first = 0
                if section == "mla_kv":
                    continue
                if section == "mla_q":
                    with n.loop(sp, chunks, chunk=2) as i:
                        load("mla_q", i, WQ)
                        load("mla_kv", i, WKV)
                    continue
                while first < chunks and (chunks < 8 or n.n["chunk"] < 2):
                    load(section, first, width)
                    first += 1
                turns = (chunks - first) // 2
                if turns:
                    with n.loop(sp, turns, chunk=2) as i:
                        load(section, i * 2 + first, width)
                        load(section, i * 2 + first + 1, width)
                if (chunks - first) % 2:
                    load(section, chunks - 1, width)
            for t in range(NT):
                sp.wait_ge(x_ready, X_UPDATES - NT + 1 + t)
                sp.dma_start(out[t * P:(t + 1) * P, :], x[:, t, :]).then_inc(out_done, 16)
            sp.wait_ge(out_done, 16 * NT)

        @block.gpsimd
        def _(pool):
            n = Count()

            def split(width=CHUNK):
                n.step("chunk")
                s = (n.n["chunk"] - 1) % 2
                for _, share, end in halves_of(width):
                    part = slice(share, end)
                    pool.wait_ge(hi_ready, n.step("half"))
                    pool.tensor_tensor(w_lo[:, s, part], raw[:, s, part], w_hi[:, s, part].bitcast(f32),
                                       ALU.subtract).then_inc(lo_ready_pool, 1)

            def splits(chunks):
                with n.loop(pool, chunks // 2, chunk=2, half=4):
                    split()
                    split()
                if chunks % 2:
                    split()

            names = [name for name, _, _ in SECTIONS]
            before = sum(c for _, c, _ in SECTIONS[:names.index("mla_q")])
            groups = MH // GH
            splits(before)
            with n.loop(pool, groups, chunk=2, half=4):
                split(WQ)
                split(WKV)
            splits(STREAM - before - 2 * groups)

        @block.tensor
        def _(te):
            n = Count()

            def chunk():
                n.step("chunk")
                split_half(1)
                return (n.n["chunk"] - 1) % 2

            def split_half(back):
                te.wait_ge(lo_ready, 2 * n.at("chunk") - back)
                te.wait_ge(lo_ready_pool, 2 * n.at("chunk") - back)

            def weights(s, j0, j1):
                return w_hi[:, s, j0:j1], w_lo[:, s, j0:j1]

            rot = {"first": 0, "banks": 4}

            def rotation(banks):
                if n.n["unit"]:
                    te.wait_ge(gemm_read, n.at("unit"))
                rot["first"], rot["banks"] = n.n["unit"], banks

            def unit():
                n.step("unit")
                if n.n["unit"] > rot["banks"]:
                    te.wait_ge(gemm_read, n.at("unit", rot["banks"]))
                return bank[(n.n["unit"] - 1 - rot["first"]) % rot["banks"]]

            def product(dst, terms, second=None, also=None, before_last=None):
                for j, ((sh, sl), (mh, ml)) in enumerate(terms):
                    if before_last and j == len(terms) - 1:
                        before_last()
                    if j == second:
                        split_half(0)
                        if also:
                            also()
                    te.matmul(dst, sh, mh, start=(j == 0), stop=False)
                    te.matmul(dst, sh, ml, start=False, stop=False)
                    last = te.matmul(dst, sl, mh, start=False, stop=(j == len(terms) - 1))
                return last

            def act_rows(tt, k):
                t = slice((tt % NT) * P, (tt % NT + 1) * P)
                return act_hi[:, tt // NT, k, t], act_lo[:, tt // NT, k, t]

            def turn(pieces):
                n.step("tr")
                if n.n["tr"] > 2:
                    te.wait_ge(tr_read, n.at("tr", 2))
                dst = turned[(n.n["tr"] - 1) % 2]
                for j, src in enumerate(pieces):
                    m = src.shape[-1]
                    last = te.transpose(dst[0:m, j * P:(j + 1) * P], src, ident)
                last.then_inc(tr_done, 1)

            def turn_rows(buf):
                te.wait_ge(xn_ready, n.step("xn"))
                for half in range(2):
                    turn([xn[:, buf, (4 * half + j) * P:(4 * half + j + 1) * P] for j in range(4)])

            def mod_product():
                s = chunk()
                m = n.step("mod")
                if n.n["mod"] > 1:
                    te.wait_ge(mod_row_ready, n.at("mod", 1))
                for k in range(KT):
                    if k == KT // 2:
                        split_half(0)
                    h, l = weights(s, k * COLS, (k + 1) * COLS)
                    te.matmul(mod_ps[:, :], cond_w[:, k, :], h, start=(k == 0), stop=False)
                    last = te.matmul(mod_ps[:, :], cond_w[:, k, :], l, start=False, stop=(k == KT - 1))
                last.then_inc(mod_done, 1)

            def small_bank():
                n.step("small")
                if n.n["small"] > 1:
                    te.wait_ge(small_read, n.at("small", 1))

            def mod_columns():
                te.wait_ge(mod_row_ready, n.at("mod"))
                small_bank()
                for j in range(4):
                    last = te.matmul(small[:, 2 * j:2 * j + 2], mod_row[0:4, j * P:(j + 1) * P], table("sel_col", 2, 4),
                                     start=True, stop=True)
                last.then_inc(small_done, 1)

            def gate_rows(s, back=0):
                if s == 0:
                    te.wait_ge(mod_row_ready, n.at("mod", back))
                    te.wait_ge(modbias_loaded, 16 * n.step("gate"))
                small_bank()
                te.matmul(small[:, :], table("sel_row", P, 5, s * P), mod_row[0:5, :], start=True, stop=True).then_inc(small_done, 1)

            def mod_gate(seqs):
                for s in range(seqs):
                    gate_rows(s)

            te.wait_ge(const_loaded, 16 * 3)
            turn_rows(0)
            turn_rows(1)
            for k, width in enumerate((COLS, COLS, 256)):
                s = chunk()
                for t in range(NT):
                    if k == 0:
                        te.wait_ge(norm_ready, n.step("norm", 2))
                    b = unit()
                    product(b[:, 0:width], [(act_rows(t, k), weights(s, k * width, (k + 1) * width)) for k in range(KT)],
                            second=0 if width < COLS else 4 if t == 0 else None).then_inc(gemm_done, 1)
            te.wait_ge(gemm_read, n.at("unit"))
            for pair in range(2):
                b = unit()
                for g in (2 * pair, 2 * pair + 1):
                    d0, c0 = (g % 2) * SEQ, g * P
                    te.matmul(b[:, d0:d0 + P], proj[:, 0, c0:c0 + P], pool_m[:, g, 0, :], start=True, stop=True)
                    te.matmul(b[:, d0 + P:d0 + 2 * P], proj[:, 0, c0:c0 + P], pool_m[:, g, 1, :], start=True, stop=False)
                    last = te.matmul(b[:, d0 + P:d0 + 2 * P], proj[:, 1, c0:c0 + P], pool_m[:, g, 2, :], start=False, stop=True)
                last.then_inc(gemm_done, 1)

            def rows_chunk():
                s = chunk()
                for t in range(NT):
                    b = unit()
                    product(b[:, :], [(act_rows(t, k), weights(s, k * COLS, (k + 1) * COLS)) for k in range(KT)],
                            second=4 if t == 0 else None).then_inc(gemm_done, 1)

            rows_chunk()
            te.wait_ge(rope_ready, 1)
            for t in range(NT):
                for half in range(2):
                    turn([proj[:, t, Q0 + h * HD:Q0 + (h + 1) * HD] for h in range(4 * half, 4 * half + 4)])
            turn([proj[:, t, K0 + j * HD:K0 + (j + 1) * HD] for j in range(KVH) for t in range(NT)])
            rows_chunk()

            def scores(u):
                t, p = u // 4, u % 4
                nk = (t + 1) * P
                b = unit()
                for e in range(2):
                    last = te.matmul(b[:, e * nk:(e + 1) * nk], qT[:, 2 * p + e, t * P:(t + 1) * P], kT[:, p // 2, 0:nk],
                                     start=True, stop=True)
                last.then_inc(gemm_done, 1)

            def turn_probs(u):
                te.wait_ge(probs_ready, u + 1)
                turn([prob[:, u % 4, e, j * P:(j + 1) * P] for e in range(2) for j in range(u // 4 + 1)])

            def values(u, tr):
                t, p = u // 4, u % 4
                if p == 0:
                    small_bank()
                te.wait_ge(tr_read, tr)
                for e in range(2):
                    for j in range(t + 1):
                        last = te.matmul(small[:, (2 * p + e) * HD:(2 * p + e + 1) * HD], pT[:, u % 2, e * (t + 1) + j, :],
                                         proj[:, j, V0 + (p // 2) * HD:V0 + (p // 2 + 1) * HD], start=(j == 0), stop=(j == t))
                last.then_inc(pv_done, 1)

            def attend(first):
                trs = []
                for u in range(first, first + 4):
                    turn_probs(u)
                    trs.append(n.n["tr"])
                    if u > first:
                        values(u - 1, trs[-2])
                values(first + 3, trs[-1])

            te.wait_ge(tr_read, n.at("tr"))
            for u in range(2):
                scores(u)
            for pair in range(2):
                b = unit()
                for g in (2 * pair, 2 * pair + 1):
                    last = te.matmul(b[:, (g % 2) * SEQ:(g % 2 + 1) * SEQ], w_pool[:, g, :], diff[:, g, :], start=True, stop=True)
                last.then_inc(gemm_done, 1)
            for u in range(2, 4):
                scores(u)
            rows_chunk()
            attend(0)
            for u in range(4, 8):
                scores(u)
            rows_chunk()
            attend(4)

            def branch(hi, lo):
                s = chunk()
                for cb in range(2):
                    for t in range(NT):
                        b = unit()
                        product(b[:, :], [((hi[:, k, t * P:(t + 1) * P], lo[:, k, t * P:(t + 1) * P]),
                                           weights(s, (4 * cb + k) * COLS, (4 * cb + k + 1) * COLS)) for k in range(4)],
                                second=0 if cb == 1 and t == 0 else None).then_inc(gemm_done, 1)

            te.wait_ge(pool_lo, 2)
            branch(ypool_hi, ypool_lo)
            te.wait_ge(small_read, n.at("small"))
            for t in range(NT):
                turn([proj[:, t, j * P:(j + 1) * P] for j in range(4)])
            te.wait_ge(cond_ready, 1)
            mod_product()
            te.wait_ge(tr_read, n.at("tr"))
            branch(yattn_hi, yattn_lo)
            mod_columns()
            for half in range(2):
                for t in range(NT):
                    te.wait_ge(merged_ready, 2 * half + t + 1)
                    turn([proj[:, t, G0 + (4 * half + j) * P:G0 + (4 * half + j + 1) * P] for j in range(4)])
            mod_product()
            te.wait_ge(tr_read, n.at("tr"))
            rows_chunk()
            mod_columns()
            rows_chunk()
            mod_product()
            turn_rows(0)
            mod_columns()
            turn_rows(1)
            mod_product()

            def up(first=False):
                s = chunk()
                if first:
                    te.wait_ge(norm_ready, n.step("norm", 4))
                for pair in range(2):
                    b = unit()
                    for f in (2 * pair, 2 * pair + 1):
                        last = product(b[:, (f % 2) * SEQ:(f % 2 + 1) * SEQ],
                                       [(weights(s, j * COLS + f * P, j * COLS + (f + 1) * P), (act_hi[:, 0, j, :], act_lo[:, 0, j, :]))
                                        for j in range(KT)], second=4 if f == 0 else None)
                    last.then_inc(gemm_done, 1)
                    if first and pair == 0:
                        mod_columns()
                n.step("hidden", 2)

            def down():
                s = chunk()
                for t in range(NT):
                    b = unit()
                    product(b[:, :], [((h1_hi[:, j, t * P:(t + 1) * P], h1_lo[:, j, t * P:(t + 1) * P]),
                                       weights(s, j * COLS, (j + 1) * COLS)) for j in range(8)],
                            second=4 if t == 0 else None, also=hidden_split).then_inc(gemm_done, 1)

            def hidden_split():
                te.wait_ge(hidden_ready, n.at("hidden"))

            def mlp_turn(first=False):
                up(first)
                mod_product()
                up()
                mod_columns()
                mod_product()
                te.wait_ge(hidden_ready, n.at("hidden", 2))
                down()
                mod_columns()
                if first:
                    turn_rows(0)
                down()
                if first:
                    turn_rows(1)

            mlp_turn(first=True)
            with n.loop(te, 3, chunk=6, unit=8, mod=2, small=2, hidden=4):
                mlp_turn()
            mod_product()
            mod_product()

            def moving(k):
                return act_hi[:, :, k, :], act_lo[:, :, k, :]

            def conv_weights(s, part):
                return [weights(s, k * 384 + part * P, k * 384 + (part + 1) * P) for k in range(KT)]

            def conv_in():
                s = chunk()
                for part in (1, 2, 0):
                    b = unit()
                    product(b[:, :].rearrange("p (s t) -> p s t", s=2), [(w, moving(k)) for k, w in enumerate(conv_weights(s, part))],
                            second=5 if part == 1 else None).then_inc(gemm_done, 1)

            rotation(3)
            te.wait_ge(norm_ready, n.step("norm", 4))
            s = chunk()
            for j, part in enumerate((1, 2, 0)):
                b = unit()
                product(b[:, SEQ:2 * SEQ], [(w, (act_hi[:, 1, k, :], act_lo[:, 1, k, :])) for k, w in enumerate(conv_weights(s, part))],
                        second=5 if part == 1 else None)
                if j < 2:
                    turn_rows(j)
                    gate_rows(j, 1)
            te.wait_ge(norm_ready, n.step("norm", 4))
            for j, part in enumerate((1, 2, 0)):
                product(bank[j][:, 0:SEQ], [(w, (act_hi[:, 0, k, :], act_lo[:, 0, k, :])) for k, w in enumerate(conv_weights(s, part))]
                        ).then_inc(gemm_done, 1)
                if j < 2:
                    gate_rows(j)
            conv_in()
            with n.loop(te, 3, chunk=2, unit=6):
                conv_in()
                conv_in()
            rotation(4)

            def features(kts):
                n.step("h", kts)
                te.wait_ge(h_lo, n.at("h", 1))

            def last_feature():
                te.wait_ge(h_lo, n.at("h"))

            def conv_out(s, tt, first):
                b = unit()
                q, t = tt // NT, slice((tt % NT) * P, (tt % NT + 1) * P)
                product(b[:, :], [((conv_hi[:, k, q, t], conv_lo[:, k, q, t]), weights(s, k * COLS, (k + 1) * COLS))
                                  for k in range(KT)], second=4 if tt == 0 else None,
                        before_last=last_feature if first else None).then_inc(gemm_done, 1)

            def norm_both(rows_unit):
                for tt in range(2 * NT):
                    rows_unit(tt)
                    if 1 <= tt <= NT:
                        turn_rows(tt - 1)
                mod_product()
                mod_product()
                te.wait_ge(norm_ready, n.step("norm", 4))

            features(8)
            s = chunk()
            for tt in range(2 * NT):
                conv_out(s, tt, tt == 0)
            s = chunk()
            norm_both(lambda tt: conv_out(s, tt, False))

            def gate_up(apart=False):
                s = chunk()
                for f in range(2):
                    for part in range(2):
                        b = unit()
                        cols_of = [weights(s, k * COLS + part * 256 + f * P, k * COLS + part * 256 + (f + 1) * P) for k in range(KT)]
                        half = 4 if f == part == 0 else None
                        if apart:
                            product(b[:, 0:SEQ], [(cols_of[k], (act_hi[:, 0, k, :], act_lo[:, 0, k, :])) for k in range(KT)], second=half)
                            if f == 0:
                                turn_rows(part)
                                gate_rows(part, 1)
                            else:
                                gate_rows(part)
                        else:
                            product(b[:, :].rearrange("p (s t) -> p s t", s=2), [(cols_of[k], moving(k)) for k in range(KT)],
                                    second=half).then_inc(gemm_done, 1)
                if apart:
                    te.wait_ge(norm_ready, n.step("norm", 4))
                    for f in range(2):
                        for part in range(2):
                            cols_of = [weights(s, k * COLS + part * 256 + f * P, k * COLS + part * 256 + (f + 1) * P) for k in range(KT)]
                            product(bank[2 * f + part][:, SEQ:2 * SEQ], [(cols_of[k], (act_hi[:, 1, k, :], act_lo[:, 1, k, :])) for k in range(KT)]
                                    ).then_inc(gemm_done, 1)

            def down0(s, kts, cb, tt):
                b = unit()
                q, t = tt // NT, slice((tt % NT) * P, (tt % NT + 1) * P)
                product(b[:, :], [((h2_hi[:, k, q, t], h2_lo[:, k, q, t]),
                                   weights(s, (kts * cb + k) * COLS, (kts * cb + k + 1) * COLS)) for k in range(kts)],
                        second=0 if cb == 1 and tt == 0 else None,
                        before_last=last_feature if cb == tt == 0 else None).then_inc(gemm_done, 1)

            def down0_all(kts=4):
                features(kts)
                s = chunk()
                for cb in range(2):
                    for tt in range(2 * NT):
                        down0(s, kts, cb, tt)

            gate_up(apart=True)
            down0_all(2)
            with n.loop(te, 4, chunk=4, unit=16, mod=1, small=1, h=4):
                gate_up()
                mod_product()
                gate_up()
                mod_columns()
                down0_all()
            gate_up()
            gate_up()
            features(4)
            s = chunk()

            def down0_rows(tt):
                down0(s, 4, 0, tt)
                down0(s, 4, 1, tt)

            norm_both(down0_rows)
            s = chunk()
            for t in range(NT):
                b = unit()
                product(b[:, :], [(act_rows(t, k), weights(s, k * COLS, (k + 1) * COLS)) for k in range(KT)],
                        second=4 if t == 0 else None).then_inc(gemm_done, 1)
                turn_rows(t)
                if t == 0:
                    gate_rows(0, 1)
            s = chunk()
            for tt in range(2 * NT):
                b = unit()
                if tt == NT:
                    te.wait_ge(norm_ready, n.step("norm", 4))
                first = 0 if tt < NT else 256
                product(b[:, first:COLS], [(act_rows(tt, k), weights(s, k * COLS + first, (k + 1) * COLS)) for k in range(KT)],
                        second=4 if tt == 0 else None).then_inc(gemm_done, 1)
                if tt == 0:
                    gate_rows(0)
            b = unit()
            te.wait_ge(wpe_lo, 1)
            for tt in range(2 * NT):
                last = product(b[:, tt * ROPE:(tt + 1) * ROPE],
                               [(act_rows(tt, k), (w_pe_hi[:, k, :], w_pe_lo[:, k, :])) for k in range(KT)])
            last.then_inc(gemm_done, 1)
            for t in range(NT):
                te.wait_ge(xn_ready, n.step("xn"))
                turn([xn[:, t, j * P:(j + 1) * P] for j in range(4)])
                turn([xn[:, t, j * P:(j + 1) * P] for j in range(4, QKT)])
            mod_product()
            for q in range(2):
                te.wait_ge(xn_ready, n.step("xn", 2))
                turn([kv_nat[:, 2 * q + t, k * P:(k + 1) * P] for k in range(KVT) for t in range(NT)])
            te.wait_ge(norm_ready, n.step("norm", 4))
            te.wait_ge(gemm_read, n.at("unit"))
            held = {}

            def project(j):
                if j in (0, NT):
                    held["slot"] = chunk()
                s = held["slot"]
                n.step("unit")
                te.wait_ge(gemm_read, n.at("unit", 2))
                b = bank[2 + j % 2]
                if j < NT:
                    t = slice(j * P, (j + 1) * P)
                    last = product(b[:, 0:GH * QK], [((ql_hi[:, k, t], ql_lo[:, k, t]), weights(s, k * GH * QK, (k + 1) * GH * QK))
                                                     for k in range(QKT)], second=3 if j == 0 else None)
                else:
                    t = slice((j - NT) * P, (j - NT + 1) * P)
                    last = product(b[:, :], [((kvl_hi[:, k, t], kvl_lo[:, k, t]), weights(s, k * COLS, (k + 1) * COLS))
                                             for k in range(KVT)], second=1 if j == NT else None)
                last.then_inc(gemm_done, 1)

            def mla_scores(u):
                t, h = u // GH, u % GH
                te.matmul(bank[u % 2][:, :], qgT[:, h, t * P:(t + 1) * P], kgT[:, h, :], start=True, stop=True).then_inc(scores_done, 1)

            def mla_values(u, tr):
                h = u % GH
                te.wait_ge(tr_read, tr)
                for j in range(4):
                    last = te.matmul(small[:, u * VD:(u + 1) * VD], prT[:, u % 2, j, :], vg[:, j, h, :], start=(j == 0), stop=(j == 3))
                last.then_inc(pv_done, 1)

            def attend_group(following=True):
                for tt in range(2 * NT):
                    te.wait_ge(qk_ready, n.step("qk"))
                    turn([kg[:, tt, h, :] for h in range(GH)])
                te.wait_ge(qk_ready, n.step("qk"))
                for t in range(NT):
                    turn([qg[:, t, h, :] for h in range(GH)])
                te.wait_ge(tr_read, n.at("tr"))
                small_bank()
                for u in range(2):
                    mla_scores(u)
                trs = []
                for u in range(8):
                    if following and u < 6:
                        project(u)
                    te.wait_ge(probs_ready, 8 + n.step("probs"))
                    turn([pr[:, u % 2, j * P:(j + 1) * P] for j in range(4)])
                    trs.append(n.at("tr"))
                    if u + 2 < 8:
                        mla_scores(u + 2)
                    if u == 1:
                        te.wait_ge(v_ready, n.step("v"))
                    if u:
                        mla_values(u - 1, trs[u - 1])
                mla_values(7, trs[7])

            for j in range(6):
                project(j)
                if j == 0:
                    mod_gate(1)
                if j == 1:
                    te.wait_ge(norm_ready, n.step("norm", 2))
            with n.loop(te, 2, chunk=2, unit=6, tr=14, small=1, probs=8, qk=5, v=1):
                attend_group()
            attend_group()
            attend_group(following=False)
            te.wait_ge(small_read, n.at("small"))
            for half in range(2):
                for t in range(NT):
                    turn([o_nat[:, t, (4 * half + j) * P:(4 * half + j + 1) * P] for j in range(4)])
            mod_product()
            te.wait_ge(tr_read, n.at("tr"))
            rotation(4)
            rows_chunk()
            rows_chunk()
            turn_rows(0)
            mod_gate(1)
            turn_rows(1)

            te.wait_ge(norm_ready, n.step("norm", 4))

            def gate_up1():
                s = chunk()
                for f in range(2):
                    b = unit()
                    for part in range(2):
                        first = part * 256 + f * P
                        last = product(b[:, part * SEQ:(part + 1) * SEQ],
                                       [(weights(s, j * COLS + first, j * COLS + first + P), (act_hi[:, 0, j, :], act_lo[:, 0, j, :]))
                                        for j in range(KT)], second=4 if f == part == 0 else None)
                    last.then_inc(gemm_done, 1)
                n.step("hidden", 2)

            def down1(p, kts, since):
                te.wait_ge(hidden_ready, n.at("hidden", since))
                s = chunk()
                for t in range(NT):
                    for cb in range(2):
                        b = unit()
                        product(b[:, :], [((h3_hi[:, p, k, t * P:(t + 1) * P], h3_lo[:, p, k, t * P:(t + 1) * P]),
                                           weights(s, (kts * cb + k) * COLS, (kts * cb + k + 1) * COLS)) for k in range(kts)],
                                second=0 if cb == 1 and t == 0 else None).then_inc(gemm_done, 1)

            def group1(p):
                gate_up1()
                gate_up1()
                down1(1 - p, 4, 4)

            gate_up1()
            gate_up1()
            with n.loop(te, 2, chunk=6, unit=16, hidden=8):
                group1(1)
                group1(0)
            gate_up1()
            down1(0, 4, 2)
            down1(1, 2, 0)
            assert n.n["chunk"] == STREAM, (n.n["chunk"], STREAM)

        @block.scalar
        def _(act):
            n = Count()

            def split(width=CHUNK):
                n.step("split")
                c = n.n["split"]
                if c > STREAM:
                    return
                s = (c - 1) % 2
                turns = 16 * ((c + 1) // 2)
                if n.turn is not None:
                    turns = n.turn * (8 * n.per["split"]) + turns
                act.wait_ge(loaded[s], turns)
                if n.n["unit"]:
                    act.wait_ge(gemm_done, n.at("unit"))
                if n.n["mod"]:
                    act.wait_ge(mod_done, n.at("mod"))
                for first, _, end in halves_of(width):
                    part = slice(first, end)
                    act.activation(w_hi[:, s, part], raw[:, s, part], ACT.Copy).then_inc(hi_ready, 1)

            def roots(sources, width):
                for src, junk, k in sources:
                    if n.n["ss"]:
                        act.wait_ge(ss_done, n.at("ss"))
                    act.activation(junk, src, ACT.Square, accum_out=stat[:, SS + k:SS + k + 1]).then_inc(ss_done, 1)
                    n.step("ss")
                act.wait_ge(ss_done, n.at("ss"))
                for src, junk, k in sources:
                    act.activation(stat[:, RT + k:RT + k + 1], stat[:, SS + k:SS + k + 1], ACT.Sqrt,
                                   bias=stat[:, EPSC:EPSC + 1], scale=1.0 / width).then_inc(root_ready, 1)

            def rows_out(dst, src, k):
                act.wait_ge(rstd_ready, n.step("rstd"))
                act.activation(dst, src, ACT.Copy, scale=stat[:, RS + k:RS + k + 1]).then_inc(xn_ready, 1)
                n.step("xn")

            def scaled_hi(dsts):
                for dst in dsts:
                    n.step("tr")
                    n.step("scaled")
                    act.wait_ge(tr_read, n.at("tr"))
                    k = (n.n["scaled"] - 1) % 2
                    act.activation(dst, scaled[:, k, 0:int(np.prod(dst.shape[1:]))].rearrange("p (a b) -> p a b", a=dst.shape[1]),
                                   ACT.Copy).then_inc(norm_hi, 1)

            def plain_hi(dst):
                n.step("tr")
                act.wait_ge(tr_done, n.at("tr"))
                k = (n.n["tr"] - 1) % 2
                width = int(np.prod(dst.shape[1:]))
                act.activation(dst, turned[k][:, 0:width].rearrange("p (a b) -> p a b", a=dst.shape[1]), ACT.Copy).then_inc(tr_hi, 1)

            def act_dst(hi, q, half, t):
                return hi[:, q, 4 * half:4 * half + 4, t * P:(t + 1) * P]

            def gate_bias(gate_row):
                if n.n["small"]:
                    act.wait_ge(small_done, n.at("small"))
                act.dma_start(mod_row[4:5, :], a["mod_gate_b"][gate_row:gate_row + 1, :]).then_inc(modbias_loaded, 16)

            def mod_copy(gate_row=None):
                n.step("mod")
                if n.n["small"]:
                    act.wait_ge(small_done, n.at("small"))
                if gate_row is not None:
                    gate_bias(gate_row)
                act.wait_ge(mod_done, n.at("mod"))
                act.activation(mod_row[0:4, :], mod_ps[0:4, :], ACT.Copy).then_inc(mod_row_ready, 1)

            act.wait_ge(cond_zero, 2)
            for t in range(NT):
                act.wait_ge(x_loaded[t], 16)
                roots([(x[:, t, :], xn[:, t, :], t)], D)
            for t in range(NT):
                rows_out(xn[:, t, :], x[:, t, :], t)
            scaled_hi([act_dst(act_hi, 0, half, 0) for half in range(2)])
            split()
            act.dma_start(proj[:, 1, :], a["b_in"].rearrange("(o n) -> o n", o=1).to_broadcast([P, IN_W])).then_inc(bias_loaded, 16)
            act.dma_start(pool_m[:, :, :, :], a["pool_m"]).then_inc(bias_loaded, 16)
            act.dma_start(mask[:, :], a["mask"]).then_inc(bias_loaded, 16)
            act.dma_start(w_pool[:, :, :], a["w_pool"].rearrange("g c d -> c g d")).then_inc(bias_loaded, 16)
            scaled_hi([act_dst(act_hi, 0, half, 1) for half in range(2)])
            act.wait_ge(const_loaded, 48)
            act.activation(cond_s[:, :], col("cond", 0, 2 * KT), ACT.Silu).then_inc(cond_silu, 1)
            act.wait_ge(cond_silu, 1)
            act.activation(cond_w[:, :, 0:3:2], cond_s[:, :].rearrange("p (k s) -> p k s", s=2), ACT.Copy).then_inc(cond_hi, 1)
            for k in range(3):
                split()
                n.step("unit", 2)
            n.step("unit", 2)

            def gates_sigmoid(k):
                split()
                for t in range(NT):
                    act.wait_ge(gemm_read, n.step("unit"))
                    g = proj[:, t, G0 + k * COLS:G0 + (k + 1) * COLS]
                    act.activation(g, g, ACT.Sigmoid).then_inc(gates_ready, 1)

            def exps(u):
                t, nk = u // 4, (u // 4 + 1) * P
                n.step("unit")
                act.wait_ge(negmax_ready, u + 1)
                if u >= 4:
                    act.wait_ge(tr_done, probs_turned[u - 4])
                for e in range(2):
                    last = act.activation(prob[:, u % 4, e, 0:nk], score[:, u % 2, e, 0:nk], ACT.Exp,
                                          bias=stat[:, NM + 2 * u + e:NM + 2 * u + e + 1],
                                          accum_out=stat[:, LS + 2 * u + e:LS + 2 * u + e + 1])
                last.then_inc(probs_ready, 1)

            probs_turned = {}

            def probs_out(first):
                for u in range(first, first + 4):
                    probs_turned[u] = n.step("tr")
                t = first // 4
                act.wait_ge(sink_in, t + 1)
                act.activation(stat[:, ES + 8 * t:ES + 8 * t + 8], stat[:, ES + 8 * t:ES + 8 * t + 8], ACT.Exp).then_inc(sink_exp, 1)

            gates_sigmoid(0)
            n.step("tr", 5)
            gates_sigmoid(1)
            exps(0)
            exps(1)
            for pair in range(2):
                act.wait_ge(gemm_read, n.step("unit"))
                act.activation(ypool_hi[:, 2 * pair:2 * pair + 2, :], diff[:, 2 * pair:2 * pair + 2, :], ACT.Copy).then_inc(pool_hi, 1)
            exps(2)
            exps(3)
            gates_sigmoid(2)
            probs_out(0)
            for u in range(4, 8):
                exps(u)
            gates_sigmoid(3)
            probs_out(4)
            act.wait_ge(gemm_done, n.at("unit"))
            act.dma_start(g_post1[:, :], a["g_mix_post"].rearrange("(o n) -> o n", o=1).to_broadcast([P, D])).then_inc(post1_loaded, 16)
            split()
            n.step("unit", 4)
            for t in range(NT):
                plain_hi(yattn_hi[:, 0:4, t * P:(t + 1) * P])
            split()
            mod_copy()
            split()
            n.step("unit", 4)
            n.step("small")
            for half in range(2):
                for t in range(NT):
                    plain_hi(act_dst(act_hi, 0, half, t))
            split()
            mod_copy()
            split()
            n.step("unit", 2)
            n.step("small")
            split()
            n.step("unit", 2)

            def root_before(src, scratch, t):
                act.wait_ge(gemm_read, n.at("unit", 1 - t))
                roots([(src(t), scratch, t)], D)
                n.step("rstd")

            def root_after(t):
                act.wait_ge(x_ready, n.step("x"))
                roots([(x[:, t, :], xn[:, t, :], t)], D)

            def high(q, t):
                scaled_hi([act_dst(act_hi, q, half, t) for half in range(2)])

            def mixed(t):
                return proj[:, t, 0:D]

            diff_rows = diff[:, :, :].rearrange("p a b -> p (a b)")
            root_before(mixed, diff_rows, 0)
            root_after(0)
            root_before(mixed, diff_rows, 1)
            rows_out(xn[:, 0, :], x[:, 0, :], 0)
            mod_copy()
            root_after(1)
            act.dma_start(ctx[:, :, :], a["ctx"].rearrange("(t p) d -> p t d", p=P)).then_inc(ctx_loaded, 16)
            act.dma_start(g_post2[:, :], a["g_mlp_post"].rearrange("(o n) -> o n", o=1).to_broadcast([P, D])).then_inc(post2_loaded, 16)
            rows_out(xn[:, 1, :], x[:, 1, :], 1)
            high(0, 0)
            split()
            high(0, 1)
            split()
            n.step("small")
            mod_copy()
            n.step("small")

            def square_hidden(k):
                split()
                for pair in range(2):
                    n.step("unit")
                    if pair:
                        split()
                    act.wait_ge(gemm_read, n.at("unit"))
                    h = h1[:, k, pair, :]
                    act.activation(h, h, ACT.Square).then_inc(h_ready, 1)
                    act.wait_ge(h_ready, n.step("square"))
                    act.activation(h1_hi[:, 4 * k + 2 * pair:4 * k + 2 * pair + 2, :], h.rearrange("p (f t) -> p f t", f=2),
                                   ACT.Copy).then_inc(tr_hi, 1)

            def mlp_turn(first=False):
                square_hidden(0)
                mod_copy()
                square_hidden(1)
                n.step("small")
                mod_copy()
                split()
                n.step("unit", 2)
                n.step("small")
                if first:
                    act.wait_ge(ctx_loaded, 16)
                    roots([(ctx[:, t, :], xn[:, t, :], t) for t in range(NT)], D)
                    for t in range(NT):
                        rows_out(xn[:, t, :], ctx[:, t, :], t)
                    high(1, 0)
                split()
                n.step("unit", 2)
                if first:
                    high(1, 1)

            mlp_turn(first=True)
            with n.loop(act, 3, split=6, unit=8, square=4, mod=2, small=2):
                mlp_turn()
            def mlp_rows(t):
                return mlp[:, t, :]

            h1_rows = h1[:, 0, :, :].rearrange("p a b -> p (a b)")
            gate_bias(0)
            root_before(mlp_rows, h1_rows, 0)
            split()
            mod_copy()
            root_before(mlp_rows, h1_rows, 1)
            root_after(0)
            split()
            rows_out(xn[:, 0, :], x[:, 0, :], 0)
            root_after(1)
            rows_out(xn[:, 1, :], x[:, 1, :], 1)
            high(0, 0)
            n.step("small", 2)
            mod_copy(1)
            high(0, 1)
            n.step("small", 2)
            act.wait_ge(tr_done, n.at("tr"))
            with n.loop(act, 4, split=2, unit=6) as i:
                for f in range(2):
                    split()
                    n.step("unit", 3)
                    act.wait_ge(gemm_read, n.at("unit"))
                    act.activation(conv_hi[:, bass.ds(i * 2 + f, 1), :, :].rearrange("p o s t -> p (o s) t"),
                                   conv_m[:, f, :, :], ACT.Copy).then_inc(h_hi, 1)
            for cb in range(2):
                split()
                n.step("unit", 4)

            def norm_both(gate_row, seqs, ahead):
                def root(tt):
                    act.wait_ge(x_ready, n.step("x"))
                    roots([(res(tt), junk[:, :], tt)], D)

                def high(t):
                    scaled_hi([act_dst(act_hi, 0, half, t) for half in range(2)])

                gate_bias(gate_row)
                for t in range(NT):
                    root(t)
                    rows_out(xn[:, t, :], res(t), t)
                high(0)
                root(2)
                high(1)
                split()
                act.wait_ge(tr_done, n.at("tr"))
                rows_out(xn[:, 0, :], res(2), 2)
                mod_copy()
                split()
                root(3)
                act.wait_ge(tr_done, n.at("tr"))
                rows_out(xn[:, 1, :], res(3), 3)
                scaled_hi([act_dst(act_hi, 1, half, 0) for half in range(2)])
                n.step("small", seqs)
                if ahead:
                    mod_copy(gate_row + 1)
                    split()
                scaled_hi([act_dst(act_hi, 1, half, 1) for half in range(2)])
                if not ahead:
                    mod_copy(gate_row + 1)
                n.step("small", seqs)

            norm_both(2, 2, False)

            def silu_chunk(first, early=False):
                split()
                for f in range(2):
                    n.step("unit")
                    act.wait_ge(gemm_done, n.at("unit"))
                    b = bank[(2 * f) % 4]
                    act.activation(silu[:, f, :], b[:, :], ACT.Silu).then_inc(silu_ready, 1)
                    n.step("unit")
                    if early and f:
                        split()
                    act.wait_ge(gemm_read, n.at("unit"))
                    act.activation(h2_hi[:, first + f, :, :], h2[:, f, :].rearrange("p (s t) -> p s t", s=2), ACT.Copy).then_inc(h_hi, 1)

            silu_chunk(0)
            split()
            n.step("unit", 8)
            with n.loop(act, 4, split=4, unit=16, mod=1, small=1):
                silu_chunk(0, early=True)
                mod_copy()
                silu_chunk(2)
                n.step("small")
                split()
                n.step("unit", 8)
            silu_chunk(0)
            silu_chunk(2)
            split()
            n.step("unit", 8)
            norm_both(4, 1, True)
            act.wait_ge(xn_ready, n.at("xn"))
            act.dma_start(w_pe[:, :, :], a["w_pe"]).then_inc(pe_loaded, 16)
            n.step("unit", 2)
            split()
            act.wait_ge(pe_loaded, 16)
            act.activation(w_pe_hi[:, :, :], w_pe[:, :, :], ACT.Copy).then_inc(wpe_hi, 1)
            n.step("unit", 4)
            act.wait_ge(tr_done, n.at("tr"))
            act.wait_ge(gemm_read, n.at("unit", 2))
            roots([(q_nat[:, t, :], xn[:, t, 0:QL], t) for t in range(NT)], QL)
            for t in range(NT):
                rows_out(xn[:, t, 0:QL], q_nat[:, t, :], t)
            act.wait_ge(gemm_read, n.at("unit"))
            roots([(kv_nat[:, tt, :], scaled[:, 0, 0:KVL], 4 + tt) for tt in range(2 * NT)], KVL)
            for tt in range(2 * NT):
                rows_out(kv_nat[:, tt, :], kv_nat[:, tt, :], 4 + tt)
            n.step("unit")
            scaled_hi([dst for t in range(NT) for dst in (ql_hi[:, 0:4, t * P:(t + 1) * P], ql_hi[:, 4:6, t * P:(t + 1) * P])])
            split(WQ)
            mod_copy(6)
            scaled_hi([kvl_hi[:, 0:2, q * SEQ:(q + 1) * SEQ] for q in range(2)])
            n.step("small")
            act.wait_ge(pe_sum, 1)
            act.activation(stat[:, RT + 8:RT + 12], stat[:, SS + 8:SS + 12], ACT.Sqrt, bias=stat[:, EPSC:EPSC + 1],
                           scale=1.0 / ROPE).then_inc(pe_root, 1)
            act.wait_ge(tr_done, n.at("tr"))

            def take(j):
                act.wait_ge(gemm_done, n.step("unit"))
                b = bank[2 + j % 2]
                if j < NT:
                    act.activation(qg[:, j, :, :].rearrange("p h d -> p (h d)"), b[:, 0:GH * QK], ACT.Copy).then_inc(gemm_read, 1)
                else:
                    kv = b[:, :].rearrange("p (h d) -> p h d", h=GH)
                    act.activation(kg[:, j - NT, :, 0:NOPE], kv[:, :, 0:NOPE], ACT.Copy)
                    act.activation(v_next[:, j - NT, :, :], kv[:, :, NOPE:NOPE + VD], ACT.Copy).then_inc(gemm_read, 1)

            def squares(queries):
                act.wait_ge(gemm_read, n.at("unit"))
                if n.n["gsum"]:
                    act.wait_ge(gsum_ready, n.at("gsum"))
                if queries:
                    act.activation(sq[:, 0:NT * GH * QK], qg[:, :, :, :].rearrange("p t h d -> p (t h d)"), ACT.Square).then_inc(sq_ready, 1)
                else:
                    act.activation(sq[:, :].rearrange("p (a d) -> p a d", d=NOPE), kg[:, :, :, 0:NOPE].rearrange("p t h d -> p (t h) d"),
                                   ACT.Square).then_inc(sq_ready, 1)
                n.step("gsum")

            def group_roots():
                act.wait_ge(gsum_ready, n.at("gsum"))
                act.activation(stat[:, GQ:GQ + 24], stat[:, GQ:GQ + 24], ACT.Sqrt, bias=stat[:, EPSC:EPSC + 1], scale=1.0 / NOPE)
                act.activation(stat[:, GQ + 24:GQ + 32], stat[:, GQ + 24:GQ + 32], ACT.Sqrt, bias=stat[:, EPSC:EPSC + 1],
                               scale=1.0 / ROPE).then_inc(groot_ready, 1)

            def attend_group(following=True, width=WQ):
                for tt in range(2 * NT):
                    act.wait_ge(tr_done, n.step("tr"))
                    k = (n.n["tr"] - 1) % 2
                    act.activation(kgT[:, :, tt * P:(tt + 1) * P], turned[k][0:QK, :].rearrange("p (h t) -> p h t", h=GH),
                                   ACT.Copy).then_inc(tr_read, 1)
                for t in range(NT):
                    act.wait_ge(tr_done, n.step("tr"))
                    k = (n.n["tr"] - 1) % 2
                    act.activation(qgT[:, :, t * P:(t + 1) * P], turned[k][0:QK, :].rearrange("p (h t) -> p h t", h=GH),
                                   ACT.Copy).then_inc(tr_read, 1)
                if following:
                    split(WKV)
                for u in range(8):
                    act.wait_ge(negmax_ready, 8 + n.step("negmax"))
                    if u >= 2:
                        act.wait_ge(tr_done, n.at("tr", 1))
                    act.activation(pr[:, u % 2, :], bank[u % 2][:, :], ACT.Exp, bias=stat[:, NM + u:NM + u + 1], scale=QK ** -0.5,
                                   accum_out=stat[:, LS + u:LS + u + 1]).then_inc(probs_ready, 1)
                    n.step("tr")
                    if u == 0:
                        act.wait_ge(pv_done, n.at("pv"))
                        n.step("pv", 8)
                        act.activation(vg[:, :, :, :].rearrange("p a h d -> p (a h d)"), v_next[:, :, :, :].rearrange("p a h d -> p (a h d)"),
                                       ACT.Copy).then_inc(v_ready, 1)
                        n.step("v")
                    if following and u < 6:
                        if u == NT:
                            act.wait_ge(v_ready, n.at("v"))
                        take(u)
                        if u == 1:
                            squares(True)
                        if u == 3:
                            split(width)
                        if u == 5:
                            squares(False)
                if following:
                    group_roots()

            split(WKV)
            take(0)
            take(1)
            squares(True)
            split(WQ)
            for j in range(NT, 6):
                take(j)
            squares(False)
            group_roots()
            n.step("pv", 8)
            with n.loop(act, 2, split=2, unit=6, tr=14, gsum=2, negmax=8, pv=8, v=1):
                attend_group()
            attend_group(width=CHUNK)
            attend_group(following=False)
            split()
            for half in range(2):
                for t in range(NT):
                    plain_hi(act_dst(act_hi, 0, half, t))
            mod_copy(7)
            for cb in range(2):
                split()
                n.step("unit", 2)
            n.step("small")
            for t in range(NT):
                root_after(t)
                rows_out(xn[:, t, :], x[:, t, :], t)
            scaled_hi([act_dst(act_hi, 0, half, t) for t in range(NT) for half in range(2)])

            def silu_chunk1(p, k):
                split()
                for f in range(2):
                    act.wait_ge(gemm_done, n.step("unit"))
                    b = bank[(2 * k + f) % 4]
                    act.activation(silu3[:, f, :], b[:, 0:SEQ], ACT.Silu).then_inc(silu_ready, 1)
                    act.wait_ge(gemm_read, n.at("unit"))
                    act.activation(h3_hi[:, p, 2 * k + f, :], h3[:, k, f, :], ACT.Copy).then_inc(tr_hi, 1)

            def group1(p):
                silu_chunk1(p, 0)
                silu_chunk1(p, 1)
                split()
                n.step("unit", 4)

            silu_chunk1(0, 0)
            silu_chunk1(0, 1)
            with n.loop(act, 2, split=6, unit=16):
                group1(1)
                group1(0)
            silu_chunk1(1, 0)
            split()
            n.step("unit", 4)
            split()

        @block.vector
        def _(ve):
            n = Count()

            def chained(ins):
                ins.then_inc(dve_chain, 1)
                ve.wait_ge(dve_chain, n.step("chain"))

            def split(width=CHUNK):
                n.step("split")
                if n.n["split"] > STREAM:
                    return
                s = (n.n["split"] - 1) % 2
                for half, (first, share, _) in enumerate(halves_of(width)):
                    part = slice(first, share)
                    ve.wait_ge(hi_ready, 2 * n.at("split") - 1 + half)
                    ve.tensor_tensor(w_lo[:, s, part], raw[:, s, part], w_hi[:, s, part].bitcast(f32),
                                     ALU.subtract).then_inc(lo_ready, 1)

            rot = {"first": 0, "banks": 4}

            def rotation(banks):
                rot["first"], rot["banks"] = n.n["unit"], banks

            def unit():
                ve.wait_ge(gemm_done, n.step("unit"))
                return bank[(n.n["unit"] - 1 - rot["first"]) % rot["banks"]]

            def recips(ks):
                for k in ks:
                    ve.wait_ge(root_ready, n.step("root"))
                    ve.reciprocal(stat[:, RS + k:RS + k + 1], stat[:, RT + k:RT + k + 1]).then_inc(rstd_ready, 1)
                    n.step("rstd")

            def scaled_rows(items, after_first=None):
                def lower(hi, lo):
                    ve.wait_ge(norm_hi, n.step("norm"))
                    k = (n.n["norm"] - 1) % 2
                    src = scaled[:, k, 0:int(np.prod(lo.shape[1:]))].rearrange("p (a b) -> p a b", a=lo.shape[1])
                    ve.tensor_tensor(lo, src, hi.bitcast(f32), ALU.subtract).then_inc(norm_ready, 1)

                before = None
                for gain, shift, hi, lo in items:
                    n.step("scaled")
                    ve.wait_ge(tr_done, n.step("tr"))
                    k, b = (n.n["scaled"] - 1) % 2, (n.n["tr"] - 1) % 2
                    m, w = lo.shape[1], lo.shape[2]
                    dst = scaled[:, k, 0:m * w].rearrange("p (a b) -> p a b", a=m)
                    if n.n["scaled"] > 2:
                        ve.wait_ge(norm_ready, n.at("scaled", 2))
                    src = turned[b][:, 0:m * w].rearrange("p (a b) -> p a b", a=m)
                    if shift is None:
                        last = ve.tensor_tensor(dst, src, gain.to_broadcast([P, m, w]), ALU.mult)
                    else:
                        for j in range(m):
                            last = ve.tensor_scalar(dst[:, j, :], src[:, j, :], gain[:, j, :], shift[:, j, :], ALU.mult, ALU.add)
                    last.then_inc(tr_read, 1)
                    if before:
                        lower(*before)
                    elif after_first:
                        after_first()
                    before = (hi, lo)
                lower(*before)

            def plain_rows(hi, lo):
                n.step("tr")
                ve.wait_ge(tr_hi, n.step("tr_hi"))
                b = (n.n["tr"] - 1) % 2
                m, w = lo.shape[1], lo.shape[2]
                ve.tensor_tensor(lo, turned[b][:, 0:m * w].rearrange("p (a b) -> p a b", a=m), hi.bitcast(f32),
                                 ALU.subtract).then_inc(tr_read, 1)

            def act_dst(buf, q, half, t):
                return buf[:, q, 4 * half:4 * half + 4, t * P:(t + 1) * P]

            def gain_cols(name, j, m):
                return col(name, j, m).rearrange("p (a o) -> p a o", o=1)

            def gained(name, t):
                return [(gain_cols(name, 4 * half, 4), None, act_dst(act_hi, 0, half, t), act_dst(act_lo, 0, half, t)) for half in range(2)]

            def modulated(c, shift_at, q, t):
                return [(coef[:, c, 4 * half:4 * half + 4, q:q + 1], mod_col[:, shift_at + 4 * half:shift_at + 4 * half + 4, q:q + 1],
                         act_dst(act_hi, q, half, t), act_dst(act_lo, q, half, t)) for half in range(2)]

            def coefs(c, name, layer, scale_at):
                chained(ve.scalar_tensor_tensor(coef[:, c, :, :], mod_col[:, scale_at:scale_at + KT, :], 1.0,
                                                gain_cols(name, layer * KT, KT).to_broadcast([P, KT, 2]), ALU.add, ALU.mult))

            def mod_read(chunk, turn=None, step=0):
                n.step("small")
                ve.wait_ge(small_done, n.step("mod_small"))
                if turn is None:
                    dst, b = mod_col[:, 4 * chunk:4 * chunk + 4, :], col("mod_b", 4 * chunk, 4)
                else:
                    dst = mod_col[:, bass.ds(turn * (4 * step) + 4 * chunk, 4), :]
                    b = cols[:, bass.ds(turn * (4 * step) + COL["mod_b"] + 4 * chunk, 4)]
                ve.tensor_tensor(dst, small[:, 0:8].rearrange("p (k s) -> p k s", s=2),
                                 b.rearrange("p (a o) -> p a o", o=1).to_broadcast([P, 4, 2]), ALU.add).then_inc(small_read, 1)

            def gate_read(half, slots):
                for s in slots:
                    n.step("small")
                    ve.wait_ge(small_done, n.step("mod_small"))
                    ve.tensor_copy(gate[:, s, half * COLS:(half + 1) * COLS], small[:, :]).then_inc(small_read, 1)

            def post_norm(src, g, t):
                recips([t])
                ve.wait_ge(rstd_ready, n.at("rstd"))
                chained(ve.scalar_tensor_tensor(src, src, stat[:, RS + t:RS + t + 1], g[:, :], ALU.mult, ALU.mult))
                ve.tensor_tensor(x[:, t, :], x[:, t, :], src, ALU.add).then_inc(x_ready, 1)
                n.step("x")

            ve.memset(cond_w[:, :, :].bitcast(f32), 0.0).then_inc(cond_zero, 1)
            ve.memset(stat[:, EPSC:EPSC + 1], EPS).then_inc(cond_zero, 1)
            recips([0, 1])
            ve.wait_ge(const_loaded, 48)
            ve.tensor_scalar(stat[:, NSINK:NSINK + 8], row("sinks", HEADS), -1.0, None, ALU.mult)
            ve.tensor_tensor(row("kn_nope", NOPE), row("kn_nope", NOPE), row("qn_nope", NOPE), ALU.mult)
            scaled_rows(gained("g_mix", 0))
            split()
            scaled_rows(gained("g_mix", 1))
            ve.wait_ge(cond_hi, 1)
            ve.tensor_tensor(cond_w[:, :, 1:4:2], cond_s[:, :].rearrange("p (k s) -> p k s", s=2),
                             cond_w[:, :, 0:3:2].bitcast(f32), ALU.subtract).then_inc(cond_ready, 1)
            for k, (c0, width) in enumerate(((0, COLS), (Q0, COLS), (K0, 256))):
                split()
                if k == 0:
                    ve.wait_ge(bias_loaded, 64)
                for t in range(NT):
                    b = unit()
                    ve.tensor_tensor(proj[:, t, c0:c0 + width], b[:, 0:width], proj[:, 1, c0:c0 + width], ALU.add).then_inc(gemm_read, 1)
            for pair in range(2):
                b = unit()
                ve.tensor_copy(diff[:, 2 * pair:2 * pair + 2, :].rearrange("p g t -> p (g t)"), b[:, :]).then_inc(gemm_read, 1)
            for t in range(NT):
                heads = proj[:, t, Q0:V0].rearrange("p (h d) -> p h d", d=HD)
                lo, hi = heads[:, :, 0:8], heads[:, :, 8:16]
                c = table("cos1", 8, j=8 * t).rearrange("p (o d) -> p o d", o=1).to_broadcast([P, 10, 8])
                s = table("sin1", 8, j=8 * t).rearrange("p (o d) -> p o d", o=1).to_broadcast([P, 10, 8])
                for j, (src, by) in enumerate(((lo, c), (hi, s), (hi, c), (lo, s))):
                    last = ve.tensor_tensor(rope_t[:, j, t, :, :], src, by, ALU.mult)
                chained(last)
                ve.tensor_tensor(lo, rope_t[:, 0, t, :, :], rope_t[:, 1, t, :, :], ALU.subtract)
                last = ve.tensor_tensor(hi, rope_t[:, 2, t, :, :], rope_t[:, 3, t, :, :], ALU.add)
            last.then_inc(rope_ready, 1)

            def gates_bias(k):
                split()
                for t in range(NT):
                    b = unit()
                    g = slice(G0 + k * COLS, G0 + (k + 1) * COLS)
                    ve.tensor_tensor(proj[:, t, g], b[:, :], proj[:, 1, g], ALU.add).then_inc(gemm_read, 1)

            gates_bias(0)
            for t in range(NT):
                for half in range(2):
                    ve.wait_ge(tr_done, n.step("tr"))
                    ve.tensor_copy(qT[:, 4 * half:4 * half + 4, t * P:(t + 1) * P],
                                   turned[(n.n["tr"] - 1) % 2][0:HD, :].rearrange("p (h t) -> p h t", h=4)).then_inc(tr_read, 1)
            ve.wait_ge(tr_done, n.step("tr"))
            ve.tensor_copy(kT[:, :, :], turned[(n.n["tr"] - 1) % 2][0:HD, :].rearrange("p (j t) -> p j t", j=KVH)).then_inc(tr_read, 1)
            gates_bias(1)

            def maxima(u):
                t, p = u // 4, u % 4
                nk = (t + 1) * P
                b = unit()
                if u >= 2:
                    ve.wait_ge(probs_ready, u - 1)
                seen = mask[:, (1 - t) * P:(1 - t) * P + nk].rearrange("p (o k) -> p o k", o=1).to_broadcast([P, 2, nk])
                sc = score[:, u % 2, :, 0:nk]
                ve.scalar_tensor_tensor(sc, b[:, 0:2 * nk].rearrange("p (e k) -> p e k", e=2), HD ** -0.5, seen,
                                        ALU.mult, ALU.add).then_inc(gemm_read, 1)
                ve.wait_ge(gemm_read, n.at("unit"))
                chained(ve.tensor_reduce(stat[:, MX:MX + 2], sc, AX.X, ALU.max))
                ve.scalar_tensor_tensor(stat[:, NM + 2 * u:NM + 2 * u + 2], stat[:, MX:MX + 2], -1.0,
                                        stat[:, NSINK + 2 * p:NSINK + 2 * p + 2], ALU.mult, ALU.min).then_inc(negmax_ready, 1)

            def probs_out(first):
                t = first // 4
                ve.wait_ge(negmax_ready, first + 4)
                ve.tensor_tensor(stat[:, ES + 8 * t:ES + 8 * t + 8], row("sinks", HEADS), stat[:, NM + 8 * t:NM + 8 * t + 8],
                                 ALU.add).then_inc(sink_in, 1)
                for u in range(first, first + 4):
                    ve.wait_ge(tr_done, n.step("tr"))
                    if u >= 2:
                        ve.wait_ge(pv_done, u - 1)
                    m = 2 * (t + 1)
                    ve.tensor_copy(pT[:, u % 2, 0:m, :], turned[(n.n["tr"] - 1) % 2][:, 0:m * P].rearrange("p (a b) -> p a b", a=m)
                                   ).then_inc(tr_read, 1)
                ve.wait_ge(sink_exp, t + 1)
                ve.wait_ge(probs_ready, first + 4)
                den = stat[:, RD + 8 * t:RD + 8 * t + 8]
                chained(ve.tensor_tensor(den, stat[:, LS + 8 * t:LS + 8 * t + 8], stat[:, ES + 8 * t:ES + 8 * t + 8], ALU.add))
                chained(ve.reciprocal(den, den))
                ve.wait_ge(pv_done, first + 4)
                n.step("small")
                ve.tensor_tensor(proj[:, t, 0:POOL].rearrange("p (h d) -> p h d", d=HD), small[:, :].rearrange("p (h d) -> p h d", d=HD),
                                 den.rearrange("p (h o) -> p h o", o=1).to_broadcast([P, HEADS, HD]), ALU.mult).then_inc(small_read, 1)

            maxima(0)
            maxima(1)
            for pair in range(2):
                b = unit()
                g = slice(2 * pair, 2 * pair + 2)
                ve.tensor_tensor(diff[:, g, :], b[:, :].rearrange("p (g t) -> p g t", g=2),
                                 gain_cols("pool_scale", 2 * pair, 2).to_broadcast([P, 2, SEQ]), ALU.mult).then_inc(gemm_read, 1)
            maxima(2)
            maxima(3)
            for pair in range(2):
                g = slice(2 * pair, 2 * pair + 2)
                ve.wait_ge(pool_hi, pair + 1)
                ve.tensor_tensor(ypool_lo[:, g, :], diff[:, g, :], ypool_hi[:, g, :].bitcast(f32), ALU.subtract).then_inc(pool_lo, 1)
            gates_bias(2)
            probs_out(0)
            for u in range(4, 8):
                maxima(u)
            gates_bias(3)
            probs_out(4)

            def branch(g0, first):
                split()
                for cb in range(2):
                    for t in range(NT):
                        b = unit()
                        g = proj[:, t, g0 + cb * COLS:g0 + (cb + 1) * COLS]
                        ve.wait_ge(gates_ready, 2 * (first + cb) + t + 1)
                        ve.tensor_tensor(g, g, b[:, :], ALU.mult).then_inc(gemm_read, 1)
                        if first:
                            ve.wait_ge(gemm_read, n.at("unit"))
                            m = proj[:, t, G0 + cb * COLS:G0 + (cb + 1) * COLS]
                            ve.tensor_tensor(m, m, g, ALU.add).then_inc(merged_ready, 1)

            branch(G0, 0)
            for t in range(NT):
                plain_rows(yattn_hi[:, 0:4, t * P:(t + 1) * P], yattn_lo[:, 0:4, t * P:(t + 1) * P])
            split()
            branch(G0 + D, 2)
            mod_read(0)
            for half in range(2):
                for t in range(NT):
                    plain_rows(act_dst(act_hi, 0, half, t), act_dst(act_lo, 0, half, t))
            split()

            def mixed_rows(cb, t):
                b = unit()
                ve.tensor_copy(proj[:, t, cb * COLS:(cb + 1) * COLS], b[:, :]).then_inc(gemm_read, 1)
                ve.wait_ge(gemm_read, n.at("unit"))

            split()
            for t in range(NT):
                mixed_rows(0, t)
            mod_read(1)
            split()
            ve.wait_ge(post1_loaded, 16)
            mixed_rows(1, 0)
            post_norm(proj[:, 0, 0:D], g_post1, 0)
            mixed_rows(1, 1)
            recips([0])
            post_norm(proj[:, 1, 0:D], g_post1, 1)
            recips([1])
            scaled_rows(gained("g_mlp", 0))
            mod_read(2)
            split()
            scaled_rows(gained("g_mlp", 1))
            split()
            ve.memset(mlp[:, :, :], 0.0).then_inc(dve_chain, 1)
            ve.wait_ge(dve_chain, n.step("chain"))

            def rectify(i, k):
                split()
                for pair in range(2):
                    if i is not None:
                        ve.wait_ge(hidden_ready, n.at("hidden1", 3))
                    b = unit()
                    ve.tensor_scalar(h1[:, k, pair, :], b[:, :], 0.0, None, ALU.max).then_inc(gemm_read, 1)
                    if pair:
                        split()
                    tiles = slice(4 * k + 2 * pair, 4 * k + 2 * pair + 2)
                    ve.wait_ge(tr_hi, n.step("tr_hi"))
                    ve.tensor_tensor(h1_lo[:, tiles, :], h1[:, k, pair, :].rearrange("p (f t) -> p f t", f=2), h1_hi[:, tiles, :].bitcast(f32),
                                     ALU.subtract).then_inc(hidden_ready, 1)
                    n.step("hidden1")

            def down_rows(cb):
                split()
                for t in range(NT):
                    b = unit()
                    dst = mlp[:, t, cb * COLS:(cb + 1) * COLS]
                    ve.tensor_tensor(dst, b[:, :], dst, ALU.add).then_inc(gemm_read, 1)

            def mlp_turn(i=None):
                at_chunk, step = (4, 0) if i is None else (6, 2)
                for k in range(2):
                    rectify(i, k)
                    if k:
                        mod_read(at_chunk, i, step)
                    elif i is None:
                        mod_read(3)
                        ve.wait_ge(small_read, n.at("small"))
                        coefs(0, "norm_mix", 0, 8)
                if i is None:
                    recips([0, 1])
                down_rows(0)
                mod_read(at_chunk + 1, i, step)
                if i is None:
                    scaled_rows(modulated(0, 0, 1, 0))
                down_rows(1)
                if i is None:
                    scaled_rows(modulated(0, 0, 1, 1))

            mlp_turn()
            with n.loop(ve, 3, split=6, unit=8, tr_hi=4, hidden1=4, small=2, mod_small=2) as i:
                mlp_turn(i)
            ve.wait_ge(post2_loaded, 16)
            post_norm(mlp[:, 0, :], g_post2, 0)
            split()
            post_norm(mlp[:, 1, :], g_post2, 1)
            recips([0])
            split()
            recips([1])
            for t in range(NT):
                scaled_rows(modulated(0, 0, 0, t))
                gate_read(0, (t,))
            gate_read(1, (0, 1))
            ve.wait_ge(tr_done, n.at("tr"))
            ve.memset(z_pad[:, :, 0:1], 0.0)
            chained(ve.memset(z_pad[:, :, SEQ + 1:SEQ + 2], 0.0))
            rotation(3)

            def tap(name, i, f):
                return cols[:, bass.ds(i * 2 + COL[name] + f, 1)]

            with n.loop(ve, 4, split=2, unit=6, h=2, chain=6) as i:
                for f in range(2):
                    split()
                    b = unit()
                    ve.tensor_copy(c_sb[:, :, :].rearrange("p s t -> p (s t)"), b[:, :]).then_inc(gemm_read, 1)
                    ve.wait_ge(gemm_read, n.at("unit"))
                    b = unit()
                    ve.tensor_tensor(z_pad[:, :, 1:SEQ + 1], c_sb[:, :, :], b[:, :].rearrange("p (s t) -> p s t", s=2),
                                     ALU.mult).then_inc(gemm_read, 1)
                    ve.wait_ge(gemm_read, n.at("unit"))
                    chained(ve.tensor_scalar(conv_y[:, :, :], z_pad[:, :, 1:SEQ + 1], tap("conv_k1", i, f), tap("conv_b", i, f),
                                             ALU.mult, ALU.add))
                    chained(ve.scalar_tensor_tensor(conv_y[:, :, :], z_pad[:, :, 0:SEQ], tap("conv_k0", i, f), conv_y[:, :, :],
                                                    ALU.mult, ALU.add))
                    chained(ve.scalar_tensor_tensor(conv_y[:, :, :], z_pad[:, :, 2:SEQ + 2], tap("conv_k2", i, f), conv_y[:, :, :],
                                                    ALU.mult, ALU.add))
                    b = unit()
                    ve.tensor_tensor(conv_m[:, f, :, :], conv_y[:, :, :], b[:, :].rearrange("p (s t) -> p s t", s=2),
                                     ALU.mult).then_inc(gemm_read, 1)
                    ve.wait_ge(h_hi, n.step("h"))
                    ve.tensor_tensor(conv_lo[:, bass.ds(i * 2 + f, 1), :, :].rearrange("p o s t -> p (o s) t"), conv_m[:, f, :, :],
                                     conv_hi[:, bass.ds(i * 2 + f, 1), :, :].rearrange("p o s t -> p (o s) t").bitcast(f32),
                                     ALU.subtract).then_inc(h_lo, 1)
            rotation(4)

            def add_gated(tt, cb, g, last):
                b = unit()
                k = n.n["unit"] % 2
                r = res(tt)[:, cb * COLS:(cb + 1) * COLS]
                ve.tensor_tensor(gated[:, k, :], b[:, :], gate[:, g, cb * COLS:(cb + 1) * COLS], ALU.mult).then_inc(gemm_read, 1)
                ve.wait_ge(gemm_read, n.at("unit"))
                ins = ve.tensor_tensor(r, r, gated[:, k, :], ALU.add)
                if last:
                    ins.then_inc(x_ready, 1)
                else:
                    ins.then_inc(dve_chain, 1)
                    n.step("chain")

            split()
            for tt in range(2 * NT):
                add_gated(tt, 0, tt // NT, False)
            split()

            def norm_both(add, c, layer, gain, shift_at, slots, ahead):
                coefs(c, gain, layer, shift_at + 8)
                def summed(tt):
                    ve.wait_ge(norm_ready, n.at("norm"))
                    add(tt)
                    ve.wait_ge(x_ready, n.step("x"))

                def normed(t):
                    scaled_rows(modulated(c, shift_at, 0, t))

                summed(0)
                recips([0])
                summed(1)
                recips([1])
                normed(0)
                summed(2)
                normed(1)
                summed(3)
                recips([2])
                split()
                split()
                recips([3])
                for t in range(NT):
                    scaled_rows(modulated(c, shift_at, 1, t))
                    gate_read(0, slots[t::NT])
                    if ahead and t == 0:
                        split()
            norm_both(lambda tt: add_gated(tt, 1, tt // NT, True), 1, 0, "norm_ffn", 16, (0, 1), False)
            gate_read(1, (0, 1))

            def hidden_chunk(first, early=False):
                split()
                for f in range(2):
                    n.step("unit")
                    b = unit()
                    ve.wait_ge(silu_ready, n.step("silu"))
                    ve.tensor_tensor(h2[:, f, :], silu[:, f, :], b[:, :], ALU.mult).then_inc(gemm_read, 2)
                    if early and f:
                        split()
                    ve.wait_ge(h_hi, 8 + n.step("hidden"))
                    k = first + f
                    ve.tensor_tensor(h2_lo[:, k, :, :], h2[:, f, :].rearrange("p (s t) -> p s t", s=2), h2_hi[:, k, :, :].bitcast(f32),
                                     ALU.subtract).then_inc(h_lo, 1)

            def down_gated():
                split()
                for cb in range(2):
                    for tt in range(2 * NT):
                        add_gated(tt, cb, tt // NT, False)

            hidden_chunk(0)
            down_gated()
            with n.loop(ve, 4, split=4, unit=16, small=1, mod_small=1, silu=4, hidden=4, chain=8) as i:
                hidden_chunk(0, early=True)
                hidden_chunk(2)
                mod_read(12, i, 1)
                down_gated()
            hidden_chunk(0)
            hidden_chunk(2)
            split()

            def down_rows0(tt):
                for cb in range(2):
                    add_gated(tt, cb, tt // NT, cb == 1)

            ve.wait_ge(small_read, n.at("small"))
            norm_both(down_rows0, 2, 1, "norm_mix", 32, (0,), True)
            for t in range(NT):
                b = unit()
                ve.tensor_copy(q_nat[:, t, 0:COLS], b[:, :]).then_inc(gemm_read, 1)
            split()
            ve.wait_ge(wpe_hi, 1)
            ve.tensor_tensor(w_pe_lo[:, :, :], w_pe[:, :, :], w_pe_hi[:, :, :].bitcast(f32), ALU.subtract).then_inc(wpe_lo, 1)
            for tt in range(2 * NT):
                b = unit()
                if tt < NT:
                    ve.tensor_copy(q_nat[:, tt, COLS:QL], b[:, 0:256])
                ve.tensor_copy(kv_nat[:, tt, :], b[:, 256:COLS]).then_inc(gemm_read, 1)
                if tt == 0:
                    gate_read(1, (0,))
                if tt == 1:
                    recips([0, 1])
            recips(range(4, 8))
            b = unit()
            ve.tensor_copy(pe[:, :, :].rearrange("p t d -> p (t d)"), b[:, 0:2 * NT * ROPE]).then_inc(gemm_read, 1)
            ve.wait_ge(gemm_read, n.at("unit"))
            scaled_rows([item for t in range(NT) for item in (
                (gain_cols("q_norm", 0, 4), None, ql_hi[:, 0:4, t * P:(t + 1) * P], ql_lo[:, 0:4, t * P:(t + 1) * P]),
                (gain_cols("q_norm", 4, 2), None, ql_hi[:, 4:6, t * P:(t + 1) * P], ql_lo[:, 4:6, t * P:(t + 1) * P]))])
            split(WQ)
            scaled_rows([(gain_cols("kv_norm", 0, 2), None, kvl_hi[:, 0:2, q * SEQ:(q + 1) * SEQ], kvl_lo[:, 0:2, q * SEQ:(q + 1) * SEQ])
                         for q in range(2)])
            gate_read(0, (1,))
            chained(ve.tensor_tensor(pe_t[:, :, :], pe[:, :, :], pe[:, :, :], ALU.mult))
            ve.tensor_reduce(stat[:, SS + 8:SS + 12], pe_t[:, :, :], AX.X, ALU.add).then_inc(pe_sum, 1)
            ve.wait_ge(pe_root, 1)
            chained(ve.reciprocal(stat[:, RS + 8:RS + 12], stat[:, RT + 8:RT + 12]))
            chained(ve.tensor_tensor(pe[:, :, :], pe[:, :, :],
                                     stat[:, RS + 8:RS + 12].rearrange("p (t o) -> p t o", o=1).to_broadcast([P, 2 * NT, ROPE]), ALU.mult))
            chained(ve.tensor_tensor(pe[:, :, :], pe[:, :, :],
                                     row("kn_rope", ROPE).rearrange("p (o d) -> p o d", o=1).to_broadcast([P, 2 * NT, ROPE]), ALU.mult))

            def halves(ap, k):
                return ap.rearrange("p h (a k d) -> p h a k d", a=2, k=2)[:, :, :, k, :]

            def rotate(src, tmp, t, heads):
                def tabs(name):
                    return table(name, ROPE, j=ROPE * t).rearrange("p (o d) -> p o d", o=1)

                for k in range(2):
                    s = halves(tabs("sinm"), k).to_broadcast([P, heads, 2, 8])
                    last = ve.tensor_tensor(halves(tmp, k), halves(src, 1 - k), s, ALU.mult)
                chained(last)
                chained(ve.tensor_tensor(src, src, tabs("cosm").to_broadcast([P, heads, ROPE]), ALU.mult))
                return ve.tensor_tensor(src, src, tmp, ALU.add)

            for t in range(NT):
                chained(rotate(pe[:, t:t + 1, :], pe_t[:, t:t + 1, :], t, 1))
            for tt in range(2 * NT):
                last = ve.tensor_copy(kg[:, tt, :, NOPE:QK], pe[:, tt:tt + 1, :].to_broadcast([P, GH, ROPE]))
            chained(last)

            QH, KH = NT * GH, 2 * NT * GH
            qf = qg[:, :, :, :].rearrange("p t h d -> p (t h) d")

            def of_heads(first, heads):
                return stat[:, GQ + first:GQ + first + heads].rearrange("p (a o) -> p a o", o=1)

            def query_sums():
                sf = sq[:, 0:QH * QK].rearrange("p (a d) -> p a d", d=QK)
                ve.wait_ge(sq_ready, n.step("sq"))
                ve.tensor_reduce(stat[:, GQ:GQ + QH], sf[:, :, 0:NOPE], AX.X, ALU.add)
                ve.tensor_reduce(stat[:, GQ + QH + KH:GQ + 2 * QH + KH], sf[:, :, NOPE:QK], AX.X, ALU.add).then_inc(gsum_ready, 1)

            def query_gains():
                ve.tensor_tensor(qf[:, :, 0:NOPE], qf[:, :, 0:NOPE],
                                 row("kn_nope", NOPE).rearrange("p (o d) -> p o d", o=1).to_broadcast([P, QH, NOPE]), ALU.mult)
                chained(ve.tensor_tensor(qf[:, :, NOPE:QK], qf[:, :, NOPE:QK],
                                         row("qn_rope", ROPE).rearrange("p (o d) -> p o d", o=1).to_broadcast([P, QH, ROPE]), ALU.mult))

            def query_rotation():
                for t in range(NT):
                    last = rotate(qg[:, t, :, NOPE:QK], qr_t[:, t, :, :], t, GH)
                chained(last)

            def key_sums():
                ve.wait_ge(sq_ready, n.step("sq"))
                ve.tensor_reduce(stat[:, GQ + QH:GQ + QH + KH], sq[:, :].rearrange("p (a d) -> p a d", d=NOPE), AX.X,
                                 ALU.add).then_inc(gsum_ready, 1)

            def normalise():
                ve.wait_ge(groot_ready, n.step("groot"))
                every = stat[:, GQ:GQ + 2 * QH + KH]
                chained(ve.reciprocal(every, every))
                for tt in range(2 * NT):
                    k = kg[:, tt, :, 0:NOPE]
                    ve.tensor_tensor(k, k, of_heads(QH + GH * tt, GH).to_broadcast([P, GH, NOPE]), ALU.mult).then_inc(qk_ready, 1)
                q = qf[:, :, 0:NOPE]
                ve.tensor_tensor(q, q, of_heads(0, QH).to_broadcast([P, QH, NOPE]), ALU.mult)
                q = qf[:, :, NOPE:QK]
                ve.tensor_tensor(q, q, of_heads(QH + KH, QH).to_broadcast([P, QH, ROPE]), ALU.mult).then_inc(qk_ready, 1)

            def mla_max(u):
                ve.wait_ge(scores_done, n.step("scores"))
                chained(ve.tensor_reduce(stat[:, MX + u:MX + u + 1], bank[u % 2][:, :], AX.X, ALU.max))
                ve.tensor_scalar(stat[:, NM + u:NM + u + 1], stat[:, MX + u:MX + u + 1], -QK ** -0.5, None, ALU.mult).then_inc(negmax_ready, 1)

            def attend_group(columns, following=True, width=WQ):
                n.step("tr", 6)
                for u in range(2):
                    mla_max(u)
                if following:
                    split(WKV)
                    n.step("unit", 6)
                for u in range(8):
                    ve.wait_ge(tr_done, n.step("tr"))
                    n.step("pv")
                    if u >= 2:
                        ve.wait_ge(pv_done, 8 + n.at("pv", 2))
                    ve.tensor_copy(prT[:, u % 2, :, :], turned[(n.n["tr"] - 1) % 2][:, :].rearrange("p (a b) -> p a b", a=4)).then_inc(tr_read, 1)
                    if u + 2 < 8:
                        mla_max(u + 2)
                    if following:
                        if u == 2:
                            query_sums()
                        if u == 3:
                            query_gains()
                        if u == 4:
                            split(width)
                        if u == 5:
                            query_rotation()
                        if u == 6:
                            key_sums()
                if following:
                    normalise()
                rd = stat[:, RD:RD + 8]
                ve.wait_ge(probs_ready, 8 + n.step("probs", 8))
                chained(ve.reciprocal(rd, stat[:, LS:LS + 8]))
                ve.wait_ge(pv_done, 8 + n.at("pv"))
                n.step("small")
                for t in range(NT):
                    dst = o_nat[:, t, columns].rearrange("p (h d) -> p h d", d=VD)
                    last = ve.tensor_tensor(dst, small[:, t * GH * VD:(t + 1) * GH * VD].rearrange("p (h d) -> p h d", d=VD),
                                            rd[:, t * GH:(t + 1) * GH].rearrange("p (h o) -> p h o", o=1).to_broadcast([P, GH, VD]), ALU.mult)
                last.then_inc(small_read, 1)

            split(WKV)
            n.step("unit", 6)
            query_sums()
            query_gains()
            query_rotation()
            split(WQ)
            key_sums()
            normalise()
            GV = GH * VD
            with n.loop(ve, 2, split=2, unit=6, tr=14, scores=8, small=1, sq=2, groot=1, probs=8, pv=8, chain=16) as i:
                attend_group(bass.ds(i * GV, GV))
            attend_group(slice(2 * GV, 3 * GV), width=CHUNK)
            attend_group(slice(3 * GV, 4 * GV), following=False)
            split()
            for half in range(2):
                for t in range(NT):
                    plain_rows(act_dst(act_hi, 0, half, t), act_dst(act_lo, 0, half, t))
            rotation(4)
            coefs(3, "norm_ffn", 1, 56)
            for cb in range(2):
                split()
                for t in range(NT):
                    add_gated(t, cb, 0, cb == 1)
                    if cb and t == 0:
                        recips([0])
            ve.wait_ge(x_ready, n.step("x", 2))
            scaled_rows(modulated(3, 48, 0, 0) + modulated(3, 48, 0, 1), after_first=lambda: recips([1]))
            gate_read(1, (1,))

            def hidden_chunk1(p, k, again=True):
                split()
                for f in range(2):
                    if again:
                        ve.wait_ge(hidden_ready, n.at("hidden1", 3))
                    b = unit()
                    ve.wait_ge(silu_ready, n.step("silu"))
                    ve.tensor_tensor(h3[:, k, f, :], silu3[:, f, :], b[:, SEQ:2 * SEQ], ALU.mult).then_inc(gemm_read, 1)
                    ve.wait_ge(tr_hi, n.step("tr_hi"))
                    ve.tensor_tensor(h3_lo[:, p, 2 * k + f, :], h3[:, k, f, :], h3_hi[:, p, 2 * k + f, :].bitcast(f32),
                                     ALU.subtract).then_inc(hidden_ready, 1)
                    n.step("hidden1")

            def down1(final=False):
                split()
                for t in range(NT):
                    for cb in range(2):
                        add_gated(t, cb, 1, final and cb == 1)

            def group1(p):
                hidden_chunk1(p, 0)
                hidden_chunk1(p, 1)
                down1()

            hidden_chunk1(0, 0, again=False)
            hidden_chunk1(0, 1, again=False)
            with n.loop(ve, 2, split=6, unit=16, tr_hi=8, silu=8, hidden1=8, chain=8):
                group1(1)
                group1(0)
            hidden_chunk1(1, 0)
            down1()
            down1(final=True)


def _rows_first(w, kts):
    return w.reshape(kts, P, w.shape[1]).transpose(1, 0, 2).reshape(P, -1)


def _blocks(w):
    return [_rows_first(w[:, c:c + COLS], KT) for c in range(0, w.shape[1], COLS)]


def _down(w):
    kts = w.shape[0] // P
    return w.reshape(kts, P, 2, COLS).transpose(1, 2, 0, 3).reshape(P, -1)


def _tables():
    ident = np.eye(P, dtype=np.float32)
    rel = np.arange(P)[:, None] + P - np.arange(2 * P)[None, :]
    mask = np.where((rel >= 0) & (rel < P), 0.0, -1e30).astype(np.float32)

    def token_rows(t):
        return t.astype(np.float32).reshape(NT, P, -1).transpose(1, 0, 2).reshape(P, -1)

    inv1 = (500000.0 ** (-np.arange(0, ROT, 2, dtype=np.float32).astype(np.float64) / ROT)).astype(np.float32)
    ang1 = (np.arange(SEQ, dtype=np.float32)[:, None] * inv1[None, :]).astype(np.float64)
    inv2 = (10000.0 ** (-np.arange(0, ROPE // 2, 2).astype(np.float64) / (ROPE // 2))).astype(np.float32)
    grid = 64
    r = (np.arange(SEQ) // grid).astype(np.float32)[:, None] * inv2
    c = (np.arange(SEQ) % grid).astype(np.float32)[:, None] * inv2
    ang2 = np.concatenate([r, r, c, c], axis=1).astype(np.float64)
    sign = np.tile(np.repeat([-1.0, 1.0], 8), 2)
    sel_col = np.zeros((P, 2), np.float32)
    sel_col[0:2, 0] = sel_col[2:4, 1] = 1.0
    sel_row = np.zeros((P, 2, P), np.float32)
    sel_row[0:2, 0] = sel_row[2:4, 1] = sel_row[4] = 1.0
    return mask, np.concatenate([ident, token_rows(np.cos(ang1)), token_rows(np.sin(ang1)), token_rows(np.cos(ang2)),
                           token_rows(np.sin(ang2) * sign), sel_col, sel_row.reshape(P, 2 * P)], axis=1)


def _pool_matrices():
    s, t = np.arange(SEQ)[:, None], np.arange(SEQ)[None, :]
    out = np.zeros((P, len(POOL_WINDOWS), 3, P), np.float32)
    for g, w in enumerate(POOL_WINDOWS):
        m = ((s <= t) & (t - s < w)) / np.minimum(t + 1, w) - (s == t)
        for j, (a, b) in enumerate(((0, 0), (0, 1), (1, 1))):
            out[:, g, j] = m[a * P:(a + 1) * P, b * P:(b + 1) * P]
    return out


def kernel(**inputs):
    import concourse.bacc as bacc
    from concourse.bass_utils import run_bass_kernel_spmd

    v = {name: np.asarray(value) for name, value in inputs.items()}

    def columns(vec):
        return vec.reshape(-1, P).T

    mod_w, mod_b = v["mod_w_2"], v["mod_b_2"]
    kinds = (0, 1, 3, 4)
    mod_cols = [_rows_first(mod_w[l][:, k * D + h * COLS:k * D + (h + 1) * COLS], KT) for l in range(2) for k in kinds for h in range(2)]
    gates = [(l, k) for l in range(2) for k in (2, 5)]
    mod_gates = [[_rows_first(mod_w[l][:, k * D + h * COLS:k * D + (h + 1) * COLS], KT) for h in range(2)] for l, k in gates]
    w_in = v["w_in"][0]
    mlp = []
    up, down = _blocks(v["w_up"][0]), v["w_down"][0]
    for i in range(4):
        d = down[i * D:(i + 1) * D]
        mlp += [up[2 * i], mod_cols[4 + 2 * i], up[2 * i + 1], mod_cols[5 + 2 * i], _rows_first(d[:, 0:COLS], KT), _rows_first(d[:, COLS:D], KT)]
    conv = v["conv_w_in_2"][0].reshape(D, 3, KT, P)
    ffn = []
    for l in range(2):
        wg, wu, wd = v["ffn_w_gate_2"][l], v["ffn_w_up_2"][l], v["ffn_w_down_2"][l]
        gu = [_rows_first(np.concatenate([wg[:, j:j + 256], wu[:, j:j + 256]], axis=1), KT) for j in range(0, FH, 256)]
        dn = [_down(wd[i * COLS:(i + 1) * COLS]) for i in range(6)]
        seq = []
        for i in range(5):
            if l == 0:
                seq += [gu[2 * i]] + ([mod_cols[12 + i]] if i < 4 else []) + [gu[2 * i + 1], dn[i]]
            else:
                seq += [gu[2 * i], gu[2 * i + 1]] + ([dn[i - 1]] if i else [])
        ffn.append((seq + ([gu[10], dn[4]] if l else []), [gu[10]], [dn[5]]))
    mla_in = v["mla_w_in_2"][0]
    q_up, kv_up = v["mla_w_q_up_2"][0], v["mla_w_kv_up_2"][0]
    stream = {
        "w_in": _blocks(w_in[:, 0:K0]), "w_kv": [_rows_first(w_in[:, K0:G0], KT)],
        "w_gates": _blocks(w_in[:, G0:]), "w_branch": [_down(v["w_branch_pool"][0]), mod_cols[0], _down(v["w_branch_attn"][0]), mod_cols[1]],
        "w_out": _blocks(v["w_out"][0]), "mod_scale": mod_cols[2:4], "mlp": mlp, "mod_gate0": mod_gates[0],
        "conv_in": [_rows_first(conv[:, :, f, :].reshape(D, 3 * P), KT) for f in range(KT)], "conv_out": _blocks(v["conv_w_out_2"][0]),
        "mod_gate1": mod_gates[1], "ffn0_first": ffn[0][1], "ffn0_half": ffn[0][2], "ffn0": ffn[0][0], "mod_gate2": mod_gates[2],
        "mla_in": _blocks(mla_in[:, 0:QL + KVL]), "mod_gate3": mod_gates[3][0:1], "mod_gate3_half": mod_gates[3][1:2],
        "mla_q": [_rows_first(q_up[:, g * GH * QK:(g + 1) * GH * QK], QKT) for g in range(MH // GH)],
        "mla_kv": [_rows_first(kv_up[:, g * COLS:(g + 1) * COLS], KVT) for g in range(MH // GH)], "mla_out": _blocks(v["mla_w_out_2"][0]),
        "ffn1": ffn[1][0], "ffn1_half": ffn[1][2],
    }
    arrays = {}
    for name, n, width in SECTIONS:
        arrays[name] = np.stack(stream[name])
        assert arrays[name].shape == (n, P, width), (name, arrays[name].shape)
    arrays["x"] = v["x"][0]
    arrays["ctx"] = v["ctx_2"][0]
    arrays["cols"] = np.concatenate(
        [columns(v[k]) for k in ("g_mix_pre", "g_mlp_pre", "pool_scale", "norm_mix_g_2", "norm_ffn_g_2", "mla_q_norm_g_2", "mla_kv_norm_g_2")]
        + [columns(v["conv_k_2"][0, j]) for j in range(3)] + [columns(v["conv_b_2"])]
        + [np.stack([columns(v["c_2"]), columns(v["c_ctx_2"])], axis=2).reshape(P, 2 * KT)]
        + [columns(mod_b[l, k * D:(k + 1) * D]) for l in range(2) for k in kinds], axis=1)
    arrays["rows"] = np.concatenate([v[k].reshape(-1) for k in (
        "attn_sinks", "mla_qn_nope_g_2", "mla_qn_rope_g_2", "mla_kn_nope_g_2", "mla_kn_rope_g_2")])
    arrays["mask"], arrays["tab"] = _tables()
    arrays["pool_m"] = _pool_matrices()
    arrays["w_pool"] = v["w_pool"][0]
    arrays["b_in"] = v["b_in"][0]
    arrays["g_mix_post"] = v["g_mix_post"][0]
    arrays["g_mlp_post"] = v["g_mlp_post"][0]
    arrays["mod_gate_b"] = np.concatenate([mod_b[l, k * D:(k + 1) * D].reshape(2, COLS) for l, k in gates])
    arrays["w_pe"] = mla_in[:, QL + KVL:].reshape(KT, P, ROPE).transpose(1, 0, 2)

    f32 = mybir.dt.float32
    nc = bacc.Bacc("TRN2", target_bir_lowering=False, num_devices=1)
    feeds, args = {}, {}
    for name, value in arrays.items():
        feeds["in_" + name] = np.ascontiguousarray(value)
        args[name] = nc.dram_tensor("in_" + name, value.shape, f32, kind="ExternalInput").ap()
    out = nc.dram_tensor("out_x", (SEQ, D), f32, kind="ExternalOutput").ap()
    build(nc, args, out)
    result = run_bass_kernel_spmd(nc, [feeds], core_ids=[0])
    return result.results[0]["out_x"].reshape(1, SEQ, D)
```
